# Optimizing a Trainium2 kernel written in Bass

```python
import math
import jax, jax.numpy as jnp
from jax import lax
import numpy as np

D_MODEL = 1024
BATCH = 1
SEQ = 1024
DEPTH = 1
DEC_BATCH = 8
DEC_SEQ = 1
PAST_LEN = 1024
PAGE_SIZE = 128

DIL_GROUPS = ((128, 1), (512, 4), (2048, 16))
N_GROUPS = len(DIL_GROUPS)
HEADS_PER_GROUP = 4
ATT_HEADS = N_GROUPS * HEADS_PER_GROUP
ATT_HEAD_DIM = 64
ATT_WIDTH = ATT_HEADS * ATT_HEAD_DIM
ATT_OUT_WIDTH = HEADS_PER_GROUP * ATT_HEAD_DIM
ALIBI_EXP = 8.0

DN_HEADS = 4
DN_HEAD_DIM = 128
DN_WIDTH = DN_HEADS * DN_HEAD_DIM
DN_CONV = 4
DN_CHUNK = 64
DT_MIN = 1e-3
DT_MAX = 1e-1

D_FF = 2816
FFN_CONV = 3

DEEPNORM_ALPHA = (2 * DEPTH) ** 0.25
DEEPNORM_BETA = (8 * DEPTH) ** -0.25
LN_EPS = 1e-5
RMS_EPS = 1e-6

OFF_DN_QKV = 3 * ATT_WIDTH
OFF_DN_Z = OFF_DN_QKV + 3 * DN_WIDTH
OFF_DN_BETA = OFF_DN_Z + DN_WIDTH
OFF_DN_A = OFF_DN_BETA + DN_HEADS
OFF_GATE = OFF_DN_A + DN_HEADS
IN_WIDTH = OFF_GATE + 2 * D_MODEL

kernel_name = 'hybrid_dilated_attn_gated_deltanet_convffn_deepnorm_step'

def _layer_norm(x, g, b):
    xf = x.astype(jnp.float32)
    mu = jnp.mean(xf, axis=-1, keepdims=True)
    var = jnp.mean(jnp.square(xf - mu), axis=-1, keepdims=True)
    return ((xf - mu) * lax.rsqrt(var + LN_EPS) * g.astype(jnp.float32) + b.astype(jnp.float32)).astype(x.dtype)

def _l2norm(x):
    return x * lax.rsqrt(jnp.sum(jnp.square(x), axis=-1, keepdims=True) + RMS_EPS)

def _causal_dwconv(x, w, prev):
    width, t = w.shape[0], x.shape[1]
    xp = jnp.concatenate([prev.astype(x.dtype), x], axis=1)
    out = w[0] * xp[:, :t]
    for j in range(1, width):
        out = out + w[j] * xp[:, j:j + t]
    return out, xp[:, t:]

def _alibi_slopes():
    h = jnp.arange(1, ATT_HEADS + 1, dtype=jnp.float32)
    return jnp.exp2(-ALIBI_EXP * h / ATT_HEADS).reshape(N_GROUPS, HEADS_PER_GROUP)

def _dilated_prompt(q, k, v, window, dilation, slopes):
    b, t, h, e = q.shape
    steps = window // dilation
    n_sub = t // dilation
    n_blk = -(-n_sub // steps)
    pad = n_blk * steps - n_sub

    def to_blocks(a):
        a = a.reshape(b, n_sub, dilation, h, e).transpose(0, 2, 1, 3, 4)
        a = jnp.pad(a, ((0, 0), (0, 0), (0, pad), (0, 0), (0, 0)))
        return a.reshape(b, dilation, n_blk, steps, h, e)

    def with_prev(a):
        prev = jnp.pad(a[:, :, :-1], ((0, 0), (0, 0), (1, 0), (0, 0), (0, 0), (0, 0)))
        return jnp.concatenate([prev, a], axis=3)

    qb = to_blocks(q)
    kb = with_prev(to_blocks(k))
    vb = with_prev(to_blocks(v))
    s = jnp.einsum('brnqhe,brnkhe->brnhqk', qb, kb, preferred_element_type=jnp.float32) * (e ** -0.5)
    qi = jnp.arange(steps)[:, None]
    kj = jnp.arange(2 * steps)[None, :]
    dist = steps + qi - kj
    blk = jnp.arange(n_blk)[:, None, None]
    valid = (dist >= 0) & (dist <= steps) & ((blk > 0) | (kj >= steps))
    bias = -slopes[:, None, None] * (dilation * dist).astype(jnp.float32)
    s = jnp.where(valid[:, None], s + bias, -jnp.inf)
    m = jnp.max(s, axis=-1, keepdims=True)
    p = jnp.exp(s - m)
    l = jnp.sum(p, axis=-1, keepdims=True)
    o = jnp.einsum('brnhqk,brnkhe->brnqhe', (p / l).astype(v.dtype), vb, preferred_element_type=jnp.float32)
    lse = (m + jnp.log(l))[..., 0].transpose(0, 1, 2, 4, 3)

    def from_blocks(a):
        a = a.reshape(b, dilation, n_blk * steps, *a.shape[4:])[:, :, :n_sub]
        return jnp.swapaxes(a, 1, 2).reshape(b, t, *a.shape[3:])

    return from_blocks(o), from_blocks(lse)

def _dilated_step(q, k_ext, v_ext, n_past, window, dilation, slopes):
    b, s_new, h, e = q.shape
    steps = window // dilation
    back = jnp.arange(steps + 1)
    idx = n_past + jnp.arange(s_new)[:, None] - dilation * back[None, :]
    valid = idx >= 0
    idx = jnp.maximum(idx, 0)
    kg = jnp.take(k_ext, idx, axis=1)
    vg = jnp.take(v_ext, idx, axis=1)
    sc = jnp.einsum('bshe,bsihe->bshi', q, kg, preferred_element_type=jnp.float32) * (e ** -0.5)
    bias = -slopes[:, None] * (dilation * back).astype(jnp.float32)
    sc = jnp.where(valid[:, None, :], sc + bias, -jnp.inf)
    m = jnp.max(sc, axis=-1, keepdims=True)
    p = jnp.exp(sc - m)
    l = jnp.sum(p, axis=-1, keepdims=True)
    o = jnp.einsum('bshi,bsihe->bshe', (p / l).astype(v_ext.dtype), vg, preferred_element_type=jnp.float32)
    return o, (m + jnp.log(l))[..., 0]

def _combine_groups(outs, lses):
    w = jax.nn.softmax(jnp.stack(lses, axis=0), axis=0)
    return jnp.sum(w[..., None] * jnp.stack(outs, axis=0), axis=0)

def _delta_chunked(q, k, v, beta, g):
    b, t, h, dk = q.shape
    dv = v.shape[-1]
    c = DN_CHUNK
    nc = t // c

    def chunks(a):
        return a.reshape(b, nc, c, h, a.shape[-1]).transpose(1, 0, 3, 2, 4)

    qc, kc, vc = chunks(q), chunks(k), chunks(v)
    bc = chunks(beta[..., None])
    gcum = jnp.cumsum(chunks(g[..., None])[..., 0], axis=-1)
    tri = jnp.tril(jnp.ones((c, c), dtype=bool))
    tri_strict = jnp.tril(jnp.ones((c, c), dtype=bool), -1)
    decay = jnp.exp(jnp.where(tri, gcum[..., :, None] - gcum[..., None, :], -jnp.inf))
    kk = jnp.einsum('nbhid,nbhjd->nbhij', kc * bc, kc)
    lower = jnp.where(tri_strict, kk * decay, 0.0) + jnp.eye(c, dtype=jnp.float32)
    rhs = jnp.concatenate([vc * bc, kc * bc * jnp.exp(gcum)[..., None]], axis=-1)
    sol = lax.linalg.triangular_solve(lower, rhs, left_side=True, lower=True, unit_diagonal=True)
    u0, wk = sol[..., :dv], sol[..., dv:]
    attn = jnp.einsum('nbhid,nbhjd->nbhij', qc, kc) * decay
    q_dec = qc * jnp.exp(gcum)[..., None]
    k_dec = kc * jnp.exp(gcum[..., -1:] - gcum)[..., None]
    g_last = jnp.exp(gcum[..., -1])

    def step(s, xs):
        u0_, wk_, attn_, qd_, kd_, gl_ = xs
        u = u0_ - jnp.einsum('bhid,bhde->bhie', wk_, s)
        o = jnp.einsum('bhid,bhde->bhie', qd_, s) + jnp.einsum('bhij,bhje->bhie', attn_, u)
        s = s * gl_[..., None, None] + jnp.einsum('bhid,bhie->bhde', kd_, u)
        return s, o

    s0 = jnp.zeros((b, h, dk, dv), jnp.float32)
    s_fin, o = lax.scan(step, s0, (u0, wk, attn, q_dec, k_dec, g_last))
    return o.transpose(1, 0, 3, 2, 4).reshape(b, t, h, dv), s_fin

def _delta_recurrent(q, k, v, beta, g, s0):
    def step(s, xs):
        q_, k_, v_, b_, g_ = xs
        s = s * jnp.exp(g_)[..., None, None]
        u = b_[..., None] * (v_ - jnp.einsum('bhd,bhde->bhe', k_, s))
        s = s + jnp.einsum('bhd,bhe->bhde', k_, u)
        return s, jnp.einsum('bhd,bhde->bhe', q_, s)

    xs = (jnp.swapaxes(q, 0, 1), jnp.swapaxes(k, 0, 1), jnp.swapaxes(v, 0, 1),
          jnp.swapaxes(beta, 0, 1), jnp.swapaxes(g, 0, 1))
    s_fin, o = lax.scan(step, s0, xs)
    return jnp.swapaxes(o, 0, 1), s_fin

def _deltanet(qkv_pre, z, b_raw, a_raw, conv_prev, s_prev, w_conv, a_log, dt_bias, w_norm):
    bsz, t = qkv_pre.shape[:2]
    qkv, conv_new = _causal_dwconv(qkv_pre, w_conv, conv_prev)
    qkv = jax.nn.silu(qkv.astype(jnp.float32)).reshape(bsz, t, 3, DN_HEADS, DN_HEAD_DIM)
    q = _l2norm(qkv[:, :, 0]) * (DN_HEAD_DIM ** -0.5)
    k = _l2norm(qkv[:, :, 1])
    v = qkv[:, :, 2]
    beta = jax.nn.sigmoid(b_raw.astype(jnp.float32))
    g = -jnp.exp(a_log.astype(jnp.float32)) * jax.nn.softplus(a_raw.astype(jnp.float32) + dt_bias.astype(jnp.float32))
    if s_prev is None:
        o, s_new = _delta_chunked(q, k, v, beta, g)
    else:
        o, s_new = _delta_recurrent(q, k, v, beta, g, s_prev.astype(jnp.float32))
    zf = z.astype(jnp.float32).reshape(bsz, t, DN_HEADS, DN_HEAD_DIM)
    o = o * lax.rsqrt(jnp.mean(jnp.square(o), axis=-1, keepdims=True) + RMS_EPS) * w_norm.astype(jnp.float32) * jax.nn.silu(zf)
    return o.reshape(bsz, t, DN_WIDTH).astype(qkv_pre.dtype), conv_new, s_new.astype(qkv_pre.dtype)

def _conv_ffn(h, prev, w_up, w_conv, b_conv, w_down):
    up = h @ w_up
    a, gate = up[..., :D_FF], up[..., D_FF:]
    a_c, buf_new = _causal_dwconv(a, w_conv, prev)
    return (jax.nn.gelu(a_c + b_conv) * gate) @ w_down, buf_new

def _layer(x, kv_prev, dn_conv_prev, dn_s_prev, ffn_prev, lp):
    b, t, _ = x.shape
    prompt = kv_prev is None
    if prompt:
        dn_conv_prev = jnp.zeros((b, DN_CONV - 1, 3 * DN_WIDTH), x.dtype)
        ffn_prev = jnp.zeros((b, FFN_CONV - 1, D_FF), x.dtype)
    proj = x @ lp['w_in']

    qkv_a = proj[..., :OFF_DN_QKV].reshape(b, t, 3, N_GROUPS, HEADS_PER_GROUP, ATT_HEAD_DIM)
    slopes = _alibi_slopes()
    outs, lses, kv_new = [], [], []
    for gi, (window, dil) in enumerate(DIL_GROUPS):
        q, k, v = qkv_a[:, :, 0, gi], qkv_a[:, :, 1, gi], qkv_a[:, :, 2, gi]
        kv = jnp.stack([k, v], axis=2)
        if prompt:
            o, lse = _dilated_prompt(q, k, v, window, dil, slopes[gi])
            keep = min(window, t)
            kv_new.append(kv[:, t - keep:])
        else:
            n_past = kv_prev[gi].shape[1]
            kv_ext = jnp.concatenate([kv_prev[gi].astype(x.dtype), kv], axis=1)
            o, lse = _dilated_step(q, kv_ext[:, :, 0], kv_ext[:, :, 1], n_past, window, dil, slopes[gi])
            kv_new.append(kv_ext[:, -n_past:])
        outs.append(o)
        lses.append(lse)
    o_att = _combine_groups(outs, lses).reshape(b, t, ATT_OUT_WIDTH).astype(x.dtype)

    o_dn, dn_conv_new, dn_s_new = _deltanet(
        proj[..., OFF_DN_QKV:OFF_DN_Z], proj[..., OFF_DN_Z:OFF_DN_BETA],
        proj[..., OFF_DN_BETA:OFF_DN_A], proj[..., OFF_DN_A:OFF_GATE],
        dn_conv_prev, dn_s_prev, lp['w_dn_conv'], lp['dn_a_log'], lp['dn_dt_bias'], lp['dn_onorm_w'])

    gate = jax.nn.sigmoid(proj[..., OFF_GATE:].astype(jnp.float32))
    merged = gate[..., :D_MODEL] * (o_att @ lp['w_att_out']) + gate[..., D_MODEL:] * (o_dn @ lp['w_dn_out'])
    mix = merged.astype(x.dtype) @ lp['w_o']
    h = _layer_norm(DEEPNORM_ALPHA * x + mix, lp['ln1_g'], lp['ln1_b'])

    f, ffn_new = _conv_ffn(h, ffn_prev, lp['w_up'], lp['w_ffn_conv'], lp['b_ffn_conv'], lp['w_down'])
    y = _layer_norm(DEEPNORM_ALPHA * h + f, lp['ln2_g'], lp['ln2_b'])
    return y, (kv_new[0], kv_new[1], kv_new[2], dn_conv_new, dn_s_new, ffn_new)

def setup_inputs(seed: int = 0) -> dict:
    key = jax.random.key(seed)
    ks = jax.random.split(key, 24)
    f32 = jnp.float32

    def nrm(k, shape, scale):
        return jax.random.normal(k, shape, f32) * scale

    lw = [min(w, PAST_LEN) for w, _ in DIL_GROUPS]

    def kv_shape(n):
        return (DEPTH, DEC_BATCH, n, 2, HEADS_PER_GROUP, ATT_HEAD_DIM)

    dt = jnp.exp(jax.random.uniform(ks[11], (DEPTH, DN_HEADS), f32, math.log(DT_MIN), math.log(DT_MAX)))
    return {
        'x_prompt': nrm(ks[0], (BATCH, SEQ, D_MODEL), 1.0),
        'x_sample': nrm(ks[1], (DEC_BATCH, DEC_SEQ, D_MODEL), 1.0),
        'cache_kv_w128': nrm(ks[2], kv_shape(lw[0]), 1.0),
        'cache_kv_w512': nrm(ks[3], kv_shape(lw[1]), 1.0),
        'cache_kv_w2048': nrm(ks[4], kv_shape(lw[2]), 1.0),
        'state_dn_conv': nrm(ks[5], (DEPTH, DEC_BATCH, DN_CONV - 1, 3 * DN_WIDTH), 1.0),
        'state_dn_S': nrm(ks[6], (DEPTH, DEC_BATCH, DN_HEADS, DN_HEAD_DIM, DN_HEAD_DIM), 0.3),
        'state_ffn_conv': nrm(ks[7], (DEPTH, DEC_BATCH, FFN_CONV - 1, D_FF), 1.0),
        'w_in': nrm(ks[8], (DEPTH, D_MODEL, IN_WIDTH), D_MODEL ** -0.5),
        'w_dn_conv': nrm(ks[9], (DEPTH, DN_CONV, 3 * DN_WIDTH), DN_CONV ** -0.5),
        'dn_a_log': jnp.log(jax.random.uniform(ks[10], (DEPTH, DN_HEADS), f32, 1.0, 16.0)),
        'dn_dt_bias': dt + jnp.log(-jnp.expm1(-dt)),
        'dn_onorm_w': 1.0 + nrm(ks[12], (DEPTH, DN_HEAD_DIM), 0.02),
        'w_att_out': nrm(ks[13], (DEPTH, ATT_OUT_WIDTH, D_MODEL), ATT_OUT_WIDTH ** -0.5 * DEEPNORM_BETA),
        'w_dn_out': nrm(ks[14], (DEPTH, DN_WIDTH, D_MODEL), DN_WIDTH ** -0.5 * DEEPNORM_BETA),
        'w_o': nrm(ks[15], (DEPTH, D_MODEL, D_MODEL), D_MODEL ** -0.5 * DEEPNORM_BETA),
        'ln1_g': 1.0 + nrm(ks[16], (DEPTH, D_MODEL), 0.02),
        'ln1_b': nrm(ks[17], (DEPTH, D_MODEL), 0.02),
        'w_up': nrm(ks[18], (DEPTH, D_MODEL, 2 * D_FF), D_MODEL ** -0.5),
        'w_ffn_conv': nrm(ks[19], (DEPTH, FFN_CONV, D_FF), FFN_CONV ** -0.5),
        'b_ffn_conv': nrm(ks[20], (DEPTH, D_FF), 0.02),
        'w_down': nrm(ks[21], (DEPTH, D_FF, D_MODEL), D_FF ** -0.5 * DEEPNORM_BETA),
        'ln2_g': 1.0 + nrm(ks[22], (DEPTH, D_MODEL), 0.02),
        'ln2_b': nrm(ks[23], (DEPTH, D_MODEL), 0.02),
    }

def reference(x_prompt, x_sample, cache_kv_w128, cache_kv_w512, cache_kv_w2048, state_dn_conv,
              state_dn_S, state_ffn_conv, w_in, w_dn_conv, dn_a_log, dn_dt_bias, dn_onorm_w,
              w_att_out, w_dn_out, w_o, ln1_g, ln1_b, w_up, w_ffn_conv, b_ffn_conv, w_down,
              ln2_g, ln2_b):
    def layer_params(l):
        return {'w_in': w_in[l], 'w_dn_conv': w_dn_conv[l], 'dn_a_log': dn_a_log[l],
                'dn_dt_bias': dn_dt_bias[l], 'dn_onorm_w': dn_onorm_w[l], 'w_att_out': w_att_out[l],
                'w_dn_out': w_dn_out[l], 'w_o': w_o[l], 'ln1_g': ln1_g[l], 'ln1_b': ln1_b[l],
                'w_up': w_up[l], 'w_ffn_conv': w_ffn_conv[l], 'b_ffn_conv': b_ffn_conv[l],
                'w_down': w_down[l], 'ln2_g': ln2_g[l], 'ln2_b': ln2_b[l]}

    yp, ys = x_prompt, x_sample
    p_states, s_states = [], []
    for l in range(DEPTH):
        lp = layer_params(l)
        yp, st_p = _layer(yp, None, None, None, None, lp)
        p_states.append(st_p)
        ys, st_s = _layer(ys, (cache_kv_w128[l], cache_kv_w512[l], cache_kv_w2048[l]),
                          state_dn_conv[l], state_dn_S[l], state_ffn_conv[l], lp)
        s_states.append(st_s)

    def stacked(states, i):
        return jnp.stack([st[i] for st in states], axis=0)

    return (yp, ys,
            stacked(p_states, 0), stacked(p_states, 1), stacked(p_states, 2),
            stacked(p_states, 3), stacked(p_states, 4), stacked(p_states, 5),
            stacked(s_states, 0), stacked(s_states, 1), stacked(s_states, 2),
            stacked(s_states, 3), stacked(s_states, 4), stacked(s_states, 5))


_drawn_inputs = setup_inputs


def setup_inputs(seed=0):
    import zlib

    import numpy as np

    out = dict(_drawn_inputs(seed))
    spreads = {}
    factors = {'dn_onorm_w': 94.533,
     'ln1_g': 2.725,
     'ln1_b': 2.711,
     'b_ffn_conv': 8.0,
     'ln2_g': 22.248,
     'ln2_b': 22.95,
     'w_att_out': 3.276}
    for name, (base, spread) in spreads.items():
        noise = np.random.default_rng([zlib.crc32(name.encode()), seed]).standard_normal(out[name].shape)
        drawn = base * np.exp(spread * noise) if base else spread * noise
        out[name] = __import__('jax').numpy.asarray(drawn.astype(out[name].dtype))
    for name, factor in factors.items():
        out[name] = (out[name] * factor).astype(out[name].dtype)
    return out
```

```python
import numpy as np

import concourse.bass as bass
from concourse import mybir
from contextlib import ExitStack

F32 = mybir.dt.float32
F32R = mybir.dt.float32r
ALU = mybir.AluOpType
ACT = mybir.ActivationFunctionType
AX = mybir.AxisListType

P = 128
D_MODEL, SEQ, SAMPLES = 1024, 1024, 8
D_FF = 2816
DIL = ((128, 1), (512, 4), (2048, 16))
GROUPS, HPG, HD = 3, 4, 64
ATT_W = GROUPS * HPG * HD
DN_H, DN_D = 4, 128
TOK = SEQ + SAMPLES
THIRDS = 3
TW = TOK // THIRDS
KT = D_MODEL // P
FT = D_FF // P
OFF_DN = 3 * ATT_W
OFF_Z = OFF_DN + 3 * DN_H * DN_D
OFF_BA = OFF_Z + DN_H * DN_D
OFF_GATE = OFF_BA + 2 * DN_H
ALPHA = 2.0 ** 0.25
LN_EPS, RMS_EPS = 1e-5, 1e-6
NEG = -1e30
N_CONSTS = 4
CONV_STEPS = 16
FFN_STEPS = 12
SMALL_0, SMALL_S, DN_STEPS = 5, 18, 26
BLOCKS = 8
TILES = SEQ // P
PAST = (128, 512, 1024)
SKEYS = (8, 8, 4)
SK = sum(SKEYS)

U_BLK = 10
U_DN = 18
U_Z = U_DN + 12
U_GATE = U_Z + DN_H
U_BRANCH = U_GATE + 16
U_MIX = U_BRANCH + KT
U_FFN = U_MIX + KT
PIECES = (8, 8, 6)
LAST_USED = 3 * (U_FFN - U_BRANCH + len(PIECES) * KT)
UNITS = U_FFN + sum(2 * n + KT for n in PIECES)

C_ID, C_DNW, C_FFW, C_FFB, C_G1, C_B1, C_ON, C_R, C_END = np.cumsum(
    [0, P, 12 * 4, FT * 3, FT, KT, KT, 1, P]).tolist()
D_TRI, D_NEG, D_STR, D_ONE, D_LEV, D_END = np.cumsum([0, P, P, P, P, 7 * P]).tolist()


def third(j):
    return slice(j * TW, (j + 1) * TW)


def build(nc, I, O):
    ctx = ExitStack()
    with ctx:
        def sem(name):
            return ctx.enter_context(nc.semaphore(name))

        def held(stack, name, shape, dt=F32):
            return stack.enter_context(nc.sbuf_tensor(name, shape, dt))

        att_scr = nc.dram_tensor("att_scr", [GROUPS, SEQ, HPG * 66], F32).ap()
        dn_scr = nc.dram_tensor("dn_scr", [16, P, SEQ + P], F32).ap()
        gate_scr = nc.dram_tensor("gate_scr", [16, P, TOK], F32).ap()

        xh = held(ctx, "xh", [P, KT, TOK], F32R)
        xl = held(ctx, "xl", [P, KT, TOK], F32R)
        stage = held(ctx, "stage", [P, 2, KT * P])
        wh = held(ctx, "wh", [P, 2, KT * P], F32R)
        wl = held(ctx, "wl", [P, 2, KT * P], F32R)
        cst = held(ctx, "cst", [P, C_END])
        ident = cst[:, C_ID:C_ID + P]
        mhalf = held(ctx, "mhalf", [P, 64])
        babuf = held(ctx, "babuf", [P, 8, 9, DN_H])

        early = ExitStack()
        with early:
            qkv = held(early, "qkv", [P, 18, TOK])
            q_st = held(early, "q_st", [P, 2, P])
            k_st = held(early, "k_st", [P, 2, 2, P])
            v_st = held(early, "v_st", [P, 2, P])
            bias = held(early, "bias", [P, 4, 2, P])
            sb = held(early, "sb", [P, 4, 2, P])
            pb = held(early, "pb", [P, 4, 2, P])
            pts = held(early, "pts", [P, 8, P])
            vtok = held(early, "vtok", [P, 2, 256])
            obuf = held(early, "obuf", [P, 2, 4, 66])
            nmax = held(early, "nmax", [P, 4])
            pre = held(early, "pre", [P, 2, 3 + TOK])
            cb = held(early, "cb", [P, TOK])
            thb = held(early, "thb", [P, TOK])
            tails = held(early, "tails", [P, 12, 11])
            sconv = held(early, "sconv", [P, 12, SAMPLES, 3])
            wba = held(early, "wba", [P, KT, 8])
            bac = held(early, "bac", [P, 2, DN_H])
        xraw = qkv[:, 10:18, :]

        middle = ExitStack()
        with middle:
            oh = held(middle, "oh", [P, 6, TOK], F32R)
            ol = held(middle, "ol", [P, 6, TOK], F32R)
            with ExitStack() as part:
                kvc = held(part, "kvc", [P, SK, 2, 256])
                prod = held(part, "prod", [P, 8, 4, 64])
                sq = held(part, "sq", [SAMPLES, 3, 3, 256])
                qb = held(part, "qb", [P, 3, 256])
                ssc = held(part, "ssc", [P, SK, 4])
                sbias = held(part, "sbias", [P, SK, 4])
                og = held(part, "og", [P, 3, 256])
                rt = held(part, "rt", [P, SAMPLES])
                sm = held(part, "sm", [P, 16, 4])
                self_s = held(part, "self_s", [SAMPLES, 3, 4])
                self_p = held(part, "self_p", [SAMPLES, 3, 256])
                o8 = held(part, "o8", [SAMPLES, 256])
            with ExitStack() as part:
                gates = held(part, "gates", [P, 2, 2, TOK])
            dcst = held(middle, "dcst", [P, D_END])
            cf = held(middle, "cf", [P, 5, 4 * TILES])
            onh = held(middle, "onh", [P, 1])
            gth = held(middle, "gth", [P, 2, TOK])
            part = ExitStack()
            with part:
                dnin = held(part, "dnin", [P, 12, P])
                zin = held(part, "zin", [P, 4, P])
                abuf = held(part, "abuf", [P, 3, 4, 66])
                amx = held(part, "amx", [P, 8, 4])
                ao = held(part, "ao", [P, 4, 64])
                rn = held(part, "rn", [P, 3, 8])
                gB = held(part, "gB", [P, 4, P])
                ET = held(part, "ET", [P, 4, P])
                ETs = held(part, "ETs", [P, 4, P])
                sq2 = held(part, "sq2", [P, 8, P])
                qn, kn, kb, qd, kbe, kd, vb = (held(part, n, [P, 4, P]) for n in
                                               ("qn", "kn", "kb", "qd", "kbe", "kd", "vb"))
                kqT = held(part, "kqT", [P, 2, 4 * P])
                kbT, qdT, ATm, LTm, XT, S = (held(part, n, [P, 4 * P]) for n in (
                    "kbT", "qdT", "ATm", "LTm", "XT", "S"))
                flat4 = lambda ap: ap.rearrange("p h k -> p (h k)")
                X, Lb, Y = kbT, kqT, flat4(sq2[:, 4:8, :])
                wkT, us, of = flat4(qn[:]), flat4(kb[:]), gB
            part = ExitStack()
            with part:
                sS = held(part, "sS", [P, DN_H, SAMPLES, P])
                sin = held(part, "sin", [P, 16, SAMPLES])
                s64 = held(part, "s64", [P, 6, 64])
                sdv = held(part, "sdv", [P, 4, P])
                sdiag = held(part, "sdiag", [SAMPLES, 2, SAMPLES, DN_H])
                sof = held(part, "sof", [P, DN_H, SAMPLES])

        late = ExitStack()
        with late:
            hh = held(late, "hh", [P, KT, TOK], F32R)
            hl = held(late, "hl", [P, KT, TOK], F32R)
            acc = held(late, "acc", [P, KT, TOK])
            ab = held(late, "ab", [P, 2 + TOK])
            cc = held(late, "cc", [P, TOK])
            gl = held(late, "gl", [P, TOK])
            fstate = held(late, "fstate", [P, FT, SAMPLES, 2])
            ftails = held(late, "ftails", [P, FT, 10])
            stats = held(late, "stats", [P, 2, 6])
            mv = held(late, "mv", [P, 4])
            mt = ab[:, 0:TW]
            xn = gl[:, 0:D_MODEL]
        with ExitStack() as part:
            g2r = held(part, "g2r", [P, D_MODEL])
            b2r = held(part, "b2r", [P, D_MODEL])
            yt = held(part, "yt", [P, 2, D_MODEL])

        U = ctx.enter_context(nc.psum_tensor("U", [P, 3, 512], F32))
        B34 = ctx.enter_context(nc.psum_tensor("B34", [P, 2, 512], F32))
        B56 = ctx.enter_context(nc.psum_tensor("B56", [P, 2, 512], F32))
        B7 = ctx.enter_context(nc.psum_tensor("B7", [P, 512], F32))

        consts_in = sem("consts_in")
        x_in = [sem(f"x_in{i}") for i in range(4)]
        x_hi, x_lo, conv_in = sem("x_hi"), sem("x_lo"), sem("conv_in")
        zeroed = sem("zeroed")
        w_in = [sem("w_in0"), sem("w_in1")]
        w_hi, w_lo = sem("w_hi"), sem("w_lo")
        slice_done = sem("slice_done")
        taken = sem("taken")
        ba_done, ba_raw, ba_act, ba_dve = sem("ba_done"), sem("ba_raw"), sem("ba_act"), sem("ba_dve")
        bias_in = sem("bias_in")
        qk_staged, v_staged = sem("qk_staged"), sem("v_staged")
        s_done, biased, maxed, exped = sem("s_done"), sem("biased"), sem("maxed"), sem("exped")
        pt_done, pt_taken = sem("pt_done"), sem("pt_taken")
        v_done, v_taken = sem("v_done"), sem("v_taken")
        pv_done, o_taken = sem("pv_done"), sem("o_taken")
        o_stored = [sem("o_stored0"), sem("o_stored1")]
        kv_stored = sem("kv_stored")
        conv_step, conv_tanh, conv_out, conv_stored, tail_stored = (
            sem("conv_step"), sem("conv_tanh"), sem("conv_out"), sem("conv_stored"), sem("tail_stored"))
        small_step = sem("small_step")
        pe_step, act_step, pool_step = sem("pe_step"), sem("act_step"), sem("pool_step")
        samp_in, samp_pe, samp_act, samp_dve = sem("samp_in"), sem("samp_pe"), sem("samp_act"), sem("samp_dve")
        dcst_in, dn_in, z_in, att_in = sem("dcst_in"), sem("dn_in"), sem("z_in"), sem("att_in")
        used = sem("used")
        gates_in = [sem("gates_in0"), sem("gates_in1")]
        merged, m_high, m_low, acc_in = sem("merged"), sem("m_high"), sem("m_low"), sem("acc_in")
        ln_in, ln_var, ln_root, ln_shift, ln_norm, ln_back, ln_h, h_high, h_low, ln_step2, ln_mul = (
            sem(n) for n in ("ln_in", "ln_var", "ln_root", "ln_shift", "ln_norm", "ln_back", "ln_h", "h_high",
                             "h_low", "ln_step2", "ln_mul"))
        fstate_in, f_zero, a_taken, f_step, f_gelu, f_prod, f_high, f_low = (
            sem(n) for n in ("fstate_in", "f_zero", "a_taken", "f_step", "f_gelu", "f_prod", "f_high", "f_low"))
        rows2_in, y_ready, y_stored, ftail_stored = sem("rows2_in"), sem("y_ready"), [sem("y_s0"), sem("y_s1")], sem("ftail_stored")
        ds_in, ds_pe, ds_act, ds_dve, ds_scaled, ds_prod, ds_new, ds_o = (
            sem(n) for n in ("ds_in", "ds_pe", "ds_act", "ds_dve", "ds_scaled", "ds_prod", "ds_new", "ds_o"))
        half_set = sem("half_set")
        ss_ready, rs_ready = sem("ss_ready"), sem("rs_ready")
        cf_pe, cf_dve, cf_act = sem("cf_pe"), sem("cf_dve"), sem("cf_act")
        g_staged, g_done, decay_sum, decay_exp = sem("g_staged"), sem("g_done"), sem("decay_sum"), sem("decay_exp")
        tr1_done, squared, qkn_ready, kbqd_ready = sem("tr1_done"), sem("squared"), sem("qkn_ready"), sem("kbqd_ready")
        v_ready, tr2_done, kqT_taken, tr3_done, kbqd_taken = (
            sem("v_ready"), sem("tr2_done"), sem("kqT_taken"), sem("tr3_done"), sem("kbqd_taken"))
        la_done, y_done, y_taken, zt_done, xt_ready, x_done, x_taken = (
            sem("la_done"), sem("y_done"), sem("y_taken"), sem("zt_done"), sem("xt_ready"), sem("x_done"),
            sem("x_taken"))
        wk_done, wk_taken, u_done, u_taken, od_done, s_ready = (
            sem("wk_done"), sem("wk_taken"), sem("u_done"), sem("u_taken"), sem("od_done"), sem("s_ready"))
        o_squared, on_ready, on_done, of_ready, of_high, of_low = (
            sem("o_squared"), sem("on_ready"), sem("on_done"), sem("of_ready"), sem("of_high"), sem("of_low"))
        ae_ready, ae_exp, ao_ready, ao_done, ao_high, ao_low = (
            sem("ae_ready"), sem("ae_exp"), sem("ao_ready"), sem("ao_done"), sem("ao_high"), sem("ao_low"))
        gate_stored, dn_step, shifted, state_stored, pad_stored = (
            sem("gate_stored"), sem("dn_step"), sem("shifted"), sem("state_stored"), sem("pad_stored"))


        GT = (0, 12, 6)
        ALL_QKV = 3 * U_DN

        def pairs(eng, first, count):
            with eng.Fori(0, count // 2) as i:
                for half in (0, 1):
                    yield i * 2 + (first + half), half, i

        def peeled(first, count):
            for n in range(first, first + count):
                yield n, n % 2, None

        def after(eng, s, n):
            if not (isinstance(n, int) and n <= 0):
                eng.wait_ge(s, n)

        def bulk(eng):
            yield from peeled(0, 2)
            yield from pairs(eng, 2, U_BLK - 2)

        class Steps:

            def __init__(self, eng, s):
                self.eng, self.s, self.base, self.n = eng, s, 0, 0

            def item(self, index, per):
                self.base, self.n, self.per = index * per, 0, per

            def link(self, ins):
                self.n += 1
                ins.then_inc(self.s, 1)
                self.eng.wait_ge(self.s, self.base + self.n)

        def blocks_of(eng, before_group=None):
            for b, par, _ in peeled(0, 2):
                yield b, par, 0, b, b > 0, "att"
            for b, par, i in pairs(eng, 2, 6):
                yield b, par, 0, b, True, "att"
            if before_group:
                before_group(1)
            for b, par, i in pairs(eng, BLOCKS, BLOCKS):
                yield b, par, 1, (i, par), par == 1, "dn"
            if before_group:
                before_group(2)
            for b, par, i in pairs(eng, 2 * BLOCKS, 4):
                yield b, par, 2, i * 2 + par, False, "dn"
            for b, par, i in pairs(eng, 2 * BLOCKS + 4, 4):
                yield b, par, 2, i * 2 + (4 + par), False, "z"

        def cols(tiles, g, n):
            if g == 0:
                return tiles[:, :, bass.ds(n * P, P)]
            v = tiles.rearrange("p j (i d) -> p j d i", d=DIL[g][1])
            if g == 1:
                return v[:, :, bass.ds(n[0], 1), n[1] * P:(n[1] + 1) * P].squeeze(2)
            return v[:, :, bass.ds(n * 2, 2), :]

        def packed(t, g):
            return t.rearrange("p j (d i) -> p j d i", d=2) if g == 2 else t

        def stored_before(b, par, g, n):
            if g == 0:
                return (b - par) * 8
            if g == 1:
                return n[0] * 16 + 64
            return (n - par) * 16 + 128

        CHUNKS = 36
        LEVELS = 6

        class Beside:

            def __init__(self, u, chunk, start_unit):
                self.u, self.chunk, self.start_unit, self.c = u, chunk, start_unit, 0

            def run(self, n):
                for c in range(self.c, min(self.c + n, CHUNKS)):
                    if c % 18 == 0:
                        self.start_unit(self.u + c // 18, c // 18)
                    self.chunk(self.u + c // 18, c // 18, c % 18 // 6, c % 6)
                self.c = min(self.c + n, CHUNKS)

        def windows():
            for t in range(TILES + 1):
                yield t, t % 2, slice(t * P, min((t + 1) * P, TOK)), min(P, TOK - t * P)

        def pieces():
            f0, u0, before = 0, U_FFN, 3 * (U_FFN - U_BRANCH)
            for n in PIECES:
                yield n, f0, u0, before
                f0, u0, before = f0 + n, u0 + 2 * n + KT, before + 3 * KT

        block = ctx.enter_context(nc.Block())

        @block.sync
        def _(sp):
            for i in range(4):
                sp.dma_start(xraw[:, 2 * i:2 * i + 2, :], I["xT"][:, 2 * i:2 * i + 2, :]).then_inc(x_in[i], 16)
                if i < 2:
                    sp.dma_start(stage[:, i, :], I["wu"][i]).then_inc(w_in[i], 16)

            def load(u, par):
                sp.wait_ge(w_lo, u - 1)
                sp.dma_start(stage[:, par, :], I["wu"][bass.ds(u, 1)].squeeze(0)).then_inc(w_in[par], 16)

            sp.dma_start(dn_scr[0:12, :, TOK:SEQ + P], I["wu"][0:12, :, 0:SEQ + P - TOK]).then_inc(pad_stored, 16)
            sp.dma_start(O["dnrows"], I["dnrows"][:, 1:3, :]).then_inc(shifted, 16)
            sp.dma_start(O["ffnrows"], I["ffnrows"][:, 1:2, :]).then_inc(shifted, 16)
            for u, par, _ in bulk(sp):
                load(u + 2, par)

            def next_bias(g):
                sp.wait_ge(biased, g * BLOCKS)
                sp.dma_start(bias[:], I["bias"][g]).then_inc(bias_in, 16)

            for b, par, g, n, prev, kind in blocks_of(sp, next_bias):
                load(b + (U_BLK + 2), par)
                sp.wait_ge(o_taken, b + 1)
                src = obuf[:, par, :, :].rearrange("p h c -> p (h c)")
                if g == 0:
                    sp.dma_start(att_scr[0][bass.ds(b * P, P), :], src).then_inc(o_stored[par], 16)
                elif g == 1:
                    dst = att_scr[1].rearrange("(i d) c -> d i c", d=4)
                    sp.dma_start(dst[bass.ds(n[0], 1), par * P:(par + 1) * P, :].squeeze(0), src).then_inc(
                        o_stored[par], 16)
                else:
                    dst = att_scr[2].rearrange("(i d) c -> d i c", d=16)
                    for r in range(2):
                        sp.dma_start(dst[bass.ds(n * 2 + r, 1)].squeeze(0), src[64 * r:64 * r + 64, :]).then_inc(
                            o_stored[par], 16)
                if kind != "att":
                    f = b - BLOCKS
                    sp.wait_ge(conv_out, f + 2)
                    sp.dma_start(dn_scr[bass.ds(f, 1), :, 0:TOK].squeeze(0), cb[:]).then_inc(conv_stored, 16)
            sp.wait_ge(taken, ALL_QKV)
            sp.dma_start(O["dnconv"], tails[:]).then_inc(tail_stored, 16)
            for g in range(GROUPS):
                keep = min(DIL[g][0], SEQ)
                sp.dma_start(O[f"kv{g}"], qkv[:, GT[g] + 2:GT[g] + 6, SEQ - keep:TOK]).then_inc(kv_stored, 16)
            sp.wait_ge(kv_stored, 48)
            sp.wait_ge(conv_stored, 16 * 16)
            sp.wait_ge(tail_stored, 16)
            for par in (0, 1):
                sp.wait_ge(o_stored[par], 16 * (4 + 4 + 8))
            sp.wait_ge(pv_done, 24)
            sp.wait_ge(samp_act, 1)
            k0 = 0
            for g in (0, 2, 1):
                src = I[f"cache{g}"].rearrange("b (c j d) e -> (b c) j d e", c=16, d=DIL[g][1])
                sp.dma_start(kvc[:, k0:k0 + SKEYS[g]].rearrange("p j a e -> p j (a e)"), src[:, :, 0, :]).then_inc(
                    samp_in, 16)
                k0 += SKEYS[g]
            sp.dma_start(sbias[:], I["sbias"]).then_inc(samp_in, 16)
            sp.dma_start(rt[:], I["rt"]).then_inc(samp_in, 16)
            sp.wait_ge(ao_low, 1)
            sp.dma_start(dcst[:], I["dcst"]).then_inc(dcst_in, 16)

            def rows_in(t):
                sp.dma_start(dnin[:], dn_scr[0:12, :, bass.ds(t * P, P)].rearrange("f p t -> p f t")).then_inc(
                    dn_in, 16)

            sp.wait_ge(pad_stored, 16)
            rows_in(0)
            with sp.Fori(0, TILES) as t:
                u = t * 2 + U_GATE
                load(u + 2, 0)
                after(sp, of_low, t)
                sp.dma_start(zin[:], dn_scr[12:16, :, bass.ds(t * P, P)].rearrange("f p t -> p f t")).then_inc(z_in, 16)
                sp.wait_ge(ao_low, t + 1)
                sp.dma_start(abuf[:].rearrange("p g h c -> p g (h c)"),
                             att_scr[:, bass.ds(t * P, P), :].rearrange("g t c -> t g c")).then_inc(att_in, 16)
                for g in range(GROUPS):
                    sp.dma_start(O[f"shift{g}"][bass.ds(t, 1)], I[f"cache{g}"][bass.ds(t, 1), 1:, :]).then_inc(
                        shifted, 16)
                sp.wait_ge(v_ready, t + 1)
                sp.dma_start(dnin[:], dn_scr[0:12, :, bass.ds((t + 1) * P, P)].rearrange("f p t -> p f t")).then_inc(
                    dn_in, 16)
                load(u + 3, 1)
                for half in (0, 1):
                    sp.wait_ge(taken, (u + (half + 1)) * 3)
                    sp.dma_start(gate_scr[bass.ds(t * 2 + half, 1)].squeeze(0), gth[:, half, :]).then_inc(
                        gate_stored, 16)
            sp.wait_ge(s_ready, TILES + 1)
            sp.dma_start(O["pS"], S[:]).then_inc(state_stored, 16)
            sp.wait_ge(state_stored, 16)
            sp.wait_ge(of_low, TILES)
            sp.dma_start(sS[:], I["sS"]).then_inc(ds_in, 16)
            sp.dma_start(sin[:], dn_scr[:, :, SEQ:TOK].rearrange("f p b -> p f b")).then_inc(ds_in, 16)
            sp.wait_ge(ds_new, 8)
            sp.dma_start(O["sS"], sS[:]).then_inc(state_stored, 16)
            sp.wait_ge(of_low, TILES + 1)
            sp.wait_ge(state_stored, 32)
            sp.wait_ge(gate_stored, 16 * 16)
            sp.wait_ge(shifted, 16 * 26)

            def gates_of(f, par):
                sp.dma_start(gates[:, par, :, :], gate_scr[bass.ds(f * 2, 2)].rearrange("g p t -> p g t")).then_inc(
                    gates_in[par], 16)

            gates_of(0, 0)
            gates_of(1, 1)
            sp.dma_start(acc[:], I["xT"]).then_inc(acc_in, 16)
            sp.dma_start(fstate[:], I["fstate"]).then_inc(fstate_in, 16)
            for f, par, _ in pairs(sp, 0, KT - 2):
                load(f + (U_BRANCH + 2), par)
                sp.wait_ge(used, f * 3 + 3)
                gates_of(f + 2, par)
            for f in range(KT - 2, KT):
                load(f + (U_BRANCH + 2), f % 2)
            for u, par, _ in pairs(sp, U_MIX + 2, UNITS - U_MIX - 2):
                load(u, par)
            sp.wait_ge(used, LAST_USED)
            sp.wait_ge(f_low, FT)
            sp.wait_ge(slice_done, 3 * UNITS)
            sp.dma_start(O["ffnconv"], ftails[:]).then_inc(ftail_stored, 16)
            sp.dma_start(g2r[:], I["g2"].to_broadcast([P, D_MODEL])).then_inc(rows2_in, 16)
            sp.dma_start(b2r[:], I["b2"].to_broadcast([P, D_MODEL])).then_inc(rows2_in, 16)
            for t, par, win, m in windows():
                sp.wait_ge(y_ready, t + 1)
                sp.dma_start(O["y"][win, :], yt[0:m, par, :]).then_inc(y_stored[par], 16)
            sp.wait_ge(y_stored[0], 16 * 5)
            sp.wait_ge(y_stored[1], 16 * 4)
            sp.wait_ge(ftail_stored, 16)

        @block.gpsimd
        def _(pool):
            def low(u, par):
                pool.wait_ge(w_hi, u + 1)
                nc.gpsimd.tensor_tensor(wl[:, par, :], stage[:, par, :], wh[:, par, :].bitcast(F32),
                                        ALU.subtract).then_inc(w_lo, 1)

            def inverse_root(x, n):
                pool.wait_ge(ss_ready, n)
                nc.gpsimd.tensor_tensor(x, x, mhalf[:, 0:x.shape[1]], ALU.pow).then_inc(rs_ready, 1)

            nc.gpsimd.memset(mhalf[:], -0.5).then_inc(half_set, 1)
            for u, par, _ in pairs(pool, 0, U_GATE):
                low(u, par)
            pool.wait_ge(half_set, 1)
            low(U_GATE, 0)
            with pool.Fori(0, TILES) as t:
                low(t * 2 + (U_GATE + 1), 1)
                inverse_root(rn[:, 1, :], t * 2 + 1)
                low(t * 2 + (U_GATE + 2), 0)
                inverse_root(rn[:, 1, 0:4], t * 2 + 2)
            inverse_root(s64[:, 1, :], 2 * TILES + 1)
            inverse_root(s64[:, 1, 0:32], 2 * TILES + 2)

            def layer_norm(first):
                for t, par, win, m in windows():
                    pool.wait_ge(ln_var, t + (first + 1))
                    nc.gpsimd.tensor_tensor(mv[0:m, 2:3], mv[0:m, 1:2], mhalf[0:m, 0:1], ALU.pow).then_inc(ln_root, 1)

            for u, par, _ in pairs(pool, U_BRANCH + 1, U_FFN - U_BRANCH):
                low(u, 1 - par)
            layer_norm(0)
            for u, par, _ in pairs(pool, U_FFN + 1, UNITS - U_FFN - 2):
                low(u, 1 - par)
            low(UNITS - 1, 1)
            layer_norm(TILES + 1)


        @block.tensor
        def _(pe):
            def products(dst, par, j, ks, x=None):
                hi, lo = x or (xh, xl)
                for n, (k, xk) in enumerate(ks):
                    w = slice(k * P, (k + 1) * P)
                    for m, (a, b) in enumerate(((wh, hi), (wl, hi), (wh, lo))):
                        ins = nc.tensor.matmul(dst, a[:, par, w], b[:, xk, third(j)],
                                               start=n == 0 and m == 0, stop=n == len(ks) - 1 and m == 2)
                return ins

            def unit_slice(u, par, j):
                after(pe, taken, u * 3 + (j - 2))
                pe.wait_ge(w_lo, u + 1)
                products(U[:, j, 0:TW], par, j, [(k, k) for k in range(KT)]).then_inc(slice_done, 1)

            pe.wait_ge(consts_in, 16 * N_CONSTS)
            for i in range(4):
                pe.wait_ge(x_in[i], 16)
            for t in range(9):
                m = P if t < TILES else SAMPLES
                for k in range(KT):
                    ins = nc.tensor.matmul(B7[0:m, 8 * t:8 * t + 8], xraw[:, k, t * P:t * P + m], wba[:, k, :],
                                           start=k == 0, stop=k == KT - 1)
            ins.then_inc(ba_done, 1)
            pe.wait_ge(x_lo, KT)
            for u, par, _ in bulk(pe):
                for j in range(THIRDS):
                    unit_slice(u, par, j)
            pe.wait_ge(ba_raw, 1)
            for b, par, g, n, prev, kind in blocks_of(pe):
                u = b + U_BLK
                parts = 2 if prev else 1
                unit_slice(u, par, 0)
                pe.wait_ge(qk_staged, b + 1)
                after(pe, biased, b)
                for h in range(HPG):
                    hp, j = h % 2, h // 2
                    rows = slice(64 * hp, 64 * hp + 64)
                    for part in range(parts):
                        ins = nc.tensor.matmul(B34[:, hp, j * 256 + part * P:j * 256 + (part + 1) * P],
                                               q_st[rows, j, :], k_st[rows, (par + part) % 2, j, :],
                                               start=True, stop=True)
                ins.then_inc(s_done, 1)
                pe.wait_ge(v_staged, b + 1)
                after(pe, v_taken, b)
                after(pe, o_taken, b)
                for j in range(2):
                    ins = nc.tensor.transpose(B7[:, j * P:(j + 1) * P], v_st[:, j, :], ident)
                ins.then_inc(v_done, 1)
                unit_slice(u, par, 1)
                pe.wait_ge(exped, b + 1)
                after(pe, pt_taken, b)
                for slot in range(HPG):
                    for part in range(parts):
                        c = ((slot % 2) * 2 + part) * P
                        ins = nc.tensor.transpose(B56[:, slot // 2, c:c + P], pb[:, slot, part, :], ident)
                ins.then_inc(pt_done, 1)
                unit_slice(u, par, 2)
                pe.wait_ge(pt_taken, b + 1)
                pe.wait_ge(v_taken, b + 1)
                for h in range(HPG):
                    slot = (h % 2) * 2 + h // 2
                    for part in range(parts):
                        ins = nc.tensor.matmul(B7[:, 256 + 64 * h:256 + 64 * h + 64], pts[:, 2 * slot + part, :],
                                               vtok[:, (par + part) % 2, 64 * h:64 * h + 64],
                                               start=part == 0, stop=part == parts - 1)
                ins.then_inc(pv_done, 1)

            def step(ins):
                ins.then_inc(samp_pe, 1)

            pe.wait_ge(o_taken, 24)
            pe.wait_ge(pt_taken, 24)
            pe.wait_ge(biased, 24)
            pe.wait_ge(v_taken, 24)
            for n in range(18):
                dst = (B34, B56, B7)[n // 8]
                dst = dst[0:SAMPLES, n % 8 // 4, n % 4 * P:(n % 4 + 1) * P] if n < 16 else \
                    B7[0:SAMPLES, (n - 16) * P:(n - 15) * P]
                ins = nc.tensor.matmul(dst, qkv[:, n, SEQ:TOK], ident, start=True, stop=True)
            step(ins)
            pe.wait_ge(samp_act, 2)
            for n in range(3):
                ins = nc.tensor.matmul(B34[:, n // 2, n % 2 * 256:n % 2 * 256 + 256], cst[0:SAMPLES, C_R:C_END],
                                       sq[:, n, 0, :], start=True, stop=True)
            step(ins)
            pe.wait_ge(samp_dve, 1)
            nc.tensor.matmul(B7[0:4, 0:P], sm[:, 0, :], ident, start=True, stop=True)
            ins = nc.tensor.matmul(B7[0:4, P:P + SAMPLES], sm[0:SAMPLES, 1, :], ident[0:SAMPLES, 0:SAMPLES],
                                   start=True, stop=True)
            step(ins)
            pe.wait_ge(samp_dve, 2)
            step(nc.tensor.matmul(B34[0:SAMPLES, 0, 0:4], sm[0:4, 4:6, :].rearrange("p a c -> p (a c)"),
                                  ident[0:4, 0:4], start=True, stop=True))
            pe.wait_ge(samp_dve, 3)
            step(nc.tensor.matmul(B56[:, 0, 0:4], cst[0:SAMPLES, C_R:C_END], sm[0:SAMPLES, 6, :],
                                  start=True, stop=True))
            pe.wait_ge(samp_dve, 4)
            pe.wait_ge(samp_in, 16 * 5)
            for n in range(3):
                nc.tensor.matmul(B7[0:SAMPLES, 0:256], rt[:], og[:, n, :], start=n == 0, stop=False)
            for n in range(3):
                nc.tensor.matmul(B7[0:SAMPLES, 0:256], ident[0:SAMPLES, 0:SAMPLES], self_p[:, n, :], start=False,
                                 stop=n == 2)
            nc.tensor.matmul(B7[0:SAMPLES, 256:260], rt[:], sm[:, 7, :], start=True, stop=False)
            for n in range(3):
                ins = nc.tensor.matmul(B7[0:SAMPLES, 256:260], ident[0:SAMPLES, 0:SAMPLES], self_s[:, n, :],
                                       start=False, stop=n == 2)
            step(ins)
            pe.wait_ge(samp_dve, 5)
            for n in range(2):
                ins = nc.tensor.matmul(B34[:, 1, n * SAMPLES:(n + 1) * SAMPLES], o8[:, n * P:(n + 1) * P],
                                       ident[0:SAMPLES, 0:SAMPLES], start=True, stop=True)
            step(ins)

            pe.wait_ge(ao_low, 1)
            pe.wait_ge(dcst_in, 16)
            gall = babuf[:, 1, 0:TILES, :]
            tri = dcst[:, D_TRI:D_TRI + P]
            nc.tensor.matmul(B7[:, 0:32], tri, gall, start=True, stop=True)
            nc.tensor.matmul(B7[:, 32:64], dcst[:, D_ONE:D_ONE + P], gall, start=True, stop=True).then_inc(cf_pe, 1)
            pe.wait_ge(cf_act, 3)

            def start_unit(u, par):
                pe.wait_ge(w_lo, u + 1)

            def chunk(u, par, j, c):
                if c == 0:
                    pe.wait_ge(taken, u * 3 + (j - 2))
                for m in range(4 * c, 4 * c + 4):
                    a, x = ((wh, xh), (wl, xh), (wh, xl))[m % 3]
                    k = m // 3
                    ins = nc.tensor.matmul(U[:, j, 0:TW], a[:, par, k * P:(k + 1) * P], x[:, k, third(j)],
                                           start=m == 0, stop=m == 3 * KT - 1)
                if c == 5:
                    ins.then_inc(slice_done, 1)

            def heads():
                return [(h, slice(h * P, (h + 1) * P)) for h in range(DN_H)]

            with pe.Fori(0, TILES) as t:
                beside = Beside(t * 2 + U_GATE, chunk, start_unit)
                pe.wait_ge(dn_in, t * 16 + 16)
                pe.wait_ge(of_low, t)
                pe.wait_ge(s_ready, t + 1)
                for n in range(12):
                    dst = (B34[:, 0, :], B34[:, 1, :], B56[:, 0, :])[n // 4]
                    ins = nc.tensor.transpose(dst[:, n % 4 * P:(n % 4 + 1) * P], dnin[:, n, :], ident)
                ins.then_inc(tr1_done, 1)
                pe.wait_ge(g_staged, t + 1)
                for h, c in heads():
                    ins = nc.tensor.matmul(B56[:, 1, c], gB[:, h, :], tri, start=True, stop=True)
                ins.then_inc(g_done, 1)
                beside.run(4)
                pe.wait_ge(ao_ready, t + 1)
                for n in range(2):
                    ins = nc.tensor.transpose(B7[:, n * P:(n + 1) * P], ao[:].rearrange("p h e -> p (h e)")[
                        :, n * P:(n + 1) * P], ident)
                ins.then_inc(ao_done, 1)
                beside.run(2)
                pe.wait_ge(qkn_ready, t + 1)
                for src, dst in ((kn, B34[:, 0, :]), (qn, B34[:, 1, :])):
                    for h, c in heads():
                        ins = nc.tensor.transpose(dst[:, c], src[:, h, :], ident)
                ins.then_inc(tr2_done, 1)
                beside.run(2)
                pe.wait_ge(kbqd_ready, t + 1)
                pe.wait_ge(v_ready, t + 1)
                pe.wait_ge(ao_low, t + 2)
                for src, dst in ((kb, B56[:, 0, :]), (qd, B7[:, :])):
                    for h, c in heads():
                        ins = nc.tensor.transpose(dst[:, c], src[:, h, :], ident)
                ins.then_inc(tr3_done, 1)
                beside.run(3)
                pe.wait_ge(kqT_taken, t + 1)
                pe.wait_ge(kbqd_taken, t + 1)
                for rhs, dst in ((kbT, B34[:, 0, :]), (kqT[:, 1, :], B34[:, 1, :])):
                    for h, c in heads():
                        ins = nc.tensor.matmul(dst[:, c], kqT[:, 0, c], rhs[:, c], start=True, stop=True)
                ins.then_inc(la_done, 1)
                beside.run(4)
                for lv in range(LEVELS + 1):
                    if lv < LEVELS:
                        pe.wait_ge(xt_ready, t * (LEVELS + 1) + (lv + 1))
                        after(pe, x_taken, t * LEVELS + lv)
                        for h, c in heads():
                            ins = nc.tensor.transpose(B56[:, 0, c], XT[:, c], ident)
                        ins.then_inc(x_done, 1)
                        beside.run(1)
                        pe.wait_ge(x_taken, t * LEVELS + (lv + 1))
                        for h, c in heads():
                            ins = nc.tensor.matmul(B56[:, 1, c], Lb[:, (lv + 1) % 2, c], X[:, c], start=True, stop=True)
                        ins.then_inc(y_done, 1)
                        beside.run(1)
                        pe.wait_ge(y_taken, t * LEVELS + (lv + 1))
                        for h, c in heads():
                            ins = nc.tensor.matmul(B7[:, c], Y[:, c], XT[:, c], start=True, stop=True)
                        ins.then_inc(zt_done, 1)
                        beside.run(1)
                pe.wait_ge(xt_ready, t * (LEVELS + 1) + (LEVELS + 1))
                for h, c in heads():
                    ins = nc.tensor.matmul(B34[:, 0, c], kbe[:, h, :], XT[:, c], start=True, stop=True)
                ins.then_inc(wk_done, 1)
                beside.run(1)
                pe.wait_ge(wk_taken, t + 1)
                for h, c in heads():
                    nc.tensor.matmul(B34[:, 1, c], XT[:, c], vb[:, h, :], start=True, stop=False)
                    ins = nc.tensor.matmul(B34[:, 1, c], wkT[:, c], S[:, c], start=False, stop=True)
                ins.then_inc(u_done, 1)
                beside.run(1)
                pe.wait_ge(u_taken, t + 1)
                for h, c in heads():
                    nc.tensor.matmul(B56[:, 0, c], qdT[:, c], S[:, c], start=True, stop=False)
                    nc.tensor.matmul(B56[:, 0, c], ATm[:, c], us[:, c], start=False, stop=True)
                for h, c in heads():
                    ins = nc.tensor.matmul(B56[:, 1, c], kd[:, h, :], us[:, c], start=True, stop=True)
                ins.then_inc(od_done, 1)
                beside.run(1)
                pe.wait_ge(on_ready, t + 1)
                for h, c in heads():
                    ins = nc.tensor.transpose(B7[:, c], of[:, h, :], ident)
                ins.then_inc(on_done, 1)
                beside.run(CHUNKS)


            pe.wait_ge(of_low, TILES)
            pe.wait_ge(ds_dve, 1)
            nc.tensor.matmul(B34[:, 0, 0:64], dcst[0:SAMPLES, D_ONE:D_ONE + P],
                             sdiag[:].rearrange("s x b h -> s (x b h)"), start=True, stop=True).then_inc(ds_pe, 1)
            pe.wait_ge(ds_act, 2)
            nc.tensor.matmul(B34[:, 1, 0:64], dcst[:, D_ONE:D_ONE + P], s64[:, 0, :], start=True,
                             stop=True).then_inc(ds_pe, 1)
            pe.wait_ge(ds_dve, 2)
            for n in range(8):
                h, b0 = n // 2, n % 2 * 4
                pe.wait_ge(ds_scaled, n + 1)
                bank = B56[:, n % 2, :]
                for i in range(4):
                    c = slice(i * P, (i + 1) * P)
                    col = h * SAMPLES + b0 + i
                    nc.tensor.matmul(bank[:, c], s64[:, 4, col:col + 1].to_broadcast([P, P]), sS[:, h, b0 + i, :],
                                     start=True, stop=False)
                    ins = nc.tensor.matmul(bank[:, c], dcst[:, D_ONE:D_ONE + P], sdv[:, i, :], start=False, stop=True)
                ins.then_inc(ds_prod, 1)
                pe.wait_ge(ds_new, n + 1)
                for i in range(4):
                    col = h * SAMPLES + b0 + i
                    ins = nc.tensor.matmul(B7[:, col:col + 1], sS[:, h, b0 + i, :], s64[:, 2, col:col + 1], start=True,
                                           stop=True)
            ins.then_inc(ds_o, 1)
            pe.wait_ge(ds_act, 3)
            nc.tensor.matmul(B34[:, 1, 0:32], dcst[:, D_ONE:D_ONE + P], s64[:, 0, 0:32], start=True,
                             stop=True).then_inc(ds_pe, 1)

            dbank = (B34[:, 0, :], B34[:, 1, :], B56[:, 0, :])
            pe.wait_ge(of_low, TILES + 1)
            pe.wait_ge(taken, 3 * U_BRANCH)

            def branch(f, par, skip_wait):
                u = f + U_BRANCH
                pe.wait_ge(w_lo, u + 1)
                for j in range(THIRDS):
                    if not skip_wait:
                        pe.wait_ge(used, f * 3 + (j - 2))
                    products(U[:, j, 0:TW], par, j, [(k, k) for k in range(2)], (oh, ol))
                    products(dbank[j][:, 0:TW], par, j, [(k, k) for k in range(2, 6)], (oh, ol)).then_inc(slice_done, 1)

            for f in range(2):
                branch(f, f, f == 0)
            for f, par, _ in pairs(pe, 2, KT - 2):
                branch(f, par, False)
            pe.wait_ge(m_low, 3 * KT)

            def from_used(u, par, j, n, parts, ks):
                pe.wait_ge(used, n)
                pe.wait_ge(w_lo, u + 1)
                products(U[:, j, 0:TW], par, j, ks, parts).then_inc(slice_done, 1)

            all_k = [(k, k) for k in range(KT)]
            for f, par, _ in pairs(pe, 0, KT):
                for j in range(THIRDS):
                    from_used(f + U_MIX, par, j, f * 3 + (3 * KT + j - 2), (xh, xl), all_k)

            def layer_norm(first, back):
                for t, par, win, m in windows():
                    bank = (B34, B56)[par]
                    after(pe, ln_norm, t + first)
                    for k in range(KT):
                        ins = nc.tensor.transpose(bank[0:m, k // 4, k % 4 * P:(k % 4 + 1) * P], acc[:, k, win], ident)
                    ins.then_inc(ln_in, 1)
                    if back:
                        pe.wait_ge(ln_norm, t + (first + 1))
                        after(pe, ln_h, t)
                        for k in range(KT):
                            ins = nc.tensor.transpose(U[:, k // 4, k % 4 * P:k % 4 * P + m],
                                                      xn[0:m, k * P:(k + 1) * P], ident[0:m, 0:m])
                        ins.then_inc(ln_back, 1)

            pe.wait_ge(used, 3 * (U_FFN - U_BRANCH))
            layer_norm(0, True)
            pe.wait_ge(h_low, TILES + 1)
            for n, f0, u0, before in pieces():
                pe.wait_ge(used, before)
                for p, par, i in pairs(pe, 0, n):
                    for j in range(THIRDS):
                        after(pe, f_prod, (p + f0) * 3)
                        pe.wait_ge(w_lo, p * 2 + (u0 + 1))
                        products(U[:, j, 0:TW], 0, j, all_k, (hh, hl)).then_inc(slice_done, 1)
                    for j in range(THIRDS):
                        pe.wait_ge(a_taken, (p + f0) * 3 + (j + 1))
                        pe.wait_ge(w_lo, p * 2 + (u0 + 2))
                        products(U[:, j, 0:TW], 1, j, all_k, (hh, hl)).then_inc(slice_done, 1)
                pe.wait_ge(f_low, f0 + n)
                for f, par, i in pairs(pe, 0, KT):
                    for j in range(THIRDS):
                        from_used(f + (u0 + 2 * n), par, j, f * 3 + (before + j - 2), (xh, xl),
                                  [(k, k) for k in range(n)])
            pe.wait_ge(used, LAST_USED)
            layer_norm(TILES + 1, False)

        @block.scalar
        def _(act):
            act.dma_start(cst[:], I["cst"]).then_inc(consts_in, 16)
            act.dma_start(wba[:], I["wba"]).then_inc(consts_in, 16)
            act.dma_start(sconv[:], I["sconv"]).then_inc(consts_in, 16)
            act.dma_start(bac[:], I["bac"].to_broadcast([P, 2, DN_H])).then_inc(consts_in, 16)
            act.dma_start(bias[:], I["bias"][0]).then_inc(bias_in, 16)

            def high(u, par):
                act.wait_ge(w_in[par], (u - par) * 8 + 16)
                after(act, slice_done, u * 3 - 3)
                nc.scalar.activation(wh[:, par, :], stage[:, par, :], ACT.Copy).then_inc(w_hi, 1)

            def take(u, j, dst):
                act.wait_ge(slice_done, u * 3 + (j + 1))
                nc.scalar.activation(dst, U[:, j, 0:TW], ACT.Copy).then_inc(taken, 1)

            high(0, 0)
            for k in range(KT):
                act.wait_ge(x_in[k // 2], 16)
                nc.scalar.activation(xh[:, k, :], xraw[:, k, :], ACT.Copy).then_inc(x_hi, 1)
            act.wait_ge(ba_raw, 1)
            act.wait_ge(ba_dve, 1)
            nc.scalar.activation(babuf[:, 2], babuf[:, 0], ACT.Tanh, scale=0.5).then_inc(ba_act, 1)
            nc.scalar.activation(babuf[:, 4], babuf[:, 3], ACT.Exp, scale=-1.0).then_inc(ba_act, 1)
            nc.scalar.activation(bac[:, 0, :], bac[:, 0, :], ACT.Exp).then_inc(ba_act, 1)
            act.wait_ge(ba_dve, 2)
            nc.scalar.activation(babuf[:, 5], babuf[:, 4], ACT.Ln).then_inc(ba_act, 1)
            act.wait_ge(x_lo, KT)
            for u, par, _ in bulk(act):
                high(u + 1, 1 - par)
                for j in range(THIRDS):
                    take(u, j, qkv[:, bass.ds(u, 1), third(j)].squeeze(1))
            act.wait_ge(zeroed, 1)
            for b, par, g, n, prev, kind in blocks_of(act):
                u = b + U_BLK
                parts = 2 if prev else 1
                high(u + 1, 1 - par)

                def take_part(j):
                    if kind == "att":
                        take(u, j, qkv[:, bass.ds(u, 1), third(j)].squeeze(1))
                        return
                    if j == 0:
                        act.wait_ge(conv_out, b - BLOCKS)
                    take(u, j, pre[:, par, 3 + j * TW:3 + (j + 1) * TW])

                take_part(0)
                act.wait_ge(v_done, b + 1)
                after(act, pv_done, b)
                nc.scalar.activation(vtok[:, par, :], B7[:, 0:256], ACT.Copy).then_inc(v_taken, 1)
                act.wait_ge(maxed, b + 1)
                after(act, pt_done, b)
                after(act, o_stored[par], stored_before(b, par, g, n))
                for slot in range(HPG):
                    h = (slot % 2) * 2 + slot // 2
                    ins = nc.scalar.activation(pb[:, slot, 0:parts, :], sb[:, slot, 0:parts, :], ACT.Exp,
                                               bias=nmax[:, slot:slot + 1], accum_out=obuf[:, par, h, 64:65])
                ins.then_inc(exped, 1)
                take_part(1)
                act.wait_ge(pt_done, b + 1)
                after(act, pv_done, b)
                if parts == 2:
                    src, dst = B56[:, :, :], pts[:].rearrange("p (a c) k -> p a (c k)", a=2)
                else:
                    src = B56[:].rearrange("p a (c t k) -> p a c t k", t=2, k=P)[:, :, :, 0, :]
                    dst = pts[:].rearrange("p (a c t) k -> p a c t k", a=2, t=2)[:, :, :, 0, :]
                nc.scalar.activation(dst, src, ACT.Copy).then_inc(pt_taken, 1)
                take_part(2)
                if kind != "att":
                    f = b - BLOCKS
                    act.wait_ge(conv_out, f + 1)
                if kind == "dn":
                    act.wait_ge(conv_step, f * CONV_STEPS + CONV_STEPS)
                    nc.scalar.activation(thb[:], cb[:], ACT.Tanh, scale=0.5).then_inc(conv_tanh, 1)
                elif kind == "z":
                    act.wait_ge(taken, u * 3 + 3)
                    nc.scalar.activation(thb[:], pre[:, par, 3:3 + TOK], ACT.Tanh, scale=0.5).then_inc(conv_tanh, 1)


            act.wait_ge(samp_pe, 1)
            act.wait_ge(pv_done, 24)
            for par in (0, 1):
                act.wait_ge(o_stored[par], 16 * (4 + 4 + 8))
            act.wait_ge(kv_stored, 48)
            act.wait_ge(conv_stored, 16 * 16)
            act.wait_ge(tail_stored, 16)
            act.wait_ge(conv_out, 17)
            flat = sq[:].rearrange("b g k e -> b (g k e)")
            nc.scalar.activation(flat[:, 0:1024], B34[0:SAMPLES, :, :], ACT.Copy)
            nc.scalar.activation(flat[:, 1024:2048], B56[0:SAMPLES, :, :], ACT.Copy)
            nc.scalar.activation(flat[:, 2048:2304], B7[0:SAMPLES, 0:256], ACT.Copy).then_inc(samp_act, 1)
            act.wait_ge(samp_act, 1)
            nc.scalar.activation(sq[:, :, 0, :], sq[:, :, 0, :], ACT.Copy, scale=HD ** -0.5).then_inc(samp_act, 1)
            act.wait_ge(samp_pe, 2)
            nc.scalar.activation(qb[:, 0:2, :], B34[:, 0, :], ACT.Copy)
            nc.scalar.activation(qb[:, 2, :], B34[:, 1, 0:256], ACT.Copy).then_inc(samp_act, 1)
            act.wait_ge(samp_pe, 5)
            act.wait_ge(samp_dve, 3)
            act.wait_ge(small_step, SMALL_S)
            nc.scalar.activation(ssc[:], ssc[:], ACT.Exp)
            nc.scalar.activation(self_s[:], self_s[:], ACT.Exp).then_inc(samp_act, 1)
            act.wait_ge(samp_pe, 7)
            osp = B34[:, 1, 0:2 * SAMPLES].rearrange("p (n b) -> p n b", n=2)
            nc.scalar.activation(oh[:, 0:2, SEQ:TOK], osp, ACT.Copy).then_inc(ao_high, 1)

            act.wait_ge(cf_pe, 1)
            act.wait_ge(ao_low, 1)
            nc.scalar.activation(cf[:, 1, :], B7[:, 0:32], ACT.Exp)
            nc.scalar.activation(cf[:, 2, :], B7[:, 32:64], ACT.Exp).then_inc(cf_act, 1)
            act.wait_ge(cf_dve, 1)
            nc.scalar.activation(cf[:, 3, :], cf[:, 3, :], ACT.Exp).then_inc(cf_act, 1)
            nc.scalar.activation(onh[:], cst[:, C_ON:C_ON + 1], ACT.Copy, scale=0.5).then_inc(cf_act, 1)

            def start_unit(u, par):
                high(u + 1, 1 - par)

            def chunk(u, par, j, c):
                if c == 5:
                    act.wait_ge(slice_done, u * 3 + (j + 1))
                    if j == 0:
                        after(act, gate_stored, (u - (U_GATE + par)) * 8)
                    nc.scalar.activation(gth[:, par, third(j)], U[:, j, 0:TW], ACT.Tanh, scale=0.5).then_inc(taken, 1)

            with act.Fori(0, TILES) as t:
                beside = Beside(t * 2 + U_GATE, chunk, start_unit)
                act.wait_ge(ae_ready, t + 1)
                nc.scalar.activation(amx[:, 1:4, :], amx[:, 1:4, :], ACT.Exp).then_inc(ae_exp, 1)
                act.wait_ge(tr1_done, t + 1)
                act.wait_ge(of_low, t)
                nc.scalar.activation(sq2[:].rearrange("p (a h) k -> p a (h k)", a=2), B34[:, :, :], ACT.Square,
                                     scale=0.5).then_inc(squared, 1)
                beside.run(4)
                act.wait_ge(ao_done, t + 1)
                nc.scalar.activation(oh[:, 0:2, bass.ds(t * P, P)], B7[:, 0:256].rearrange("p (n k) -> p n k", n=2),
                                     ACT.Copy).then_inc(ao_high, 1)
                act.wait_ge(decay_sum, t + 1)
                act.wait_ge(la_done, t)
                nc.scalar.activation(ET[:], ET[:], ACT.Exp).then_inc(decay_exp, 1)
                beside.run(2)
                act.wait_ge(tr2_done, t + 1)
                nc.scalar.activation(kqT[:], B34[:, :, :], ACT.Copy).then_inc(kqT_taken, 1)
                beside.run(2)
                act.wait_ge(tr3_done, t + 1)
                nc.scalar.activation(kbT[:], B56[:, 0, :], ACT.Copy)
                nc.scalar.activation(qdT[:], B7[:, :], ACT.Copy).then_inc(kbqd_taken, 1)
                beside.run(3)
                act.wait_ge(la_done, t + 1)
                beside.run(4)
                for lv in range(LEVELS):
                    act.wait_ge(x_done, t * LEVELS + (lv + 1))
                    nc.scalar.activation(X[:], B56[:, 0, :], ACT.Copy).then_inc(x_taken, 1)
                    beside.run(1)
                    act.wait_ge(y_done, t * LEVELS + (lv + 1))
                    nc.scalar.activation(Y, B56[:, 1, :], ACT.Copy).then_inc(y_taken, 1)
                    beside.run(1)
                    act.wait_ge(zt_done, t * LEVELS + (lv + 1))
                    beside.run(1)
                act.wait_ge(wk_done, t + 1)
                nc.scalar.activation(wkT, B34[:, 0, :], ACT.Copy, scale=-1.0).then_inc(wk_taken, 1)
                beside.run(1)
                act.wait_ge(u_done, t + 1)
                nc.scalar.activation(us, B34[:, 1, :], ACT.Copy).then_inc(u_taken, 1)
                beside.run(1)
                act.wait_ge(od_done, t + 1)
                act.wait_ge(qkn_ready, t + 1)
                nc.scalar.activation(sq2[:, 0:4, :].rearrange("p h k -> p (h k)"), B56[:, 0, :], ACT.Square).then_inc(
                    o_squared, 1)
                beside.run(1)
                act.wait_ge(of_ready, t + 1)
                nc.scalar.activation(oh[:, 2:6, bass.ds(t * P, P)], of[:], ACT.Copy).then_inc(of_high, 1)
                beside.run(CHUNKS)

            nc.scalar.activation(babuf[0:SAMPLES, 6, TILES, :], babuf[0:SAMPLES, 1, TILES, :], ACT.Exp).then_inc(
                ds_act, 1)
            act.wait_ge(ds_in, 32)
            nc.scalar.activation(s64[:, 0, :], sin[:, 0:8, :].rearrange("p h b -> p (h b)"), ACT.Square,
                                 scale=0.5).then_inc(ds_act, 1)
            act.wait_ge(ds_o, 1)
            nc.scalar.activation(s64[:, 0, 0:32], B7[:, 0:32], ACT.Square).then_inc(ds_act, 1)
            act.wait_ge(of_ready, TILES + 1)
            nc.scalar.activation(oh[:, 2:6, SEQ:TOK], sof[:], ACT.Copy).then_inc(of_high, 1)

            def merge_high(f):
                for j in range(THIRDS):
                    act.wait_ge(merged, f * 3 + (j + 1))
                    nc.scalar.activation(xh[:, bass.ds(f, 1), third(j)].squeeze(1), cc[:, third(j)], ACT.Copy,
                                         scale=0.5).then_inc(m_high, 1)

            for f, par, _ in pairs(act, 0, KT):
                high(f + (U_BRANCH + 1), 1 - par)
                merge_high(f)
            for f, par, _ in pairs(act, 0, KT):
                high(f + (U_MIX + 1), 1 - par)

            def normed(t, par, m, first):
                act.wait_ge(ln_shift, t + (first + 1))
                nc.scalar.activation(xn[0:m].rearrange("p (a n) -> p a n", a=2), (B34, B56)[par][0:m], ACT.Identity,
                                     bias=mv[0:m, 3:4], scale=mv[0:m, 2:3]).then_inc(ln_norm, 1)

            for t, par, win, m in windows():
                after(act, ln_back, t)
                normed(t, par, m, 0)
                act.wait_ge(ln_h, t + 1)
                nc.scalar.activation(hh[:, :, win], acc[:, :, win], ACT.Copy).then_inc(h_high, 1)
            for n, f0, u0, before in pieces():
                for p, par, i in pairs(act, 0, n):
                    u, F = p * 2 + u0, p + f0
                    high(u + 1, 1)
                    after(act, f_step, F * FFN_STEPS)
                    for j in range(THIRDS):
                        act.wait_ge(slice_done, u * 3 + (j + 1))
                        nc.scalar.activation(ab[:, 2 + j * TW:2 + (j + 1) * TW], U[:, j, 0:TW], ACT.Copy).then_inc(
                            a_taken, 1)
                    high(u + 2, 0)
                    act.wait_ge(f_step, F * FFN_STEPS + FFN_STEPS)
                    after(act, f_prod, F * 3)
                    nc.scalar.activation(gl[:], cc[:], ACT.Gelu_apprx_tanh,
                                         bias=cst[:, bass.ds(F + C_FFB, 1)]).then_inc(f_gelu, 1)
                    for j in range(THIRDS):
                        act.wait_ge(f_prod, F * 3 + (j + 1))
                        nc.scalar.activation(xh[:, bass.ds(p, 1), third(j)].squeeze(1), cc[:, third(j)],
                                             ACT.Copy).then_inc(f_high, 1)
                last = u0 + 2 * n + KT == UNITS
                for f, par, i in pairs(act, 0, KT - 2 * last):
                    high(f + (u0 + 2 * n + 1), 1 - par)
                if last:
                    high(UNITS - 1, 1)
            for t, par, win, m in windows():
                after(act, y_ready, t)
                normed(t, par, m, TILES + 1)

        @block.vector
        def _(dve):
            nc.vector.memset(pre[:, 0, 0:3], 0.0).then_inc(zeroed, 1)
            nc.vector.memset(pre[:, 1, 0:3], 0.0).then_inc(conv_out, 1)
            nc.vector.memset(babuf[:], 0.0).then_inc(zeroed, 1)
            for k in range(KT):
                dve.wait_ge(x_hi, k + 1)
                nc.vector.tensor_tensor(xl[:, k, :], xraw[:, k, :], xh[:, k, :].bitcast(F32),
                                        ALU.subtract).then_inc(x_lo, 1)
            dve.wait_ge(ba_done, 1)
            dve.wait_ge(zeroed, 2)
            ba = B7[:, 0:72].rearrange("p (t c) -> p t c", c=8)
            nc.vector.tensor_copy(babuf[:, 0, 0:TILES, :], ba[:, 0:TILES, 0:4])
            nc.vector.tensor_copy(babuf[0:SAMPLES, 0, TILES, :], ba[0:SAMPLES, TILES, 0:4])
            nc.vector.tensor_copy(babuf[:, 1, 0:TILES, :], ba[:, 0:TILES, 4:8])
            nc.vector.tensor_copy(babuf[0:SAMPLES, 1, TILES, :], ba[0:SAMPLES, TILES, 4:8]).then_inc(ba_raw, 1)
            st = Steps(dve, small_step)
            dve.wait_ge(ba_raw, 1)
            dve.wait_ge(consts_in, 16 * N_CONSTS)
            st.link(nc.vector.tensor_tensor(babuf[:, 1], babuf[:, 1], bac[:, 1, :].unsqueeze(1).to_broadcast(
                [P, 9, DN_H]), ALU.add))
            nc.vector.scalar_tensor_tensor(babuf[:, 3], babuf[:, 1], -1.0, babuf[:, 1], ALU.mult, ALU.max).then_inc(
                ba_dve, 1)
            dve.wait_ge(ba_act, 3)
            nc.vector.tensor_scalar(babuf[:, 4], babuf[:, 4], 1.0, None, ALU.add).then_inc(ba_dve, 1)
            st.link(nc.vector.tensor_scalar(babuf[:, 0], babuf[:, 2], 0.5, 0.5, ALU.mult, ALU.add))
            dve.wait_ge(ba_dve, 1)
            st.link(nc.vector.tensor_scalar(babuf[:, 1], babuf[:, 1], 0.0, None, ALU.max))
            dve.wait_ge(ba_act, 4)
            st.link(nc.vector.tensor_tensor(babuf[:, 1], babuf[:, 1], babuf[:, 5], ALU.add))
            st.link(nc.vector.scalar_tensor_tensor(babuf[:, 1], babuf[:, 1], -1.0, bac[:, 0, :].unsqueeze(1)
                                                   .to_broadcast([P, 9, DN_H]), ALU.mult, ALU.mult))
            cv = Steps(dve, conv_step)
            for b, par, g, n, prev, kind in blocks_of(dve):
                parts = 2 if prev else 1
                u = b + U_BLK
                dve.wait_ge(taken, 3 * 6 if g == 0 else ALL_QKV)
                after(dve, s_done, b)
                t = GT[g]
                for dst, tile, scale in ((q_st[:], 0, HD ** -0.5), (k_st[:, par], 2, 1.0)):
                    ins = nc.vector.tensor_scalar(packed(dst, g), cols(qkv[:, t + tile:t + tile + 2, 0:SEQ], g, n),
                                                  scale, None, ALU.mult)
                ins.then_inc(qk_staged, 1)
                after(dve, v_done, b)
                nc.vector.tensor_scalar(packed(v_st[:], g), cols(qkv[:, t + 4:t + 6, 0:SEQ], g, n),
                                        1.0, None, ALU.mult).then_inc(v_staged, 1)
                dve.wait_ge(s_done, b + 1)
                after(dve, exped, b)
                dve.wait_ge(bias_in, 16 * (g + 1))
                s_all = B34[:].rearrange("p a (j t k) -> p (a j) t k", j=2, t=2)
                nc.vector.tensor_tensor(sb[:, :, 0:parts, :], s_all[:, :, 0:parts, :], bias[:, :, 0:parts, :],
                                        ALU.add).then_inc(biased, 1)
                dve.wait_ge(biased, b + 1)
                after(dve, o_taken, b)
                nc.vector.tensor_reduce(nmax[:], sb[:, :, 0:parts, :], AX.XY, ALU.max, negate=True).then_inc(maxed, 1)
                if kind == "dn":
                    f = b - BLOCKS
                    cv.item(f, CONV_STEPS)
                    dnw = [cst[:, bass.ds(f * 4 + (C_DNW + i), 1)] for i in range(4)]
                    after(dve, conv_stored, f * 16)
                    for j in range(THIRDS):
                        dve.wait_ge(taken, u * 3 + (j + 1))
                        a, w = j * TW, (TW if j < 2 else SEQ - 2 * TW)
                        cv.link(nc.vector.tensor_scalar(cb[:, a:a + w], pre[:, par, a + 3:a + 3 + w], dnw[3], None,
                                                        ALU.mult))
                        for i in (2, 1, 0):
                            cv.link(nc.vector.scalar_tensor_tensor(cb[:, a:a + w], pre[:, par, a + i:a + i + w],
                                                                   dnw[i], cb[:, a:a + w], ALU.mult, ALU.add))
                    cv.link(nc.vector.tensor_scalar(cb[:, SEQ:TOK], pre[:, par, SEQ + 3:TOK + 3], dnw[3], None,
                                                    ALU.mult))
                    for i in (2, 1, 0):
                        cv.link(nc.vector.scalar_tensor_tensor(
                            cb[:, SEQ:TOK], sconv[:, bass.ds(f, 1), :, i].squeeze(1), dnw[i], cb[:, SEQ:TOK],
                            ALU.mult, ALU.add))
                    nc.vector.tensor_scalar(tails[:, bass.ds(f, 1), :].squeeze(1), pre[:, par, SEQ:SEQ + 11], 1.0, None,
                                            ALU.mult)
                dve.wait_ge(pv_done, b + 1)
                dve.wait_ge(maxed, b + 1)
                after(dve, o_stored[par], stored_before(b, par, g, n))
                nc.vector.tensor_scalar(obuf[:, par, :, 65].rearrange("p (j a) -> p a j", a=2),
                                        nmax[:].rearrange("p (a j) -> p a j", a=2), -1.0, None, ALU.mult)
                nc.vector.tensor_scalar(obuf[:, par, :, 0:64], B7[:, 256:512].rearrange("p (h e) -> p h e", e=64),
                                        1.0, None, ALU.mult).then_inc(o_taken, 1)
                if kind != "att":
                    dve.wait_ge(conv_tanh, b - (BLOCKS - 1))
                    if kind == "z":
                        dve.wait_ge(conv_stored, (b - BLOCKS) * 16)
                    src = cb[:] if kind == "dn" else pre[:, par, 3:3 + TOK]
                    nc.vector.scalar_tensor_tensor(cb[:], thb[:], 1.0, src, ALU.add, ALU.mult).then_inc(conv_out, 1)


            def mark(ins):
                ins.then_inc(samp_dve, 1)

            def wide(ap, n):
                return ap.unsqueeze(3).to_broadcast([*ap.shape, n])

            st.n = SMALL_0
            dve.wait_ge(samp_act, 3)
            st.link(nc.vector.tensor_tensor(self_p[:], sq[:, :, 0, :], sq[:, :, 1, :], ALU.mult))
            st.link(nc.vector.tensor_reduce(self_s[:], self_p[:].rearrange("b g (h e) -> b g h e", e=HD), AX.X, ALU.add))
            dve.wait_ge(samp_in, 16 * 5)
            k0 = 0
            for n, g in enumerate((0, 2, 1)):
                m = SKEYS[g]
                pr = prod[:, 0:m].rearrange("p j h e -> p j (h e)")
                st.link(nc.vector.tensor_tensor(pr, kvc[:, k0:k0 + m, 0, :], qb[:, n, :].unsqueeze(1).to_broadcast(
                    [P, m, 256]), ALU.mult))
                st.link(nc.vector.tensor_reduce(ssc[:, k0:k0 + m, :], prod[:, 0:m], AX.X, ALU.add))
                k0 += m
            st.link(nc.vector.tensor_tensor(ssc[:], ssc[:], sbias[:], ALU.add))
            nc.vector.tensor_reduce(sm[0:SAMPLES, 1, :], self_s[:].rearrange("b g h -> b h g"), AX.X, ALU.max)
            mark(nc.vector.tensor_reduce(sm[:, 0, :], ssc[:].rearrange("p k h -> p h k"), AX.X, ALU.max))
            dve.wait_ge(samp_pe, 3)
            m48 = sm[0:4, 2:4, :].rearrange("p a c -> p (a c)")
            n48 = sm[0:4, 4:6, :].rearrange("p a c -> p (a c)")
            st.link(nc.vector.tensor_reduce(m48, B7[0:4, 0:P].rearrange("p (b c) -> p b c", c=16), AX.X, ALU.max))
            mark(nc.vector.tensor_tensor(n48, B7[0:4, P:P + SAMPLES], m48, ALU.max))
            dve.wait_ge(samp_pe, 4)
            mark(nc.vector.tensor_copy(sm[0:SAMPLES, 6, :], B34[0:SAMPLES, 0, 0:4]))
            dve.wait_ge(samp_pe, 5)
            dve.wait_ge(samp_dve, 3)
            st.link(nc.vector.tensor_copy(sm[:, 8, :], B56[:, 0, 0:4]))
            st.link(nc.vector.tensor_tensor(ssc[:], ssc[:], sm[:, 8, :].unsqueeze(1).to_broadcast([P, SK, 4]),
                                            ALU.subtract))
            st.link(nc.vector.tensor_tensor(self_s[:], self_s[:], sm[0:SAMPLES, 6, :].unsqueeze(1).to_broadcast(
                [SAMPLES, 3, 4]), ALU.subtract))
            assert st.n == SMALL_S
            dve.wait_ge(samp_act, 4)
            st.link(nc.vector.tensor_reduce(sm[:, 7, :], ssc[:].rearrange("p k h -> p h k"), AX.X, ALU.add))
            k0 = 0
            for n, g in enumerate((0, 2, 1)):
                m = SKEYS[g]
                st.link(nc.vector.tensor_tensor(prod[:, 0:m], kvc[:, k0:k0 + m, 1, :].rearrange(
                    "p j (h e) -> p j h e", e=HD), wide(ssc[:, k0:k0 + m, :], HD), ALU.mult))
                st.link(nc.vector.tensor_reduce(og[:, n, :], prod[:, 0:m].rearrange("p j h e -> p (h e) j"), AX.X,
                                                ALU.add))
                k0 += m
            mark(nc.vector.tensor_tensor(self_p[:].rearrange("b g (h e) -> b g h e", e=HD),
                                         sq[:, :, 2, :].rearrange("b g (h e) -> b g h e", e=HD),
                                         wide(self_s[:], HD), ALU.mult))
            dve.wait_ge(samp_pe, 6)
            st.link(nc.vector.reciprocal(sm[0:SAMPLES, 9, :], B7[0:SAMPLES, 256:260]))
            mark(nc.vector.tensor_tensor(o8[:].rearrange("b (h e) -> b h e", e=HD),
                                         B7[0:SAMPLES, 0:256].rearrange("b (h e) -> b h e", e=HD),
                                         sm[0:SAMPLES, 9, :].unsqueeze(2).to_broadcast([SAMPLES, 4, HD]), ALU.mult))
            dve.wait_ge(ao_high, 1)
            nc.vector.tensor_tensor(ol[:, 0:2, SEQ:TOK], B34[:, 1, 0:2 * SAMPLES].rearrange("p (n b) -> p n b", n=2),
                                    oh[:, 0:2, SEQ:TOK].bitcast(F32), ALU.subtract).then_inc(ao_low, 1)

            dve.wait_ge(ao_low, 1)
            dve.wait_ge(cf_act, 1)
            st.link(nc.vector.tensor_copy(cf[:, 0, :], B7[:, 0:32]))
            nc.vector.tensor_tensor(cf[:, 3, :], B7[:, 32:64], cf[:, 0, :], ALU.subtract).then_inc(cf_dve, 1)
            nc.vector.memset(S[:], 0.0).then_inc(s_ready, 1)
            dve.wait_ge(cf_act, 3)
            dve.wait_ge(dcst_in, 16)
            dn = Steps(dve, dn_step)
            heads4 = lambda ap: ap.rearrange("p (h k) -> p h k", h=DN_H)
            per_head = lambda ap: ap.unsqueeze(2).to_broadcast([P, DN_H, P])
            same = lambda ap: ap.unsqueeze(1).to_broadcast([P, DN_H, P])
            with dve.Fori(0, TILES) as t:
                dn.item(t, DN_STEPS)
                q4, k4, v4, G4 = (heads4(x) for x in (B34[:, 0, :], B34[:, 1, :], B56[:, 0, :], B56[:, 1, :]))
                th = bass.ds(t * DN_H, DN_H)
                gc, eg, egt, ekd = (cf[:, n, th] for n in range(4))
                beta = babuf[:, 0, bass.ds(t, 1), :].squeeze(1)
                after(dve, of_low, t)
                nc.vector.tensor_scalar(gB[:], per_head(babuf[:, 1, bass.ds(t, 1), :].squeeze(1)), 1.0, None,
                                        ALU.mult).then_inc(g_staged, 1)
                dve.wait_ge(att_in, t * 16 + 16)
                dve.wait_ge(ao_low, t + 1)
                dn.link(nc.vector.tensor_tensor(amx[:, 0, :], abuf[:, 0, :, 65], abuf[:, 1, :, 65], ALU.max))
                dn.link(nc.vector.tensor_tensor(amx[:, 0, :], amx[:, 0, :], abuf[:, 2, :, 65], ALU.max))
                nc.vector.tensor_tensor(amx[:, 1:4, :], abuf[:, :, :, 65], amx[:, 0, :].unsqueeze(1).to_broadcast(
                    [P, 3, 4]), ALU.subtract).then_inc(ae_ready, 1)
                dve.wait_ge(squared, t + 1)
                dn.link(nc.vector.tensor_reduce(rn[:, 0, :], sq2[:], AX.X, ALU.add))
                nc.vector.tensor_scalar(rn[:, 1, :], rn[:, 0, :], RMS_EPS, None, ALU.add).then_inc(ss_ready, 1)
                dve.wait_ge(rs_ready, t * 2 + 1)
                dn.link(nc.vector.tensor_scalar(rn[:, 2, 0:4], rn[:, 1, 0:4], 0.5 * DN_D ** -0.5, None, ALU.mult))
                dn.link(nc.vector.tensor_scalar(rn[:, 2, 4:8], rn[:, 1, 4:8], 0.5, None, ALU.mult))
                dn.link(nc.vector.tensor_tensor(qn[:], q4, per_head(rn[:, 2, 0:4]), ALU.mult))
                nc.vector.tensor_tensor(kn[:], k4, per_head(rn[:, 2, 4:8]), ALU.mult).then_inc(qkn_ready, 1)
                nc.vector.scalar_tensor_tensor(vb[:], v4, 0.5, per_head(beta), ALU.mult, ALU.mult).then_inc(v_ready, 1)
                dve.wait_ge(ae_exp, t + 1)
                w3 = amx[:, 1:4, :].unsqueeze(3).to_broadcast([P, 3, 4, 65])
                dn.link(nc.vector.tensor_tensor(abuf[:, :, :, 0:65], abuf[:, :, :, 0:65], w3, ALU.mult))
                dn.link(nc.vector.tensor_tensor(abuf[:, 0, :, 0:65], abuf[:, 0, :, 0:65], abuf[:, 1, :, 0:65], ALU.add))
                dn.link(nc.vector.tensor_tensor(abuf[:, 0, :, 0:65], abuf[:, 0, :, 0:65], abuf[:, 2, :, 0:65], ALU.add))
                dn.link(nc.vector.reciprocal(amx[:, 4, :], abuf[:, 0, :, 64]))
                nc.vector.tensor_tensor(ao[:], abuf[:, 0, :, 0:64], amx[:, 4, :].unsqueeze(2).to_broadcast([P, 4, 64]),
                                        ALU.mult).then_inc(ao_ready, 1)
                dve.wait_ge(qkn_ready, t + 1)
                dn.link(nc.vector.tensor_tensor(kb[:], kn[:], per_head(beta), ALU.mult))
                nc.vector.tensor_tensor(qd[:], qn[:], per_head(eg), ALU.mult).then_inc(kbqd_ready, 1)
                dve.wait_ge(g_done, t + 1)
                dn.link(nc.vector.tensor_tensor(ET[:], G4, same(dcst[:, D_NEG:D_NEG + P]), ALU.add))
                nc.vector.tensor_tensor(ET[:], ET[:], per_head(gc), ALU.subtract).then_inc(decay_sum, 1)
                dve.wait_ge(ao_high, t + 2)
                nc.vector.tensor_tensor(ol[:, 0:2, bass.ds(t * P, P)], B7[:, 0:256].rearrange("p (n k) -> p n k", n=2),
                                        oh[:, 0:2, bass.ds(t * P, P)].bitcast(F32), ALU.subtract).then_inc(ao_low, 1)
                dn.link(nc.vector.tensor_tensor(kbe[:], kb[:], per_head(eg), ALU.mult))
                dn.link(nc.vector.tensor_tensor(kd[:], kn[:], per_head(ekd), ALU.mult))
                dve.wait_ge(decay_exp, t + 1)
                dn.link(nc.vector.tensor_tensor(ETs[:], ET[:], same(dcst[:, D_STR:D_STR + P]), ALU.mult))
                dve.wait_ge(la_done, t + 1)
                lev = lambda n: same(dcst[:, D_LEV + n * P:D_LEV + (n + 1) * P])
                dn.link(nc.vector.tensor_tensor(heads4(LTm[:]), q4, ETs[:], ALU.mult))
                dn.link(nc.vector.tensor_tensor(heads4(XT[:]), heads4(LTm[:]), lev(0), ALU.mult))
                dn.link(nc.vector.tensor_tensor(heads4(Lb[:, 1]), heads4(LTm[:]), lev(1), ALU.mult))
                nc.vector.tensor_tensor(heads4(XT[:]), heads4(XT[:]), same(ident), ALU.add).then_inc(xt_ready, 1)
                dn.link(nc.vector.tensor_tensor(heads4(ATm[:]), k4, ET[:], ALU.mult))
                for lv in range(LEVELS):
                    if lv + 2 < LEVELS + 1:
                        after(dve, y_done, t * LEVELS + lv)
                        dn.link(nc.vector.tensor_tensor(heads4(Lb[:, lv % 2]), heads4(LTm[:]), lev(lv + 2), ALU.mult))
                    dve.wait_ge(zt_done, t * LEVELS + (lv + 1))
                    dve.wait_ge(xt_ready, t * (LEVELS + 1) + (lv + 1))
                    nc.vector.tensor_tensor(XT[:], XT[:], B7[:, :], ALU.add).then_inc(xt_ready, 1)
                dve.wait_ge(od_done, t + 1)
                dve.wait_ge(s_ready, t + 1)
                dn.link(nc.vector.tensor_tensor(heads4(S[:]), heads4(S[:]), per_head(egt), ALU.mult))
                nc.vector.tensor_tensor(S[:], S[:], B56[:, 1, :], ALU.add).then_inc(s_ready, 1)
                dve.wait_ge(o_squared, t + 1)
                dn.link(nc.vector.tensor_reduce(rn[:, 0, 0:4], sq2[:, 0:4, :], AX.X, ALU.add))
                nc.vector.tensor_scalar(rn[:, 1, 0:4], rn[:, 0, 0:4], 1.0 / DN_D, RMS_EPS, ALU.mult, ALU.add).then_inc(
                    ss_ready, 1)
                dve.wait_ge(rs_ready, t * 2 + 2)
                nc.vector.tensor_tensor(of[:], v4, per_head(rn[:, 1, 0:4]), ALU.mult).then_inc(on_ready, 1)
                dve.wait_ge(on_done, t + 1)
                dve.wait_ge(z_in, t * 16 + 16)
                nc.vector.scalar_tensor_tensor(of[:], heads4(B7[:, :]), onh[:], zin[:], ALU.mult, ALU.mult).then_inc(
                    of_ready, 1)
                dve.wait_ge(of_high, t + 1)
                nc.vector.tensor_tensor(ol[:, 2:6, bass.ds(t * P, P)], of[:], oh[:, 2:6, bass.ds(t * P, P)].bitcast(F32),
                                        ALU.subtract).then_inc(of_low, 1)
                assert dn.n == DN_STEPS, dn.n

            dve.wait_ge(of_low, TILES)
            dve.wait_ge(ds_in, 32)
            dve.wait_ge(ds_act, 2)
            by_b = lambda ap: ap.unsqueeze(1).to_broadcast([SAMPLES, SAMPLES, DN_H])
            eye8 = ident[0:SAMPLES, 0:SAMPLES].unsqueeze(2).to_broadcast([SAMPLES, SAMPLES, DN_H])
            nc.vector.tensor_tensor(sdiag[:, 0], eye8, by_b(babuf[0:SAMPLES, 0, TILES, :]), ALU.mult)
            nc.vector.tensor_tensor(sdiag[:, 1], eye8, by_b(babuf[0:SAMPLES, 6, TILES, :]), ALU.mult).then_inc(ds_dve, 1)
            dve.wait_ge(ds_pe, 2)
            nc.vector.tensor_scalar(s64[:, 1, :], B34[:, 1, 0:64], RMS_EPS, None, ALU.add).then_inc(ss_ready, 1)
            st.link(nc.vector.tensor_scalar(s64[:, 3, :].rearrange("p (x h b) -> p x b h", x=2, h=DN_H),
                                            B34[:, 0, 0:64].rearrange("p (x b h) -> p x b h", x=2, h=DN_H), 1.0, None,
                                            ALU.mult))
            dve.wait_ge(rs_ready, 2 * TILES + 1)
            qk = sin[:, 0:8, :].rearrange("p h b -> p (h b)")
            st.link(nc.vector.scalar_tensor_tensor(s64[:, 2, :], qk, 0.5, s64[:, 1, :], ALU.mult, ALU.mult))
            nc.vector.tensor_scalar(s64[:, 4, 0:32], s64[:, 2, 32:64], -1.0, None, ALU.mult)
            nc.vector.tensor_tensor(s64[:, 4, 32:64], s64[:, 2, 32:64], s64[:, 3, 0:32], ALU.mult)
            nc.vector.tensor_scalar(s64[:, 5, 0:32], sin[:, 8:12, :].rearrange("p h b -> p (h b)"), 0.5, None, ALU.mult)
            nc.vector.tensor_scalar(s64[:, 2, 0:32], s64[:, 2, 0:32], DN_D ** -0.5, None, ALU.mult).then_inc(ds_dve, 1)
            dve.wait_ge(ds_dve, 2)
            across = lambda ap: ap.unsqueeze(2).to_broadcast([P, 4, P])
            for n in range(8):
                h, b0 = n // 2, n % 2 * 4
                col = slice(h * SAMPLES + b0, h * SAMPLES + b0 + 4)
                more = lambda base: slice(base + col.start, base + col.stop)
                state = sS[:, h, b0:b0 + 4, :]
                st.link(nc.vector.tensor_tensor(state, state, across(s64[:, 3, more(32)]), ALU.mult))
                nc.vector.tensor_tensor(sdv[:], same(ident), across(s64[:, 5, col]), ALU.mult).then_inc(ds_scaled, 1)
                dve.wait_ge(ds_prod, n + 1)
                st.link(nc.vector.tensor_tensor(sdv[:], heads4(B56[:, n % 2, :]), across(s64[:, 4, more(32)]), ALU.mult))
                nc.vector.tensor_tensor(state, state, sdv[:], ALU.add).then_inc(ds_new, 1)
                dve.wait_ge(ds_new, n + 1)
            dve.wait_ge(ds_pe, 3)
            nc.vector.tensor_scalar(s64[:, 1, 0:32], B34[:, 1, 0:32], 1.0 / DN_D, RMS_EPS, ALU.mult, ALU.add).then_inc(
                ss_ready, 1)
            dve.wait_ge(rs_ready, 2 * TILES + 2)
            hb = lambda ap: ap.rearrange("p (h b) -> p h b", h=DN_H)
            st.link(nc.vector.tensor_tensor(sof[:], hb(B7[:, 0:32]), hb(s64[:, 1, 0:32]), ALU.mult))
            nc.vector.scalar_tensor_tensor(sof[:], sof[:], onh[:], sin[:, 12:16, :], ALU.mult, ALU.mult).then_inc(
                of_ready, 1)
            dve.wait_ge(of_high, TILES + 1)
            nc.vector.tensor_tensor(ol[:, 2:6, SEQ:TOK], sof[:], oh[:, 2:6, SEQ:TOK].bitcast(F32),
                                    ALU.subtract).then_inc(of_low, 1)

            dbank = (B34[:, 0, :], B34[:, 1, :], B56[:, 0, :])
            dve.wait_ge(fstate_in, 16)
            dve.wait_ge(of_low, TILES + 1)
            for f, par, i in pairs(dve, 0, KT):
                dve.wait_ge(gates_in[par], (f - par) * 8 + 16)
                after(dve, m_low, f * 3)
                for j in range(THIRDS):
                    dve.wait_ge(slice_done, (f + U_BRANCH) * 3 + (j + 1))
                    nc.vector.scalar_tensor_tensor(cc[:, third(j)], gates[:, par, 0, third(j)], 1.0,
                                                   U[:, j, 0:TW], ALU.add, ALU.mult)
                    dve.wait_ge(merged, f * 3 + j)
                    nc.vector.scalar_tensor_tensor(mt, gates[:, par, 1, third(j)], 1.0,
                                                   dbank[j][:, 0:TW], ALU.add, ALU.mult).then_inc(used, 1)
                    dve.wait_ge(used, f * 3 + (j + 1))
                    nc.vector.tensor_tensor(cc[:, third(j)], cc[:, third(j)], mt, ALU.add).then_inc(merged, 1)
                for j in range(THIRDS):
                    dve.wait_ge(m_high, f * 3 + (j + 1))
                    x = (slice(None), bass.ds(f, 1), third(j))
                    nc.vector.scalar_tensor_tensor(xl[x].squeeze(1), cc[:, third(j)], 0.5, xh[x].squeeze(1).bitcast(F32),
                                                   ALU.mult, ALU.subtract).then_inc(m_low, 1)
            dve.wait_ge(acc_in, 16)
            for f, par, i in pairs(dve, 0, KT):
                for j in range(THIRDS):
                    dve.wait_ge(slice_done, (f + U_MIX) * 3 + (j + 1))
                    a = acc[:, bass.ds(f, 1), third(j)].squeeze(1)
                    nc.vector.scalar_tensor_tensor(a, a, ALPHA, U[:, j, 0:TW], ALU.mult, ALU.add).then_inc(used, 1)
            nc.vector.memset(ab[:, 0:2], 0.0).then_inc(f_zero, 1)

            def moments(t, par, m, first):
                dve.wait_ge(ln_in, t + (first + 1))
                for a in range(2):
                    ins = nc.vector.bn_stats(stats[0:m, a, :], (B34, B56)[par][0:m, a, :])
                ins.then_inc(ln_step2, 1)
                dve.wait_ge(ln_step2, t * 2 + (2 * first + 1))
                after(dve, ln_norm, t + first)
                nc.vector.bn_aggr(mv[0:m, 0:2], stats[0:m].rearrange("p a s -> p (a s)")).then_inc(ln_step2, 1)
                dve.wait_ge(ln_step2, t * 2 + (2 * first + 2))
                nc.vector.tensor_scalar(mv[0:m, 1:2], mv[0:m, 1:2], LN_EPS, None, ALU.add).then_inc(ln_var, 1)
                dve.wait_ge(ln_root, t + (first + 1))
                nc.vector.scalar_tensor_tensor(mv[0:m, 3:4], mv[0:m, 0:1], -1.0, mv[0:m, 2:3], ALU.mult, ALU.mult).then_inc(
                    ln_shift, 1)

            for t, par, win, m in windows():
                moments(t, par, m, 0)
                dve.wait_ge(ln_back, t + 1)
                gain = lambda c: cst[:, c:c + KT].unsqueeze(2).to_broadcast([P, KT, m])
                src = U[:, 0:2, :].rearrange("p a (k t) -> p (a k) t", k=4)[:, :, 0:m]
                nc.vector.tensor_tensor(acc[:, :, win], src, gain(C_G1), ALU.mult).then_inc(ln_mul, 1)
                dve.wait_ge(ln_mul, t + 1)
                nc.vector.tensor_tensor(acc[:, :, win], acc[:, :, win], gain(C_B1), ALU.add).then_inc(ln_h, 1)
                dve.wait_ge(h_high, t + 1)
                nc.vector.tensor_tensor(hl[:, :, win], acc[:, :, win], hh[:, :, win].bitcast(F32), ALU.subtract).then_inc(
                    h_low, 1)
            fs = Steps(dve, f_step)
            dve.wait_ge(f_zero, 1)
            for n, f0, u0, before in pieces():
                for p, par, i in pairs(dve, 0, n):
                    u, F = p * 2 + u0, p + f0
                    fs.item(F, FFN_STEPS)
                    w3 = [cst[:, bass.ds(F * 3 + (C_FFW + k), 1)] for k in range(3)]
                    after(dve, f_low, F)
                    for j in range(THIRDS):
                        dve.wait_ge(a_taken, F * 3 + (j + 1))
                        a, w = j * TW, (TW if j < 2 else SEQ - 2 * TW)
                        fs.link(nc.vector.tensor_scalar(cc[:, a:a + w], ab[:, a + 2:a + 2 + w], w3[2], None, ALU.mult))
                        for k in (1, 0):
                            fs.link(nc.vector.scalar_tensor_tensor(cc[:, a:a + w], ab[:, a + k:a + k + w], w3[k],
                                                                   cc[:, a:a + w], ALU.mult, ALU.add))
                    fs.link(nc.vector.tensor_scalar(cc[:, SEQ:TOK], ab[:, SEQ + 2:TOK + 2], w3[2], None, ALU.mult))
                    fs.link(nc.vector.scalar_tensor_tensor(cc[:, SEQ:TOK], fstate[:, bass.ds(F, 1), :, 1].squeeze(1),
                                                           w3[1], cc[:, SEQ:TOK], ALU.mult, ALU.add))
                    nc.vector.tensor_scalar(ftails[:, bass.ds(F, 1), :].squeeze(1), ab[:, SEQ:SEQ + 10], 1.0, None,
                                            ALU.mult)
                    fs.link(nc.vector.scalar_tensor_tensor(cc[:, SEQ:TOK], fstate[:, bass.ds(F, 1), :, 0].squeeze(1),
                                                           w3[0], cc[:, SEQ:TOK], ALU.mult, ALU.add))
                    dve.wait_ge(f_gelu, F + 1)
                    for j in range(THIRDS):
                        dve.wait_ge(slice_done, u * 3 + (3 + j + 1))
                        nc.vector.tensor_tensor(cc[:, third(j)], gl[:, third(j)], U[:, j, 0:TW],
                                                ALU.mult).then_inc(f_prod, 1)
                    dve.wait_ge(f_high, F * 3 + 3)
                    x = (slice(None), bass.ds(p, 1), slice(None))
                    nc.vector.tensor_tensor(xl[x].squeeze(1), cc[:], xh[x].squeeze(1).bitcast(F32),
                                            ALU.subtract).then_inc(f_low, 1)
                for f, par, i in pairs(dve, 0, KT):
                    for j in range(THIRDS):
                        dve.wait_ge(slice_done, (f + (u0 + 2 * n)) * 3 + (j + 1))
                        a = acc[:, bass.ds(f, 1), third(j)].squeeze(1)
                        nc.vector.scalar_tensor_tensor(a, a, ALPHA if f0 == 0 else 1.0, U[:, j, 0:TW], ALU.mult,
                                                       ALU.add).then_inc(used, 1)
                dve.wait_ge(used, before + 3 * KT)
            dve.wait_ge(rows2_in, 32)
            for t, par, win, m in windows():
                moments(t, par, m, TILES + 1)
                dve.wait_ge(ln_norm, t + (TILES + 2))
                after(dve, y_stored[par], (t - par) * 8)
                nc.vector.tensor_tensor(yt[0:m, par, :], xn[0:m], g2r[0:m], ALU.mult).then_inc(ln_mul, 1)
                dve.wait_ge(ln_mul, t + (TILES + 2))
                nc.vector.tensor_tensor(yt[0:m, par, :], yt[0:m, par, :], b2r[0:m], ALU.add).then_inc(y_ready, 1)


def layout(x):
    f = np.float32
    g = lambda n: np.asarray(x[n])
    out = {}
    xs = np.concatenate([g("x_prompt")[0], g("x_sample")[:, 0]], 0)
    out["xT"] = np.ascontiguousarray(xs.T.reshape(KT, P, TOK).transpose(1, 0, 2))
    win, wup, wo, wdn = g("w_in")[0], g("w_up")[0], g("w_o")[0], g("w_down")[0]
    wad = np.concatenate([g("w_att_out")[0], g("w_dn_out")[0]], 0)
    wu = np.zeros((UNITS, P, KT, P), f)
    n = 0

    def put(w, k0, ks, c0):
        nonlocal n
        wu[n, :, 0:ks] = w[k0 * P:(k0 + ks) * P, c0:c0 + P].reshape(ks, P, P).transpose(1, 0, 2)
        n += 1

    for grp, kinds in ((0, (0, 1, 2)), (2, (0, 1, 2)), (1, (0, 1, 2))):
        for kind in kinds:
            for j in range(2):
                put(win, 0, KT, kind * ATT_W + grp * 256 + j * P)
    for i in range(12):
        put(win, 0, KT, OFF_DN + i * P)
    for i in range(DN_H):
        put(win, 0, KT, OFF_Z + i * P)
    for i in range(KT):
        put(win, 0, KT, OFF_GATE + i * P)
        put(win, 0, KT, OFF_GATE + D_MODEL + i * P)
    for i in range(KT):
        put(wad, 0, 6, i * P)
    for i in range(KT):
        put(wo, 0, KT, i * P)
    f0 = 0
    for m in PIECES:
        for i in range(m):
            put(wup, 0, KT, (f0 + i) * P)
            put(wup, 0, KT, D_FF + (f0 + i) * P)
        for i in range(KT):
            put(wdn, f0, m, i * P)
        f0 += m
    assert n == UNITS and f0 == FT
    out["wu"] = wu.reshape(UNITS, P, KT * P)
    out["wba"] = np.ascontiguousarray(win[:, OFF_BA:OFF_GATE].reshape(KT, P, 8).transpose(1, 0, 2))
    out["bac"] = np.stack([g("dn_a_log")[0], g("dn_dt_bias")[0]])[None]
    cst = np.zeros((P, C_END), f)
    cst[:, C_ID:C_DNW] = np.eye(P, dtype=f)
    cst[:, C_DNW:C_FFW] = g("w_dn_conv")[0].reshape(4, 12, P).transpose(2, 1, 0).reshape(P, 48)
    cst[:, C_FFW:C_FFB] = g("w_ffn_conv")[0].reshape(3, FT, P).transpose(2, 1, 0).reshape(P, 3 * FT)
    cst[:, C_FFB:C_G1] = g("b_ffn_conv")[0].reshape(FT, P).T
    cst[:, C_G1:C_B1] = g("ln1_g")[0].reshape(KT, P).T
    cst[:, C_B1:C_ON] = g("ln1_b")[0].reshape(KT, P).T
    cst[:, C_ON:C_R] = g("dn_onorm_w")[0][:, None]
    cst[0:SAMPLES, C_R:C_END] = (np.arange(P)[None] // 16 == np.arange(SAMPLES)[:, None]).astype(f)
    out["cst"] = cst
    out["sconv"] = np.ascontiguousarray(g("state_dn_conv")[0].reshape(SAMPLES, 3, 12, P).transpose(3, 2, 0, 1))
    slopes = np.exp2(np.float32(-8.0) * np.arange(1, 13, dtype=f) / np.float32(12)).astype(f).reshape(3, 4)
    q, k = np.arange(P)[:, None], np.arange(P)[None]
    bias = np.full((3, P, 4, 2, P), NEG, f)
    for grp, (win_, d) in enumerate(DIL):
        for slot in range(4):
            h = (slot % 2) * 2 + slot // 2
            if grp < 2:
                own, ok = q - k, q >= k
                pv, okp = P + q - k, k >= q
                bias[grp, :, slot, 1] = np.where(okp, -slopes[grp, h] * (d * pv).astype(f), f(NEG))
            else:
                own, ok = q - k, (q >= k) & (q // 64 == k // 64)
            bias[grp, :, slot, 0] = np.where(ok, -slopes[grp, h] * (d * own).astype(f), f(NEG))
    out["bias"] = bias
    for grp, name in enumerate(("cache_kv_w128", "cache_kv_w512", "cache_kv_w2048")):
        out[f"cache{grp}"] = g(name)[0].reshape(SAMPLES, PAST[grp], 2 * HPG * HD)
    sbias, k0 = np.zeros((P, SK, 4), f), 0
    for grp in (0, 2, 1):
        m, d = SKEYS[grp], DIL[grp][1]
        back = 16 * m - (np.arange(P)[:, None] % 16 * m + np.arange(m)[None])
        sbias[:, k0:k0 + m] = -slopes[grp][None, None] * (d * back).astype(f)[:, :, None]
        k0 += m
    out["sbias"] = sbias
    out["rt"] = np.ascontiguousarray(cst[0:SAMPLES, C_R:C_END].T)
    dc = np.zeros((P, D_END), f)
    dc[:, D_TRI:D_NEG] = q <= k
    dc[:, D_NEG:D_STR] = np.where(q <= k, f(0), f(NEG))
    dc[:, D_STR:D_ONE] = np.where(q < k, f(-1), f(0))
    dc[:, D_ONE:D_LEV] = 1
    for i in range(7):
        n = 1 << i
        dc[:, D_LEV + i * P:D_LEV + (i + 1) * P] = (q // (2 * n) == k // (2 * n)) & (k // n % 2 == 1) & (q // n % 2 == 0)
    out["dcst"] = dc
    out["dnrows"], out["ffnrows"] = g("state_dn_conv")[0], g("state_ffn_conv")[0]
    out["fstate"] = np.ascontiguousarray(g("state_ffn_conv")[0].reshape(SAMPLES, 2, FT, P).transpose(3, 2, 0, 1))
    out["g2"], out["b2"] = g("ln2_g"), g("ln2_b")
    out["sS"] = np.ascontiguousarray(g("state_dn_S")[0].transpose(2, 1, 0, 3))
    return out


OUTS = {"kv0": (P, 4, 136), "kv1": (P, 4, 520), "kv2": (P, 4, TOK), "dnconv": (P, 12, 11), "shift0": (SAMPLES, 127, 512),
        "shift1": (SAMPLES, 511, 512), "shift2": (SAMPLES, 1023, 512), "pS": (P, DN_H * P), "sS": (P, DN_H, SAMPLES, P),
        "dnrows": (SAMPLES, 2, 12 * P), "ffnrows": (SAMPLES, 1, D_FF), "ffnconv": (P, FT, 10), "y": (TOK, D_MODEL)}


def gather(r):
    y = r["y"]
    heads = (2, HPG, HD)
    kv_p, kv_s = [], []
    for grp in range(GROUPS):
        rows = r[f"kv{grp}"].transpose(2, 1, 0).reshape(-1, *heads)
        kv_p.append(rows[None, None, :-SAMPLES])
        old = r[f"shift{grp}"].reshape(SAMPLES, -1, *heads)
        kv_s.append(np.concatenate([old, rows[-SAMPLES:, None]], 1)[None])
    dn = r["dnconv"].transpose(2, 1, 0).reshape(3 + SAMPLES, 12 * P)
    ffn = r["ffnconv"].transpose(2, 1, 0).reshape(2 + SAMPLES, D_FF)
    return (y[None, :SEQ], y[SEQ:, None], *kv_p,
            dn[None, None, :3], r["pS"].reshape(P, DN_H, P).transpose(1, 0, 2)[None, None], ffn[None, None, :2],
            *kv_s,
            np.concatenate([r["dnrows"], dn[3:, None]], 1)[None], r["sS"].transpose(2, 1, 0, 3)[None],
            np.concatenate([r["ffnrows"], ffn[2:, None]], 1)[None])


def kernel(**inputs):
    import concourse.bacc as bacc
    from concourse.bass_utils import run_bass_kernel_spmd

    nc = bacc.Bacc("TRN2", target_bir_lowering=False, num_devices=1)
    arrays = {"in_" + name: np.ascontiguousarray(a) for name, a in layout(inputs).items()}
    ins = {name[3:]: nc.dram_tensor(name, a.shape, mybir.dt.from_np(a.dtype), kind="ExternalInput").ap()
           for name, a in arrays.items()}
    outs = {name: nc.dram_tensor("out_" + name, shape, F32, kind="ExternalOutput").ap() for name, shape in OUTS.items()}
    build(nc, ins, outs)
    r = run_bass_kernel_spmd(nc, [arrays], core_ids=[0])
    r = {name: r.results[0]["out_" + name] for name in OUTS}
    return tuple(np.ascontiguousarray(a) for a in gather(r))
```

```python
import numpy as np

import concourse.bass as bass
from concourse import mybir
from contextlib import ExitStack

F32 = mybir.dt.float32
F32R = mybir.dt.float32r
ALU = mybir.AluOpType
ACT = mybir.ActivationFunctionType
AX = mybir.AxisListType

P = 128
D_MODEL, SEQ, SAMPLES = 1024, 1024, 8
D_FF = 2816
DIL = ((128, 1), (512, 4), (2048, 16))
GROUPS, HPG, HD = 3, 4, 64
ATT_W = GROUPS * HPG * HD
DN_H, DN_D = 4, 128
TOK = SEQ + SAMPLES
THIRDS = 3
TW = TOK // THIRDS
KT = D_MODEL // P
FT = D_FF // P
OFF_DN = 3 * ATT_W
OFF_Z = OFF_DN + 3 * DN_H * DN_D
OFF_BA = OFF_Z + DN_H * DN_D
OFF_GATE = OFF_BA + 2 * DN_H
ALPHA = 2.0 ** 0.25
LN_EPS, RMS_EPS = 1e-5, 1e-6
NEG = -1e30
N_CONSTS = 4
CONV_STEPS = 16
FFN_STEPS = 12
SMALL_0, SMALL_S, DN_STEPS = 5, 18, 20
BLOCKS = 8
TILES = SEQ // P
PAST = (128, 512, 1024)
SKEYS = (8, 8, 4)
SK = sum(SKEYS)

U_BLK = 10
U_DN = 18
U_Z = U_DN + 12
U_GATE = U_Z + DN_H
U_BRANCH = U_GATE + 16
U_MIX = U_BRANCH + KT
U_FFN = U_MIX + KT
PIECES = (8, 8, 6)
WINDOWS = TILES + 1
LAST_USED = 3 * (U_FFN - U_BRANCH + len(PIECES) * KT)
UNITS = U_FFN + sum(2 * n + KT for n in PIECES)

C_ID, C_DNW, C_FFW, C_FFB, C_G1, C_B1, C_ON, C_R, C_END = np.cumsum(
    [0, P, 12 * 4, FT * 3, FT, KT, KT, 1, P]).tolist()
D_TRI, D_NEG, D_STR, D_ONE, D_LEV, D_END = np.cumsum([0, P, P, P, P, 7 * P]).tolist()


def third(j):
    return slice(j * TW, (j + 1) * TW)


def build(nc, I, O):
    ctx = ExitStack()
    with ctx:
        def sem(name):
            return ctx.enter_context(nc.semaphore(name))

        def held(stack, name, shape, dt=F32):
            return stack.enter_context(nc.sbuf_tensor(name, shape, dt))

        att_scr = nc.dram_tensor("att_scr", [GROUPS, SEQ, HPG * 66], F32).ap()
        dn_scr = nc.dram_tensor("dn_scr", [16, P, SEQ + P], F32).ap()
        gate_scr = nc.dram_tensor("gate_scr", [16, P, TOK], F32).ap()

        xh = held(ctx, "xh", [P, KT, TOK], F32R)
        xl = held(ctx, "xl", [P, KT, TOK], F32R)
        stage = held(ctx, "stage", [P, 2, KT * P])
        wh = held(ctx, "wh", [P, 2, KT * P], F32R)
        wl = held(ctx, "wl", [P, 2, KT * P], F32R)
        cst = held(ctx, "cst", [P, C_END])
        ident = cst[:, C_ID:C_ID + P]
        mhalf = held(ctx, "mhalf", [P, 64])
        babuf = held(ctx, "babuf", [P, 8, 9, DN_H])

        early = ExitStack()
        with early:
            qkv = held(early, "qkv", [P, 18, TOK])
            q_st = held(early, "q_st", [P, 2, P])
            k_st = held(early, "k_st", [P, 2, 2, P])
            v_st = held(early, "v_st", [P, 2, P])
            bias = held(early, "bias", [P, 4, 2, P])
            sb = held(early, "sb", [P, 4, 2, P])
            pb = held(early, "pb", [P, 4, 2, P])
            pts = held(early, "pts", [P, 8, P])
            vtok = held(early, "vtok", [P, 2, 256])
            obuf = held(early, "obuf", [P, 2, 4, 66])
            nmax = held(early, "nmax", [P, 4])
            pre = held(early, "pre", [P, 2, 3 + TOK])
            cb = held(early, "cb", [P, TOK])
            thb = held(early, "thb", [P, TOK])
            tails = held(early, "tails", [P, 12, 11])
            sconv = held(early, "sconv", [P, 12, SAMPLES, 3])
            wba = held(early, "wba", [P, KT, 8])
            bac = held(early, "bac", [P, 2, DN_H])
        xraw = qkv[:, 10:18, :]

        middle = ExitStack()
        with middle:
            oh = held(middle, "oh", [P, 6, TOK], F32R)
            ol = held(middle, "ol", [P, 6, TOK], F32R)
            with ExitStack() as part:
                prod = held(part, "prod", [P, 8, 4, 64])
                sq = held(part, "sq", [SAMPLES, 3, 3, 256])
                qb = held(part, "qb", [P, 3, 256])
                ssc = held(part, "ssc", [P, SK, 4])
                sbias = held(part, "sbias", [P, SK, 4])
                og = held(part, "og", [P, 3, 256])
                rt = held(part, "rt", [P, SAMPLES])
                sm = held(part, "sm", [P, 16, 4])
                self_s = held(part, "self_s", [SAMPLES, 3, 4])
                self_p = held(part, "self_p", [SAMPLES, 3, 256])
                o8 = held(part, "o8", [SAMPLES, 256])
                kvc = held(part, "kvc", [P, SK, 2, 256])
            with ExitStack() as part:
                gates = held(part, "gates", [P, 2, 2, TOK])
            dcst = held(middle, "dcst", [P, D_END])
            cf = held(middle, "cf", [P, 5, 4 * TILES])
            onh = held(middle, "onh", [P, 1])
            gth = held(middle, "gth", [P, 2, TOK])
            part = ExitStack()
            with part:
                dnin = held(part, "dnin", [P, 12, P])
                zin = held(part, "zin", [P, 4, P])
                abuf = held(part, "abuf", [P, 3, 4, 66])
                amx = held(part, "amx", [P, 8, 4])
                ao = held(part, "ao", [P, 4, 64])
                rn = held(part, "rn", [P, 4, 8])
                of = held(part, "of", [P, 4, P])
                ET = held(part, "ET", [P, 4, P])
                ETs = held(part, "ETs", [P, 4, P])
                sq2 = held(part, "sq2", [P, 8, P])
                qn, kn, kb, qd, kbe, kd, vb = (held(part, n, [P, 4, P]) for n in
                                               ("qn", "kn", "kb", "qd", "kbe", "kd", "vb"))
                kqT = held(part, "kqT", [P, 2, 4 * P])
                kbT, qdT, ATm, LTm, XT, S = (held(part, n, [P, 4 * P]) for n in (
                    "kbT", "qdT", "ATm", "LTm", "XT", "S"))
                flat4 = lambda ap: ap.rearrange("p h k -> p (h k)")
                X, Lb, Y = kbT, kqT, flat4(sq2[:, 4:8, :])
                wkT, us = flat4(qn[:]), flat4(kb[:])
                gB = ATm[:].rearrange("p (h k) -> p h k", h=4)
            part = ExitStack()
            with part:
                sS = held(part, "sS", [P, DN_H, SAMPLES, P])
                sin = held(part, "sin", [P, 16, SAMPLES])
                s64 = held(part, "s64", [P, 6, 64])
                sdv = held(part, "sdv", [P, 2, 4, P])
                sdiag = held(part, "sdiag", [SAMPLES, 2, SAMPLES, DN_H])
                sof = held(part, "sof", [P, DN_H, SAMPLES])

        late = ExitStack()
        with late:
            hh = held(late, "hh", [P, KT, TOK], F32R)
            hl = held(late, "hl", [P, KT, TOK], F32R)
            acc = held(late, "acc", [P, KT, TOK])
            ab = held(late, "ab", [P, 2 + TOK])
            cc = held(late, "cc", [P, TOK])
            gl = held(late, "gl", [P, TOK])
            fstate = held(late, "fstate", [P, FT, SAMPLES, 2])
            ftails = held(late, "ftails", [P, FT, 10])
            stats = held(late, "stats", [P, 2, 2, 6])
            mv = held(late, "mv", [P, 2, 4])
            mt = ab[:, 0:TW]
            xn = (gl[:, 0:D_MODEL], cc[:, 0:D_MODEL])
        with ExitStack() as part:
            g2r = held(part, "g2r", [P, D_MODEL])
            b2r = held(part, "b2r", [P, D_MODEL])
            yt = held(part, "yt", [P, 2, D_MODEL])

        U = ctx.enter_context(nc.psum_tensor("U", [P, 3, 512], F32))
        B34 = ctx.enter_context(nc.psum_tensor("B34", [P, 2, 512], F32))
        B56 = ctx.enter_context(nc.psum_tensor("B56", [P, 2, 512], F32))
        B7 = ctx.enter_context(nc.psum_tensor("B7", [P, 512], F32))

        consts_in = sem("consts_in")
        x_in = [sem(f"x_in{i}") for i in range(4)]
        x_hi, x_lo, conv_in = sem("x_hi"), sem("x_lo"), sem("conv_in")
        zeroed = sem("zeroed")
        w_in = [sem("w_in0"), sem("w_in1")]
        w_hi, w_lo = sem("w_hi"), sem("w_lo")
        slice_done = sem("slice_done")
        taken = sem("taken")
        ba_rows, ba_staged = sem("ba_rows"), sem("ba_staged")
        ba_done, ba_raw, ba_act, ba_dve = sem("ba_done"), sem("ba_raw"), sem("ba_act"), sem("ba_dve")
        bias_in = sem("bias_in")
        qk_staged, v_staged = sem("qk_staged"), sem("v_staged")
        s_done, biased, maxed, exped = sem("s_done"), sem("biased"), sem("maxed"), sem("exped")
        pt_done, pt_taken = sem("pt_done"), sem("pt_taken")
        v_done, v_taken = sem("v_done"), sem("v_taken")
        pv_done, o_taken = sem("pv_done"), sem("o_taken")
        o_stored = [sem("o_stored0"), sem("o_stored1")]
        kv_stored = sem("kv_stored")
        conv_step, conv_tanh, conv_out, conv_stored, tail_stored = (
            sem("conv_step"), sem("conv_tanh"), sem("conv_out"), sem("conv_stored"), sem("tail_stored"))
        small_step = sem("small_step")
        pe_step, act_step, pool_step = sem("pe_step"), sem("act_step"), sem("pool_step")
        samp_in, samp_pe, samp_act, samp_dve = sem("samp_in"), sem("samp_pe"), sem("samp_act"), sem("samp_dve")
        dcst_in, dn_in, z_in, att_in = sem("dcst_in"), sem("dn_in"), sem("z_in"), sem("att_in")
        used = sem("used")
        gates_in = [sem("gates_in0"), sem("gates_in1")]
        merged, m_high, m_low, acc_in = sem("merged"), sem("m_high"), sem("m_low"), sem("acc_in")
        ln_in, ln_var, ln_root, ln_shift, ln_norm, ln_back, ln_front, ln_rear, h_high, h_low, ln_step, ln_mul = (
            sem(n) for n in ("ln_in", "ln_var", "ln_root", "ln_shift", "ln_norm", "ln_back", "ln_front", "ln_rear",
                             "h_high", "h_low", "ln_step", "ln_mul"))
        y_rear = sem("y_rear")
        fstate_in, f_zero, a_taken, f_step, f_gelu, f_prod, f_high, f_low = (
            sem(n) for n in ("fstate_in", "f_zero", "a_taken", "f_step", "f_gelu", "f_prod", "f_high", "f_low"))
        rows2_in, y_ready, y_stored, ftail_stored = sem("rows2_in"), sem("y_ready"), [sem("y_s0"), sem("y_s1")], sem("ftail_stored")
        ds_in, ds_pe, ds_act, ds_dve, ds_scaled, ds_prod, ds_new, ds_o = (
            sem(n) for n in ("ds_in", "ds_pe", "ds_act", "ds_dve", "ds_scaled", "ds_prod", "ds_new", "ds_o"))
        half_set = sem("half_set")
        ss_ready, rs_ready = sem("ss_ready"), sem("rs_ready")
        cf_pe, cf_dve, cf_act = sem("cf_pe"), sem("cf_dve"), sem("cf_act")
        g_staged, g_done, decay_sum, decay_exp = sem("g_staged"), sem("g_done"), sem("decay_sum"), sem("decay_exp")
        lb_ready = sem("lb_ready")
        tv_done, g_read, x_added, z_done = sem("tv_done"), sem("g_read"), sem("x_added"), sem("z_done")
        tr1_done, squared, qkn_ready, kbqd_ready = sem("tr1_done"), sem("squared"), sem("qkn_ready"), sem("kbqd_ready")
        v_ready, tr2_done, kqT_taken, tr3_done, kbqd_taken = (
            sem("v_ready"), sem("tr2_done"), sem("kqT_taken"), sem("tr3_done"), sem("kbqd_taken"))
        la_done, y_done, y_taken, zt_done, xt_ready, x_done, x_taken = (
            sem("la_done"), sem("y_done"), sem("y_taken"), sem("zt_done"), sem("xt_ready"), sem("x_done"),
            sem("x_taken"))
        wk_done, wk_taken, u_done, u_taken, od_done, s_ready = (
            sem("wk_done"), sem("wk_taken"), sem("u_done"), sem("u_taken"), sem("od_done"), sem("s_ready"))
        o_squared, on_ready, on_done, of_ready, of_high, of_low = (
            sem("o_squared"), sem("on_ready"), sem("on_done"), sem("of_ready"), sem("of_high"), sem("of_low"))
        ae_ready, ae_exp, ao_ready, ao_done, ao_high, ao_low = (
            sem("ae_ready"), sem("ae_exp"), sem("ao_ready"), sem("ao_done"), sem("ao_high"), sem("ao_low"))
        gate_stored, dn_step, shifted, state_stored, pad_stored = (
            [sem("gate_stored0"), sem("gate_stored1")], sem("dn_step"), sem("shifted"), sem("state_stored"), sem("pad_stored"))


        GT = (0, 12, 6)
        ALL_QKV = 3 * U_DN

        def pairs(eng, first, count):
            with eng.Fori(0, count // 2) as i:
                for half in (0, 1):
                    yield i * 2 + (first + half), half, i

        def peeled(first, count):
            for n in range(first, first + count):
                yield n, n % 2, None

        def after(eng, s, n):
            if not (isinstance(n, int) and n <= 0):
                eng.wait_ge(s, n)

        def bulk(eng):
            yield from peeled(0, 2)
            yield from pairs(eng, 2, U_BLK - 2)

        class Steps:

            def __init__(self, eng, s):
                self.eng, self.s, self.base, self.n = eng, s, 0, 0

            def item(self, index, per):
                self.base, self.n, self.per = index * per, 0, per

            def link(self, ins):
                self.n += 1
                ins.then_inc(self.s, 1)
                self.eng.wait_ge(self.s, self.base + self.n)

        def blocks_of(eng, before_group=None):
            for b, par, _ in peeled(0, 2):
                yield b, par, 0, b, b > 0, "att"
            for b, par, i in pairs(eng, 2, 6):
                yield b, par, 0, b, True, "att"
            if before_group:
                before_group(1)
            for b, par, i in pairs(eng, BLOCKS, BLOCKS):
                yield b, par, 1, (i, par), par == 1, "dn"
            if before_group:
                before_group(2)
            for b, par, i in pairs(eng, 2 * BLOCKS, 4):
                yield b, par, 2, i * 2 + par, False, "dn"
            for b, par, i in pairs(eng, 2 * BLOCKS + 4, 4):
                yield b, par, 2, i * 2 + (4 + par), False, "z"

        def cols(tiles, g, n):
            if g == 0:
                return tiles[:, :, bass.ds(n * P, P)]
            v = tiles.rearrange("p j (i d) -> p j d i", d=DIL[g][1])
            if g == 1:
                return v[:, :, bass.ds(n[0], 1), n[1] * P:(n[1] + 1) * P].squeeze(2)
            return v[:, :, bass.ds(n * 2, 2), :]

        def packed(t, g):
            return t.rearrange("p j (d i) -> p j d i", d=2) if g == 2 else t

        def stored_before(b, par, g, n):
            if g == 0:
                return (b - par) * 8
            if g == 1:
                return n[0] * 16 + 64
            return (n - par) * 16 + 128

        CHUNKS = 36
        LEVELS = 6

        class Beside:

            def __init__(self, u, chunk, start_unit):
                self.u, self.chunk, self.start_unit, self.c = u, chunk, start_unit, 0

            def run(self, n):
                for c in range(self.c, min(self.c + n, CHUNKS)):
                    if c % 18 == 0:
                        self.start_unit(self.u + c // 18, c // 18)
                    self.chunk(self.u + c // 18, c // 18, c % 18 // 6, c % 6)
                self.c = min(self.c + n, CHUNKS)

        def window(t):
            return t % 2, slice(t * P, min((t + 1) * P, TOK)), min(P, TOK - t * P)

        def pieces():
            f0, u0, before = 0, U_FFN, 3 * (U_FFN - U_BRANCH)
            for n in PIECES:
                yield n, f0, u0, before
                f0, u0, before = f0 + n, u0 + 2 * n + KT, before + 3 * KT

        block = ctx.enter_context(nc.Block())

        @block.sync
        def _(sp):
            for i in range(4):
                sp.dma_start(xraw[:, 2 * i:2 * i + 2, :], I["xT"][:, 2 * i:2 * i + 2, :]).then_inc(x_in[i], 16)
                if i < 2:
                    sp.dma_start(stage[:, i, :], I["wu"][i]).then_inc(w_in[i], 16)

            def load(u, par):
                sp.wait_ge(w_lo, u - 1)
                sp.dma_start(stage[:, par, :], I["wu"][bass.ds(u, 1)].squeeze(0)).then_inc(w_in[par], 16)

            sp.dma_start(dn_scr[0:12, :, TOK:SEQ + P], I["wu"][0:12, :, 0:SEQ + P - TOK]).then_inc(pad_stored, 16)
            sp.dma_start(O["dnrows"], I["dnrows"][:, 1:3, :]).then_inc(shifted, 16)
            sp.dma_start(O["ffnrows"], I["ffnrows"][:, 1:2, :]).then_inc(shifted, 16)
            for u, par, _ in bulk(sp):
                load(u + 2, par)

            def next_bias(g):
                sp.wait_ge(biased, g * BLOCKS)
                sp.dma_start(bias[:], I["bias"][g]).then_inc(bias_in, 16)
                if g == 2:
                    sp.wait_ge(taken, ALL_QKV)
                    for grp in range(GROUPS):
                        keep = min(DIL[grp][0], SEQ)
                        sp.dma_start(O[f"kv{grp}"], qkv[:, GT[grp] + 2:GT[grp] + 6, SEQ - keep:TOK]).then_inc(
                            kv_stored, 16)

            for b, par, g, n, prev, kind in blocks_of(sp, next_bias):
                load(b + (U_BLK + 2), par)
                sp.wait_ge(o_taken, b + 1)
                src = obuf[:, par, :, :].rearrange("p h c -> p (h c)")
                if g == 0:
                    sp.dma_start(att_scr[0][bass.ds(b * P, P), :], src).then_inc(o_stored[par], 16)
                elif g == 1:
                    dst = att_scr[1].rearrange("(i d) c -> d i c", d=4)
                    sp.dma_start(dst[bass.ds(n[0], 1), par * P:(par + 1) * P, :].squeeze(0), src).then_inc(
                        o_stored[par], 16)
                else:
                    dst = att_scr[2].rearrange("(i d) c -> d i c", d=16)
                    for r in range(2):
                        sp.dma_start(dst[bass.ds(n * 2 + r, 1)].squeeze(0), src[64 * r:64 * r + 64, :]).then_inc(
                            o_stored[par], 16)
                if kind != "att":
                    f = b - BLOCKS
                    sp.wait_ge(conv_out, f + 2)
                    sp.dma_start(dn_scr[bass.ds(f, 1), :, 0:TOK].squeeze(0), cb[:]).then_inc(conv_stored, 16)
            sp.dma_start(O["dnconv"], tails[:]).then_inc(tail_stored, 16)
            sp.wait_ge(conv_stored, 16 * 16)
            sp.wait_ge(tail_stored, 16)
            for par in (0, 1):
                sp.wait_ge(o_stored[par], 16 * (4 + 4 + 8))
            sp.wait_ge(pv_done, 24)
            sp.wait_ge(conv_out, 17)
            k0 = 0
            for g in (0, 2, 1):
                src = I[f"cache{g}"].rearrange("b (c j d) e -> (b c) j d e", c=16, d=DIL[g][1])
                sp.dma_start(kvc[:, k0:k0 + SKEYS[g]].rearrange("p j a e -> p j (a e)"), src[:, :, 0, :]).then_inc(
                    samp_in, 16)
                k0 += SKEYS[g]
            sp.wait_ge(kv_stored, 48)
            sp.wait_ge(samp_act, 1)
            sp.dma_start(sbias[:], I["sbias"]).then_inc(samp_in, 16)
            sp.dma_start(rt[:], I["rt"]).then_inc(samp_in, 16)
            sp.wait_ge(ao_low, 1)
            sp.dma_start(dcst[:], I["dcst"]).then_inc(dcst_in, 16)

            def rows_in(t):
                sp.dma_start(dnin[:], dn_scr[0:12, :, bass.ds(t * P, P)].rearrange("f p t -> p f t")).then_inc(
                    dn_in, 16)

            sp.wait_ge(pad_stored, 16)
            rows_in(0)
            with sp.Fori(0, TILES) as t:
                u = t * 2 + U_GATE
                load(u + 2, 0)
                after(sp, of_low, t)
                sp.dma_start(zin[:], dn_scr[12:16, :, bass.ds(t * P, P)].rearrange("f p t -> p f t")).then_inc(z_in, 16)
                sp.wait_ge(ao_low, t + 1)
                sp.dma_start(abuf[:].rearrange("p g h c -> p g (h c)"),
                             att_scr[:, bass.ds(t * P, P), :].rearrange("g t c -> t g c")).then_inc(att_in, 16)
                for g in range(GROUPS):
                    sp.dma_start(O[f"shift{g}"][bass.ds(t, 1)], I[f"cache{g}"][bass.ds(t, 1), 1:, :]).then_inc(
                        shifted, 16)
                sp.wait_ge(v_ready, t + 1)
                sp.dma_start(dnin[:], dn_scr[0:12, :, bass.ds((t + 1) * P, P)].rearrange("f p t -> p f t")).then_inc(
                    dn_in, 16)
                load(u + 3, 1)
                for half in (0, 1):
                    sp.wait_ge(taken, (u + (half + 1)) * 3)
                    sp.dma_start(gate_scr[bass.ds(t * 2 + half, 1)].squeeze(0), gth[:, half, :]).then_inc(
                        gate_stored[half], 16)
            sp.wait_ge(s_ready, TILES + 1)
            sp.dma_start(O["pS"], S[:]).then_inc(state_stored, 16)
            sp.wait_ge(state_stored, 16)
            sp.wait_ge(of_low, TILES)
            sp.dma_start(sS[:], I["sS"]).then_inc(ds_in, 16)
            sp.dma_start(sin[:], dn_scr[:, :, SEQ:TOK].rearrange("f p b -> p f b")).then_inc(ds_in, 16)
            sp.wait_ge(ds_new, 8)
            sp.dma_start(O["sS"], sS[:]).then_inc(state_stored, 16)
            sp.wait_ge(of_low, TILES + 1)
            sp.wait_ge(state_stored, 32)
            for par in (0, 1):
                sp.wait_ge(gate_stored[par], 16 * TILES)
            sp.wait_ge(shifted, 16 * 26)

            def gates_of(f, par):
                sp.dma_start(gates[:, par, :, :], gate_scr[bass.ds(f * 2, 2)].rearrange("g p t -> p g t")).then_inc(
                    gates_in[par], 16)

            gates_of(0, 0)
            gates_of(1, 1)
            sp.dma_start(acc[:], I["xT"]).then_inc(acc_in, 16)
            sp.dma_start(fstate[:], I["fstate"]).then_inc(fstate_in, 16)
            for f, par, _ in pairs(sp, 0, KT - 2):
                load(f + (U_BRANCH + 2), par)
                sp.wait_ge(used, f * 3 + 3)
                gates_of(f + 2, par)
            for f in range(KT - 2, KT):
                load(f + (U_BRANCH + 2), f % 2)
            for u, par, _ in pairs(sp, U_MIX + 2, UNITS - U_MIX - 2):
                load(u, par)
            sp.wait_ge(used, LAST_USED)
            sp.wait_ge(f_low, FT)
            sp.wait_ge(slice_done, 3 * UNITS)
            sp.dma_start(O["ffnconv"], ftails[:]).then_inc(ftail_stored, 16)
            sp.dma_start(g2r[:], I["g2"].to_broadcast([P, D_MODEL])).then_inc(rows2_in, 16)
            sp.dma_start(b2r[:], I["b2"].to_broadcast([P, D_MODEL])).then_inc(rows2_in, 16)
            for t in range(WINDOWS):
                par, win, m = window(t)
                sp.wait_ge(y_ready, t + 1)
                sp.wait_ge(y_rear, t + 1)
                sp.dma_start(O["y"][win, :], yt[0:m, par, :]).then_inc(y_stored[par], 16)
            sp.wait_ge(y_stored[0], 16 * 5)
            sp.wait_ge(y_stored[1], 16 * 4)
            sp.wait_ge(ftail_stored, 16)

        @block.gpsimd
        def _(pool):
            def low(u, par):
                pool.wait_ge(w_hi, u + 1)
                nc.gpsimd.tensor_tensor(wl[:, par, :], stage[:, par, :], wh[:, par, :].bitcast(F32),
                                        ALU.subtract).then_inc(w_lo, 1)

            def inverse_root(x, n):
                pool.wait_ge(ss_ready, n)
                nc.gpsimd.tensor_tensor(x, x, mhalf[0:x.shape[0], 0:x.shape[1]], ALU.pow).then_inc(rs_ready, 1)

            nc.gpsimd.memset(mhalf[:], -0.5).then_inc(half_set, 1)
            for u, par, _ in pairs(pool, 0, U_GATE):
                low(u, par)
            pool.wait_ge(half_set, 1)
            low(U_GATE, 0)
            inverse_root(rn[:, 1, :], 1)
            with pool.Fori(0, TILES) as t:
                low(t * 2 + (U_GATE + 1), 1)
                low(t * 2 + (U_GATE + 2), 0)
                inverse_root(rn[:, 3, 4:8], t * 2 + 2)
                inverse_root(rn[:, 1, :], t * 2 + 3)
            inverse_root(s64[0:64, 1, 0:1], 2 * TILES + 2)
            inverse_root(s64[0:32, 1, 1:2], 2 * TILES + 3)

            def root(t, first):
                par, win, m = window(t)
                pool.wait_ge(ln_var, first + t + 1)
                nc.gpsimd.tensor_tensor(mv[0:m, par, 2:3], mv[0:m, par, 1:2], mhalf[0:m, 0:1], ALU.pow).then_inc(
                    ln_root, 1)

            for u, par, _ in pairs(pool, U_BRANCH + 1, U_FFN - U_BRANCH):
                low(u, 1 - par)
            for t in range(WINDOWS + 2):
                if t < WINDOWS:
                    root(t, 0)
                if t >= 2:
                    win = window(t - 2)[1]
                    pool.wait_ge(h_high, t - 1)
                    nc.gpsimd.tensor_tensor(hl[:, :, win], acc[:, :, win], hh[:, :, win].bitcast(F32),
                                            ALU.subtract).then_inc(h_low, 1)
            for u, par, _ in pairs(pool, U_FFN + 1, UNITS - U_FFN - 2):
                low(u, 1 - par)
            low(UNITS - 1, 1)
            pool.wait_ge(rows2_in, 32)
            for t in range(WINDOWS + 1):
                if t < WINDOWS:
                    root(t, WINDOWS)
                if t >= 1:
                    par, win, m = window(t - 1)
                    pool.wait_ge(ln_mul, WINDOWS + t)
                    nc.gpsimd.tensor_tensor(yt[0:m, par, 512:], yt[0:m, par, 512:], b2r[0:m, 512:], ALU.add).then_inc(
                        y_rear, 1)

        @block.tensor
        def _(pe):
            def products(dst, par, j, ks, x=None):
                hi, lo = x or (xh, xl)
                for n, (k, xk) in enumerate(ks):
                    w = slice(k * P, (k + 1) * P)
                    for m, (a, b) in enumerate(((wh, hi), (wl, hi), (wh, lo))):
                        ins = nc.tensor.matmul(dst, a[:, par, w], b[:, xk, third(j)],
                                               start=n == 0 and m == 0, stop=n == len(ks) - 1 and m == 2)
                return ins

            def unit_slice(u, par, j):
                after(pe, taken, u * 3 + (j - 2))
                pe.wait_ge(w_lo, u + 1)
                products(U[:, j, 0:TW], par, j, [(k, k) for k in range(KT)]).then_inc(slice_done, 1)

            pe.wait_ge(consts_in, 16 * N_CONSTS)
            for k in range(KT):
                pe.wait_ge(x_in[k // 2], 16)
                for j in range(THIRDS):
                    dst = (B34[0:8, 0, 0:TW], B34[0:8, 1, 0:TW], B56[0:8, 0, 0:TW])[j]
                    ins = nc.tensor.matmul(dst, wba[:, k, :], xraw[:, k, third(j)], start=k == 0, stop=k == KT - 1)
            ins.then_inc(ba_rows, 1)
            for u, par, _ in bulk(pe):
                if isinstance(u, int) and u == 0:
                    for k in range(KT):
                        pe.wait_ge(x_lo, k + 1)
                for j in range(THIRDS):
                    unit_slice(u, par, j)
                if isinstance(u, int) and u == 0:
                    pe.wait_ge(ba_staged, 1)
                    for t in range(TILES + 1):
                        m = P if t < TILES else SAMPLES
                        ins = nc.tensor.transpose(B7[0:m, 8 * t:8 * t + 8], cb[0:8, t * P:t * P + m], ident[0:8, 0:8])
                    ins.then_inc(ba_done, 1)
            pe.wait_ge(ba_raw, 1)
            for b, par, g, n, prev, kind in blocks_of(pe):
                u = b + U_BLK
                parts = 2 if prev else 1
                unit_slice(u, par, 0)
                pe.wait_ge(qk_staged, b + 1)
                after(pe, biased, b)
                for h in range(HPG):
                    hp, j = h % 2, h // 2
                    rows = slice(64 * hp, 64 * hp + 64)
                    for part in range(parts):
                        ins = nc.tensor.matmul(B34[:, hp, j * 256 + part * P:j * 256 + (part + 1) * P],
                                               q_st[rows, j, :], k_st[rows, (par + part) % 2, j, :],
                                               start=True, stop=True)
                ins.then_inc(s_done, 1)
                pe.wait_ge(v_staged, b + 1)
                after(pe, v_taken, b)
                after(pe, o_taken, b)
                for j in range(2):
                    ins = nc.tensor.transpose(B7[:, j * P:(j + 1) * P], v_st[:, j, :], ident)
                ins.then_inc(v_done, 1)
                unit_slice(u, par, 1)
                pe.wait_ge(exped, b + 1)
                after(pe, pt_taken, b)
                for slot in range(HPG):
                    for part in range(parts):
                        c = ((slot % 2) * 2 + part) * P
                        ins = nc.tensor.transpose(B56[:, slot // 2, c:c + P], pb[:, slot, part, :], ident)
                ins.then_inc(pt_done, 1)
                unit_slice(u, par, 2)
                pe.wait_ge(pt_taken, b + 1)
                pe.wait_ge(v_taken, b + 1)
                for h in range(HPG):
                    slot = (h % 2) * 2 + h // 2
                    for part in range(parts):
                        ins = nc.tensor.matmul(B7[:, 256 + 64 * h:256 + 64 * h + 64], pts[:, 2 * slot + part, :],
                                               vtok[:, (par + part) % 2, 64 * h:64 * h + 64],
                                               start=part == 0, stop=part == parts - 1)
                ins.then_inc(pv_done, 1)

            def step(ins):
                ins.then_inc(samp_pe, 1)

            pe.wait_ge(o_taken, 24)
            pe.wait_ge(pt_taken, 24)
            pe.wait_ge(biased, 24)
            pe.wait_ge(v_taken, 24)
            for n in range(18):
                dst = (B34, B56, B7)[n // 8]
                dst = dst[0:SAMPLES, n % 8 // 4, n % 4 * P:(n % 4 + 1) * P] if n < 16 else \
                    B7[0:SAMPLES, (n - 16) * P:(n - 15) * P]
                ins = nc.tensor.matmul(dst, qkv[:, n, SEQ:TOK], ident, start=True, stop=True)
            step(ins)
            pe.wait_ge(samp_act, 2)
            for n in range(3):
                ins = nc.tensor.matmul(B34[:, n // 2, n % 2 * 256:n % 2 * 256 + 256], cst[0:SAMPLES, C_R:C_END],
                                       sq[:, n, 0, :], start=True, stop=True)
            step(ins)
            pe.wait_ge(samp_dve, 1)
            nc.tensor.matmul(B7[0:4, 0:P], sm[:, 0, :], ident, start=True, stop=True)
            ins = nc.tensor.matmul(B7[0:4, P:P + SAMPLES], sm[0:SAMPLES, 1, :], ident[0:SAMPLES, 0:SAMPLES],
                                   start=True, stop=True)
            step(ins)
            pe.wait_ge(samp_dve, 2)
            step(nc.tensor.matmul(B34[0:SAMPLES, 0, 0:4], sm[0:4, 4:6, :].rearrange("p a c -> p (a c)"),
                                  ident[0:4, 0:4], start=True, stop=True))
            pe.wait_ge(samp_dve, 3)
            step(nc.tensor.matmul(B56[:, 0, 0:4], cst[0:SAMPLES, C_R:C_END], sm[0:SAMPLES, 6, :],
                                  start=True, stop=True))
            pe.wait_ge(samp_dve, 4)
            pe.wait_ge(samp_in, 16 * 5)
            for n in range(3):
                nc.tensor.matmul(B7[0:SAMPLES, 0:256], rt[:], og[:, n, :], start=n == 0, stop=False)
            for n in range(3):
                nc.tensor.matmul(B7[0:SAMPLES, 0:256], ident[0:SAMPLES, 0:SAMPLES], self_p[:, n, :], start=False,
                                 stop=n == 2)
            nc.tensor.matmul(B7[0:SAMPLES, 256:260], rt[:], sm[:, 7, :], start=True, stop=False)
            for n in range(3):
                ins = nc.tensor.matmul(B7[0:SAMPLES, 256:260], ident[0:SAMPLES, 0:SAMPLES], self_s[:, n, :],
                                       start=False, stop=n == 2)
            step(ins)
            pe.wait_ge(samp_dve, 5)
            for n in range(2):
                ins = nc.tensor.matmul(B34[:, 1, n * SAMPLES:(n + 1) * SAMPLES], o8[:, n * P:(n + 1) * P],
                                       ident[0:SAMPLES, 0:SAMPLES], start=True, stop=True)
            step(ins)

            pe.wait_ge(ao_low, 1)
            pe.wait_ge(dcst_in, 16)
            gall = babuf[:, 1, 0:TILES, :]
            tri = dcst[:, D_TRI:D_TRI + P]
            nc.tensor.matmul(B7[:, 0:32], tri, gall, start=True, stop=True)
            nc.tensor.matmul(B7[:, 32:64], dcst[:, D_ONE:D_ONE + P], gall, start=True, stop=True).then_inc(cf_pe, 1)
            pe.wait_ge(cf_act, 3)

            def start_unit(u, par):
                pe.wait_ge(w_lo, u + 1)

            def chunk(u, par, j, c):
                if c == 0:
                    pe.wait_ge(taken, u * 3 + (j - 2))
                for m in range(4 * c, 4 * c + 4):
                    a, x = ((wh, xh), (wl, xh), (wh, xl))[m % 3]
                    k = m // 3
                    ins = nc.tensor.matmul(U[:, j, 0:TW], a[:, par, k * P:(k + 1) * P], x[:, k, third(j)],
                                           start=m == 0, stop=m == 3 * KT - 1)
                if c == 5:
                    ins.then_inc(slice_done, 1)

            def heads():
                return [(h, slice(h * P, (h + 1) * P)) for h in range(DN_H)]

            def turn_qk(t):
                pe.wait_ge(dn_in, t * 16 + 16)
                for n in range(8):
                    ins = nc.tensor.transpose(B34[:, n // 4, n % 4 * P:(n % 4 + 1) * P], dnin[:, n, :], ident)
                ins.then_inc(tr1_done, 1)

            turn_qk(0)
            with pe.Fori(0, TILES) as t:
                beside = Beside(t * 2 + U_GATE, chunk, start_unit)
                pe.wait_ge(s_ready, t + 1)
                for h, c in heads():
                    ins = nc.tensor.transpose(B56[:, 0, c], dnin[:, 8 + h, :], ident)
                ins.then_inc(tv_done, 1)
                pe.wait_ge(g_staged, t + 1)
                for h, c in heads():
                    ins = nc.tensor.matmul(B56[:, 1, c], gB[:, h, :], tri, start=True, stop=True)
                ins.then_inc(g_done, 1)
                beside.run(3)
                pe.wait_ge(qkn_ready, t + 1)
                for src, dst in ((kn, B34[:, 0, :]), (qn, B34[:, 1, :])):
                    for h, c in heads():
                        ins = nc.tensor.transpose(dst[:, c], src[:, h, :], ident)
                ins.then_inc(tr2_done, 1)
                beside.run(2)
                pe.wait_ge(kbqd_ready, t + 1)
                pe.wait_ge(v_ready, t + 1)
                pe.wait_ge(of_low, t)
                for src, dst in ((kb, B56[:, 0, :]), (qd, B7[:, :])):
                    for h, c in heads():
                        ins = nc.tensor.transpose(dst[:, c], src[:, h, :], ident)
                ins.then_inc(tr3_done, 1)
                beside.run(3)
                pe.wait_ge(kqT_taken, t + 1)
                pe.wait_ge(kbqd_taken, t + 1)
                for rhs, dst in ((kbT, B34[:, 0, :]), (kqT[:, 1, :], B34[:, 1, :])):
                    for h, c in heads():
                        ins = nc.tensor.matmul(dst[:, c], kqT[:, 0, c], rhs[:, c], start=True, stop=True)
                ins.then_inc(la_done, 1)
                beside.run(4)
                pe.wait_ge(xt_ready, t * (LEVELS + 1) + 1)
                for h, c in heads():
                    ins = nc.tensor.transpose(B56[:, 0, c], XT[:, c], ident)
                ins.then_inc(x_done, 1)
                beside.run(1)
                for lv in range(LEVELS):
                    if lv == 0:
                        pe.wait_ge(x_taken, t + 1)
                        pe.wait_ge(lb_ready, t + 1)
                        pe.wait_ge(g_read, t + 1)
                    else:
                        pe.wait_ge(x_added, t * (LEVELS - 1) + lv)
                    for h, c in heads():
                        ins = nc.tensor.matmul(B56[:, 1, c], Lb[:, (lv + 1) % 2, c], X[:, c], start=True, stop=True)
                    ins.then_inc(y_done, 1)
                    beside.run(1)
                    pe.wait_ge(y_taken, t * LEVELS + (lv + 1))
                    pe.wait_ge(xt_ready, t * (LEVELS + 1) + (lv + 1))
                    if lv < LEVELS - 1:
                        for h, c in heads():
                            ins = nc.tensor.matmul(B56[:, 0, c], XT[:, c], Y[:, c], start=True, stop=True)
                        ins.then_inc(z_done, 1)
                    for h, c in heads():
                        ins = nc.tensor.matmul(B7[:, c], Y[:, c], XT[:, c], start=True, stop=True)
                    ins.then_inc(zt_done, 1)
                    if lv == 3:
                        pe.wait_ge(ao_ready, t + 1)
                        for n in range(2):
                            ins = nc.tensor.transpose(B34[:, 1, n * P:(n + 1) * P], ao[:].rearrange(
                                "p h e -> p (h e)")[:, n * P:(n + 1) * P], ident)
                        ins.then_inc(ao_done, 1)
                    beside.run(1)
                pe.wait_ge(xt_ready, t * (LEVELS + 1) + (LEVELS + 1))
                for h, c in heads():
                    ins = nc.tensor.matmul(B34[:, 0, c], kbe[:, h, :], XT[:, c], start=True, stop=True)
                ins.then_inc(wk_done, 1)
                beside.run(1)
                pe.wait_ge(ao_low, t + 2)
                pe.wait_ge(wk_taken, t + 1)
                for h, c in heads():
                    nc.tensor.matmul(B34[:, 1, c], XT[:, c], vb[:, h, :], start=True, stop=False)
                    ins = nc.tensor.matmul(B34[:, 1, c], wkT[:, c], S[:, c], start=False, stop=True)
                ins.then_inc(u_done, 1)
                beside.run(1)
                pe.wait_ge(u_taken, t + 1)
                for h, c in heads():
                    nc.tensor.matmul(B56[:, 0, c], qdT[:, c], S[:, c], start=True, stop=False)
                    nc.tensor.matmul(B56[:, 0, c], ATm[:, c], us[:, c], start=False, stop=True)
                for h, c in heads():
                    ins = nc.tensor.matmul(B56[:, 1, c], kd[:, h, :], us[:, c], start=True, stop=True)
                ins.then_inc(od_done, 1)
                beside.run(1)
                turn_qk(t + 1)
                beside.run(4)
                pe.wait_ge(on_ready, t + 1)
                for h, c in heads():
                    ins = nc.tensor.transpose(B7[:, c], of[:, h, :], ident)
                ins.then_inc(on_done, 1)
                beside.run(CHUNKS)

            pe.wait_ge(of_low, TILES)
            pe.wait_ge(ds_dve, 1)
            nc.tensor.matmul(B34[:, 0, 0:64], dcst[0:SAMPLES, D_ONE:D_ONE + P],
                             sdiag[:].rearrange("s x b h -> s (x b h)"), start=True, stop=True).then_inc(ds_pe, 1)
            pe.wait_ge(ds_act, 2)
            one = dcst[:, D_ONE:D_ONE + 1]
            nc.tensor.matmul(B34[0:64, 1, 0:1], s64[:, 0, :], one, start=True, stop=True).then_inc(ds_pe, 1)
            pe.wait_ge(rs_ready, 2 * TILES + 2)
            nc.tensor.matmul(B34[:, 1, 64:128], s64[0:64, 1, 0:1].to_broadcast([64, P]), ident[0:64, 0:64], start=True,
                             stop=True).then_inc(ds_pe, 1)
            pe.wait_ge(ds_dve, 2)

            def sample_out(n):
                h, b0 = n // 2, n % 2 * 4
                pe.wait_ge(ds_new, n + 1)
                for i in range(4):
                    col = h * SAMPLES + b0 + i
                    ins = nc.tensor.matmul(B7[:, col:col + 1], sS[:, h, b0 + i, :], s64[:, 2, col:col + 1], start=True,
                                           stop=True)
                return ins

            for n in range(8):
                h, b0 = n // 2, n % 2 * 4
                pe.wait_ge(ds_scaled, n + 1)
                bank = B56[:, n % 2, :]
                nc.tensor.matmul(bank, dcst[:, D_ONE:D_ONE + P], sdv[:, n % 2].rearrange("p i k -> p (i k)"),
                                 start=True, stop=False)
                for i in range(4):
                    col = h * SAMPLES + b0 + i
                    ins = nc.tensor.matmul(bank[:, i * P:(i + 1) * P], s64[:, 4, col:col + 1].to_broadcast([P, P]),
                                           sS[:, h, b0 + i, :], start=False, stop=i == 3)
                ins.then_inc(ds_prod, 1)
                if n > 0:
                    sample_out(n - 1)
            sample_out(7).then_inc(ds_o, 1)
            pe.wait_ge(ds_act, 3)
            nc.tensor.matmul(B34[0:32, 1, 0:1], s64[:, 0, 0:32], one, start=True, stop=True).then_inc(ds_pe, 1)
            pe.wait_ge(rs_ready, 2 * TILES + 3)
            nc.tensor.matmul(B34[:, 1, 64:96], s64[0:32, 1, 1:2].to_broadcast([32, P]), ident[0:32, 0:32], start=True,
                             stop=True).then_inc(ds_pe, 1)

            dbank = (B34[:, 0, :], B34[:, 1, :], B56[:, 0, :])
            pe.wait_ge(of_low, TILES + 1)
            pe.wait_ge(taken, 3 * U_BRANCH)

            def branch(f, par, skip_wait):
                u = f + U_BRANCH
                pe.wait_ge(w_lo, u + 1)
                for j in range(THIRDS):
                    if not skip_wait:
                        pe.wait_ge(used, f * 3 + (j - 2))
                    products(U[:, j, 0:TW], par, j, [(k, k) for k in range(2)], (oh, ol))
                    products(dbank[j][:, 0:TW], par, j, [(k, k) for k in range(2, 6)], (oh, ol)).then_inc(slice_done, 1)

            for f in range(2):
                branch(f, f, f == 0)
            for f, par, _ in pairs(pe, 2, KT - 2):
                branch(f, par, False)
            pe.wait_ge(m_low, 3 * KT)

            def from_used(u, par, j, n, parts, ks):
                pe.wait_ge(used, n)
                pe.wait_ge(w_lo, u + 1)
                products(U[:, j, 0:TW], par, j, ks, parts).then_inc(slice_done, 1)

            all_k = [(k, k) for k in range(KT)]
            for f, par, _ in pairs(pe, 0, KT):
                for j in range(THIRDS):
                    from_used(f + U_MIX, par, j, f * 3 + (3 * KT + j - 2), (xh, xl), all_k)

            by_feature = ((U[:, 0, :], U[:, 1, :]), (U[:, 2, :], B7[:, :]))

            def by_token(t, first):
                par, win, m = window(t)
                bank = (B34, B56)[par]
                after(pe, ln_norm, first + t - 1)
                for k in range(KT):
                    ins = nc.tensor.transpose(bank[0:m, k // 4, k % 4 * P:(k % 4 + 1) * P], acc[:, k, win], ident)
                ins.then_inc(ln_in, 1)

            pe.wait_ge(used, 3 * (U_FFN - U_BRANCH))
            by_token(0, 0)
            by_token(1, 0)
            for t in range(WINDOWS):
                par, win, m = window(t)
                pe.wait_ge(ln_norm, t + 1)
                after(pe, ln_front, t - 1)
                after(pe, ln_rear, t - 1)
                for k in range(KT):
                    ins = nc.tensor.transpose(by_feature[par][k // 4][:, k % 4 * P:k % 4 * P + m],
                                              xn[par][0:m, k * P:(k + 1) * P], ident[0:m, 0:m])
                ins.then_inc(ln_back, 1)
                if t + 2 < WINDOWS:
                    by_token(t + 2, 0)
            pe.wait_ge(h_low, WINDOWS)
            for n, f0, u0, before in pieces():
                pe.wait_ge(used, before)
                for p, par, i in pairs(pe, 0, n):
                    for j in range(THIRDS):
                        after(pe, f_prod, (p + f0) * 3)
                        pe.wait_ge(w_lo, p * 2 + (u0 + 1))
                        products(U[:, j, 0:TW], 0, j, all_k, (hh, hl)).then_inc(slice_done, 1)
                    for j in range(THIRDS):
                        pe.wait_ge(a_taken, (p + f0) * 3 + (j + 1))
                        pe.wait_ge(w_lo, p * 2 + (u0 + 2))
                        products(U[:, j, 0:TW], 1, j, all_k, (hh, hl)).then_inc(slice_done, 1)
                pe.wait_ge(f_low, f0 + n)
                for f, par, i in pairs(pe, 0, KT):
                    for j in range(THIRDS):
                        from_used(f + (u0 + 2 * n), par, j, f * 3 + (before + j - 2), (xh, xl),
                                  [(k, k) for k in range(n)])
            pe.wait_ge(used, LAST_USED)
            for t in range(WINDOWS):
                by_token(t, WINDOWS)

        @block.scalar
        def _(act):
            act.dma_start(cst[:], I["cst"]).then_inc(consts_in, 16)
            act.dma_start(wba[:], I["wba"]).then_inc(consts_in, 16)
            act.dma_start(sconv[:], I["sconv"]).then_inc(consts_in, 16)
            act.dma_start(bac[:], I["bac"].to_broadcast([P, 2, DN_H])).then_inc(consts_in, 16)
            act.dma_start(bias[:], I["bias"][0]).then_inc(bias_in, 16)

            def high(u, par):
                act.wait_ge(w_in[par], (u - par) * 8 + 16)
                after(act, slice_done, u * 3 - 3)
                nc.scalar.activation(wh[:, par, :], stage[:, par, :], ACT.Copy).then_inc(w_hi, 1)

            def take(u, j, dst):
                act.wait_ge(slice_done, u * 3 + (j + 1))
                nc.scalar.activation(dst, U[:, j, 0:TW], ACT.Copy).then_inc(taken, 1)

            high(0, 0)
            for k in range(KT):
                act.wait_ge(x_in[k // 2], 16)
                nc.scalar.activation(xh[:, k, :], xraw[:, k, :], ACT.Copy).then_inc(x_hi, 1)
            act.wait_ge(x_lo, KT)
            for u, par, _ in bulk(act):
                high(u + 1, 1 - par)
                for j in range(THIRDS):
                    take(u, j, qkv[:, bass.ds(u, 1), third(j)].squeeze(1))
            act.wait_ge(ba_raw, 1)
            act.wait_ge(ba_dve, 1)
            nc.scalar.activation(babuf[:, 2], babuf[:, 0], ACT.Tanh, scale=0.5).then_inc(ba_act, 1)
            nc.scalar.activation(babuf[:, 4], babuf[:, 3], ACT.Exp, scale=-1.0).then_inc(ba_act, 1)
            nc.scalar.activation(bac[:, 0, :], bac[:, 0, :], ACT.Exp).then_inc(ba_act, 1)
            act.wait_ge(ba_dve, 2)
            nc.scalar.activation(babuf[:, 5], babuf[:, 4], ACT.Ln).then_inc(ba_act, 1)
            act.wait_ge(zeroed, 1)
            for b, par, g, n, prev, kind in blocks_of(act):
                u = b + U_BLK
                parts = 2 if prev else 1
                high(u + 1, 1 - par)

                def take_part(j):
                    if kind == "att":
                        take(u, j, qkv[:, bass.ds(u, 1), third(j)].squeeze(1))
                        return
                    if j == 0:
                        act.wait_ge(conv_out, b - BLOCKS)
                    take(u, j, pre[:, par, 3 + j * TW:3 + (j + 1) * TW])

                take_part(0)
                act.wait_ge(v_done, b + 1)
                after(act, pv_done, b)
                nc.scalar.activation(vtok[:, par, :], B7[:, 0:256], ACT.Copy).then_inc(v_taken, 1)
                act.wait_ge(maxed, b + 1)
                after(act, pt_done, b)
                after(act, o_stored[par], stored_before(b, par, g, n))
                for slot in range(HPG):
                    h = (slot % 2) * 2 + slot // 2
                    ins = nc.scalar.activation(pb[:, slot, 0:parts, :], sb[:, slot, 0:parts, :], ACT.Exp,
                                               bias=nmax[:, slot:slot + 1], accum_out=obuf[:, par, h, 64:65])
                ins.then_inc(exped, 1)
                take_part(1)
                act.wait_ge(pt_done, b + 1)
                after(act, pv_done, b)
                if parts == 2:
                    src, dst = B56[:, :, :], pts[:].rearrange("p (a c) k -> p a (c k)", a=2)
                else:
                    src = B56[:].rearrange("p a (c t k) -> p a c t k", t=2, k=P)[:, :, :, 0, :]
                    dst = pts[:].rearrange("p (a c t) k -> p a c t k", a=2, t=2)[:, :, :, 0, :]
                nc.scalar.activation(dst, src, ACT.Copy).then_inc(pt_taken, 1)
                take_part(2)
                if kind != "att":
                    f = b - BLOCKS
                    act.wait_ge(conv_out, f + 1)
                if kind == "dn":
                    act.wait_ge(conv_step, f * CONV_STEPS + CONV_STEPS)
                    nc.scalar.activation(thb[:], cb[:], ACT.Tanh, scale=0.5).then_inc(conv_tanh, 1)
                elif kind == "z":
                    act.wait_ge(taken, u * 3 + 3)
                    nc.scalar.activation(thb[:], pre[:, par, 3:3 + TOK], ACT.Tanh, scale=0.5).then_inc(conv_tanh, 1)


            act.wait_ge(samp_pe, 1)
            act.wait_ge(pv_done, 24)
            for par in (0, 1):
                act.wait_ge(o_stored[par], 16 * (4 + 4 + 8))
            act.wait_ge(kv_stored, 48)
            act.wait_ge(conv_stored, 16 * 16)
            act.wait_ge(tail_stored, 16)
            act.wait_ge(conv_out, 17)
            flat = sq[:].rearrange("b g k e -> b (g k e)")
            nc.scalar.activation(flat[:, 0:1024], B34[0:SAMPLES, :, :], ACT.Copy)
            nc.scalar.activation(flat[:, 1024:2048], B56[0:SAMPLES, :, :], ACT.Copy)
            nc.scalar.activation(flat[:, 2048:2304], B7[0:SAMPLES, 0:256], ACT.Copy).then_inc(samp_act, 1)
            act.wait_ge(samp_act, 1)
            nc.scalar.activation(sq[:, :, 0, :], sq[:, :, 0, :], ACT.Copy, scale=HD ** -0.5).then_inc(samp_act, 1)
            act.wait_ge(samp_pe, 2)
            nc.scalar.activation(qb[:, 0:2, :], B34[:, 0, :], ACT.Copy)
            nc.scalar.activation(qb[:, 2, :], B34[:, 1, 0:256], ACT.Copy).then_inc(samp_act, 1)
            act.wait_ge(samp_pe, 5)
            act.wait_ge(samp_dve, 3)
            act.wait_ge(small_step, SMALL_S)
            nc.scalar.activation(ssc[:], ssc[:], ACT.Exp)
            nc.scalar.activation(self_s[:], self_s[:], ACT.Exp).then_inc(samp_act, 1)
            act.wait_ge(samp_pe, 7)
            osp = B34[:, 1, 0:2 * SAMPLES].rearrange("p (n b) -> p n b", n=2)
            nc.scalar.activation(oh[:, 0:2, SEQ:TOK], osp, ACT.Copy).then_inc(ao_high, 1)

            act.wait_ge(cf_pe, 1)
            act.wait_ge(ao_low, 1)
            nc.scalar.activation(cf[:, 1, :], B7[:, 0:32], ACT.Exp)
            nc.scalar.activation(cf[:, 2, :], B7[:, 32:64], ACT.Exp).then_inc(cf_act, 1)
            act.wait_ge(cf_dve, 1)
            nc.scalar.activation(cf[:, 3, :], cf[:, 3, :], ACT.Exp).then_inc(cf_act, 1)
            nc.scalar.activation(onh[:], cst[:, C_ON:C_ON + 1], ACT.Copy, scale=0.5).then_inc(cf_act, 1)

            def start_unit(u, par):
                high(u + 1, 1 - par)

            def chunk(u, par, j, c):
                if c == 5:
                    act.wait_ge(slice_done, u * 3 + (j + 1))
                    if j == 0:
                        after(act, gate_stored[par], (u - (U_GATE + par)) * 8)
                    nc.scalar.activation(gth[:, par, third(j)], U[:, j, 0:TW], ACT.Tanh, scale=0.5).then_inc(taken, 1)

            def squares(t):
                act.wait_ge(tr1_done, t + 1)
                nc.scalar.activation(sq2[:].rearrange("p (a h) k -> p a (h k)", a=2), B34[:, :, :], ACT.Square,
                                     scale=0.5).then_inc(squared, 1)

            squares(0)
            with act.Fori(0, TILES) as t:
                beside = Beside(t * 2 + U_GATE, chunk, start_unit)
                beside.run(3)
                act.wait_ge(tr2_done, t + 1)
                nc.scalar.activation(kqT[:], B34[:, :, :], ACT.Copy).then_inc(kqT_taken, 1)
                beside.run(2)
                act.wait_ge(tr3_done, t + 1)
                nc.scalar.activation(kbT[:], B56[:, 0, :], ACT.Copy)
                nc.scalar.activation(qdT[:], B7[:, :], ACT.Copy).then_inc(kbqd_taken, 1)
                act.wait_ge(decay_sum, t + 1)
                nc.scalar.activation(ET[:], ET[:], ACT.Exp).then_inc(decay_exp, 1)
                beside.run(3)
                beside.run(4)
                act.wait_ge(x_done, t + 1)
                nc.scalar.activation(X[:], B56[:, 0, :], ACT.Copy).then_inc(x_taken, 1)
                beside.run(1)
                for lv in range(LEVELS):
                    act.wait_ge(y_done, t * LEVELS + (lv + 1))
                    nc.scalar.activation(Y, B56[:, 1, :], ACT.Copy).then_inc(y_taken, 1)
                    beside.run(1)
                    if lv == 0:
                        act.wait_ge(ae_ready, t + 1)
                        nc.scalar.activation(amx[:, 1:4, :], amx[:, 1:4, :], ACT.Exp).then_inc(ae_exp, 1)
                    if lv == 3:
                        act.wait_ge(ao_done, t + 1)
                        nc.scalar.activation(oh[:, 0:2, bass.ds(t * P, P)], B34[:, 1, 0:256].rearrange(
                            "p (n k) -> p n k", n=2), ACT.Copy).then_inc(ao_high, 1)
                    beside.run(1)
                act.wait_ge(wk_done, t + 1)
                nc.scalar.activation(wkT, B34[:, 0, :], ACT.Copy, scale=-1.0).then_inc(wk_taken, 1)
                beside.run(1)
                act.wait_ge(u_done, t + 1)
                nc.scalar.activation(us, B34[:, 1, :], ACT.Copy).then_inc(u_taken, 1)
                beside.run(1)
                act.wait_ge(od_done, t + 1)
                nc.scalar.activation(X[:], B56[:, 0, :], ACT.Square).then_inc(o_squared, 1)
                beside.run(1)
                squares(t + 1)
                beside.run(4)
                act.wait_ge(of_ready, t + 1)
                nc.scalar.activation(oh[:, 2:6, bass.ds(t * P, P)], of[:], ACT.Copy).then_inc(of_high, 1)
                beside.run(CHUNKS)

            nc.scalar.activation(babuf[0:SAMPLES, 6, TILES, :], babuf[0:SAMPLES, 1, TILES, :], ACT.Exp).then_inc(
                ds_act, 1)
            act.wait_ge(ds_in, 32)
            nc.scalar.activation(s64[:, 0, :], sin[:, 0:8, :].rearrange("p h b -> p (h b)"), ACT.Square,
                                 scale=0.5).then_inc(ds_act, 1)
            act.wait_ge(ds_o, 1)
            nc.scalar.activation(s64[:, 0, 0:32], B7[:, 0:32], ACT.Square).then_inc(ds_act, 1)
            act.wait_ge(of_ready, TILES + 1)
            nc.scalar.activation(oh[:, 2:6, SEQ:TOK], sof[:], ACT.Copy).then_inc(of_high, 1)

            def merge_high(f):
                for j in range(THIRDS):
                    act.wait_ge(merged, f * 3 + (j + 1))
                    nc.scalar.activation(xh[:, bass.ds(f, 1), third(j)].squeeze(1), cc[:, third(j)], ACT.Copy,
                                         scale=0.5).then_inc(m_high, 1)

            for f, par, _ in pairs(act, 0, KT):
                high(f + (U_BRANCH + 1), 1 - par)
                merge_high(f)
            for f, par, _ in pairs(act, 0, KT):
                high(f + (U_MIX + 1), 1 - par)

            def normed(t, first):
                par, win, m = window(t)
                act.wait_ge(ln_shift, first + t + 1)
                nc.scalar.activation(xn[par][0:m].rearrange("p (a n) -> p a n", a=2), (B34, B56)[par][0:m],
                                     ACT.Identity, bias=mv[0:m, par, 3:4], scale=mv[0:m, par, 2:3]).then_inc(ln_norm, 1)

            for t in range(WINDOWS + 2):
                if t >= 2:
                    par, win, m = window(t - 2)
                    act.wait_ge(ln_back, t - 1)
                    for k in range(4, KT):
                        ins = nc.scalar.activation(acc[:, k, win], (U[:, 1, :], B7[:, :])[par][
                            :, k % 4 * P:k % 4 * P + m], ACT.Identity, bias=cst[:, C_B1 + k:C_B1 + k + 1],
                            scale=cst[:, C_G1 + k:C_G1 + k + 1])
                    ins.then_inc(ln_rear, 1)
                    act.wait_ge(ln_rear, t - 1)
                    act.wait_ge(ln_front, t - 1)
                    nc.scalar.activation(hh[:, :, win], acc[:, :, win], ACT.Copy).then_inc(h_high, 1)
                if t < WINDOWS:
                    normed(t, 0)
            for n, f0, u0, before in pieces():
                for p, par, i in pairs(act, 0, n):
                    u, F = p * 2 + u0, p + f0
                    high(u + 1, 1)
                    after(act, f_step, F * FFN_STEPS)
                    for j in range(THIRDS):
                        act.wait_ge(slice_done, u * 3 + (j + 1))
                        nc.scalar.activation(ab[:, 2 + j * TW:2 + (j + 1) * TW], U[:, j, 0:TW], ACT.Copy).then_inc(
                            a_taken, 1)
                    high(u + 2, 0)
                    act.wait_ge(f_step, F * FFN_STEPS + FFN_STEPS)
                    after(act, f_prod, F * 3)
                    nc.scalar.activation(gl[:], cc[:], ACT.Gelu_apprx_tanh,
                                         bias=cst[:, bass.ds(F + C_FFB, 1)]).then_inc(f_gelu, 1)
                    for j in range(THIRDS):
                        act.wait_ge(f_prod, F * 3 + (j + 1))
                        nc.scalar.activation(xh[:, bass.ds(p, 1), third(j)].squeeze(1), cc[:, third(j)],
                                             ACT.Copy).then_inc(f_high, 1)
                last = u0 + 2 * n + KT == UNITS
                for f, par, i in pairs(act, 0, KT - 2 * last):
                    high(f + (u0 + 2 * n + 1), 1 - par)
                if last:
                    high(UNITS - 1, 1)
            for t in range(WINDOWS):
                after(act, ln_mul, WINDOWS + t - 1)
                normed(t, WINDOWS)

        @block.vector
        def _(dve):
            nc.vector.memset(pre[:, 0, 0:3], 0.0).then_inc(zeroed, 1)
            nc.vector.memset(pre[:, 1, 0:3], 0.0).then_inc(conv_out, 1)
            nc.vector.memset(babuf[:], 0.0).then_inc(zeroed, 1)
            for k in range(KT):
                dve.wait_ge(x_hi, k + 1)
                nc.vector.tensor_tensor(xl[:, k, :], xraw[:, k, :], xh[:, k, :].bitcast(F32),
                                        ALU.subtract).then_inc(x_lo, 1)
            dve.wait_ge(ba_rows, 1)
            for j in range(THIRDS):
                src = (B34[0:8, 0, 0:TW], B34[0:8, 1, 0:TW], B56[0:8, 0, 0:TW])[j]
                ins = nc.vector.tensor_copy(cb[0:8, third(j)], src)
            ins.then_inc(ba_staged, 1)
            dve.wait_ge(ba_done, 1)
            dve.wait_ge(zeroed, 2)
            ba = B7[:, 0:72].rearrange("p (t c) -> p t c", c=8)
            nc.vector.tensor_copy(babuf[:, 0, 0:TILES, :], ba[:, 0:TILES, 0:4])
            nc.vector.tensor_copy(babuf[0:SAMPLES, 0, TILES, :], ba[0:SAMPLES, TILES, 0:4])
            nc.vector.tensor_copy(babuf[:, 1, 0:TILES, :], ba[:, 0:TILES, 4:8])
            nc.vector.tensor_copy(babuf[0:SAMPLES, 1, TILES, :], ba[0:SAMPLES, TILES, 4:8]).then_inc(ba_raw, 1)
            st = Steps(dve, small_step)
            dve.wait_ge(ba_raw, 1)
            dve.wait_ge(consts_in, 16 * N_CONSTS)
            st.link(nc.vector.tensor_tensor(babuf[:, 1], babuf[:, 1], bac[:, 1, :].unsqueeze(1).to_broadcast(
                [P, 9, DN_H]), ALU.add))
            nc.vector.scalar_tensor_tensor(babuf[:, 3], babuf[:, 1], -1.0, babuf[:, 1], ALU.mult, ALU.max).then_inc(
                ba_dve, 1)
            dve.wait_ge(ba_act, 3)
            nc.vector.tensor_scalar(babuf[:, 4], babuf[:, 4], 1.0, None, ALU.add).then_inc(ba_dve, 1)
            st.link(nc.vector.tensor_scalar(babuf[:, 0], babuf[:, 2], 0.5, 0.5, ALU.mult, ALU.add))
            dve.wait_ge(ba_dve, 1)
            st.link(nc.vector.tensor_scalar(babuf[:, 1], babuf[:, 1], 0.0, None, ALU.max))
            dve.wait_ge(ba_act, 4)
            st.link(nc.vector.tensor_tensor(babuf[:, 1], babuf[:, 1], babuf[:, 5], ALU.add))
            st.link(nc.vector.scalar_tensor_tensor(babuf[:, 1], babuf[:, 1], -1.0, bac[:, 0, :].unsqueeze(1)
                                                   .to_broadcast([P, 9, DN_H]), ALU.mult, ALU.mult))
            cv = Steps(dve, conv_step)
            for b, par, g, n, prev, kind in blocks_of(dve):
                parts = 2 if prev else 1
                u = b + U_BLK
                dve.wait_ge(taken, 3 * 6 if g == 0 else ALL_QKV)
                after(dve, s_done, b)
                t = GT[g]
                for dst, tile, scale in ((q_st[:], 0, HD ** -0.5), (k_st[:, par], 2, 1.0)):
                    ins = nc.vector.tensor_scalar(packed(dst, g), cols(qkv[:, t + tile:t + tile + 2, 0:SEQ], g, n),
                                                  scale, None, ALU.mult)
                ins.then_inc(qk_staged, 1)
                after(dve, v_done, b)
                nc.vector.tensor_scalar(packed(v_st[:], g), cols(qkv[:, t + 4:t + 6, 0:SEQ], g, n),
                                        1.0, None, ALU.mult).then_inc(v_staged, 1)
                dve.wait_ge(s_done, b + 1)
                after(dve, exped, b)
                dve.wait_ge(bias_in, 16 * (g + 1))
                s_all = B34[:].rearrange("p a (j t k) -> p (a j) t k", j=2, t=2)
                nc.vector.tensor_tensor(sb[:, :, 0:parts, :], s_all[:, :, 0:parts, :], bias[:, :, 0:parts, :],
                                        ALU.add).then_inc(biased, 1)
                dve.wait_ge(biased, b + 1)
                after(dve, o_taken, b)
                nc.vector.tensor_reduce(nmax[:], sb[:, :, 0:parts, :], AX.XY, ALU.max, negate=True).then_inc(maxed, 1)
                if kind == "dn":
                    f = b - BLOCKS
                    cv.item(f, CONV_STEPS)
                    dnw = [cst[:, bass.ds(f * 4 + (C_DNW + i), 1)] for i in range(4)]
                    after(dve, conv_stored, f * 16)
                    for j in range(THIRDS):
                        dve.wait_ge(taken, u * 3 + (j + 1))
                        a, w = j * TW, (TW if j < 2 else SEQ - 2 * TW)
                        cv.link(nc.vector.tensor_scalar(cb[:, a:a + w], pre[:, par, a + 3:a + 3 + w], dnw[3], None,
                                                        ALU.mult))
                        for i in (2, 1, 0):
                            cv.link(nc.vector.scalar_tensor_tensor(cb[:, a:a + w], pre[:, par, a + i:a + i + w],
                                                                   dnw[i], cb[:, a:a + w], ALU.mult, ALU.add))
                    cv.link(nc.vector.tensor_scalar(cb[:, SEQ:TOK], pre[:, par, SEQ + 3:TOK + 3], dnw[3], None,
                                                    ALU.mult))
                    for i in (2, 1, 0):
                        cv.link(nc.vector.scalar_tensor_tensor(
                            cb[:, SEQ:TOK], sconv[:, bass.ds(f, 1), :, i].squeeze(1), dnw[i], cb[:, SEQ:TOK],
                            ALU.mult, ALU.add))
                    nc.vector.tensor_scalar(tails[:, bass.ds(f, 1), :].squeeze(1), pre[:, par, SEQ:SEQ + 11], 1.0, None,
                                            ALU.mult)
                dve.wait_ge(pv_done, b + 1)
                dve.wait_ge(maxed, b + 1)
                after(dve, o_stored[par], stored_before(b, par, g, n))
                nc.vector.tensor_scalar(obuf[:, par, :, 65].rearrange("p (j a) -> p a j", a=2),
                                        nmax[:].rearrange("p (a j) -> p a j", a=2), -1.0, None, ALU.mult)
                nc.vector.tensor_scalar(obuf[:, par, :, 0:64], B7[:, 256:512].rearrange("p (h e) -> p h e", e=64),
                                        1.0, None, ALU.mult).then_inc(o_taken, 1)
                if kind != "att":
                    dve.wait_ge(conv_tanh, b - (BLOCKS - 1))
                    if kind == "z":
                        dve.wait_ge(conv_stored, (b - BLOCKS) * 16)
                    src = cb[:] if kind == "dn" else pre[:, par, 3:3 + TOK]
                    nc.vector.scalar_tensor_tensor(cb[:], thb[:], 1.0, src, ALU.add, ALU.mult).then_inc(conv_out, 1)


            def mark(ins):
                ins.then_inc(samp_dve, 1)

            def wide(ap, n):
                return ap.unsqueeze(3).to_broadcast([*ap.shape, n])

            st.n = SMALL_0
            dve.wait_ge(samp_act, 3)
            st.link(nc.vector.tensor_tensor(self_p[:], sq[:, :, 0, :], sq[:, :, 1, :], ALU.mult))
            st.link(nc.vector.tensor_reduce(self_s[:], self_p[:].rearrange("b g (h e) -> b g h e", e=HD), AX.X, ALU.add))
            dve.wait_ge(samp_in, 16 * 5)
            k0 = 0
            for n, g in enumerate((0, 2, 1)):
                m = SKEYS[g]
                pr = prod[:, 0:m].rearrange("p j h e -> p j (h e)")
                st.link(nc.vector.tensor_tensor(pr, kvc[:, k0:k0 + m, 0, :], qb[:, n, :].unsqueeze(1).to_broadcast(
                    [P, m, 256]), ALU.mult))
                st.link(nc.vector.tensor_reduce(ssc[:, k0:k0 + m, :], prod[:, 0:m], AX.X, ALU.add))
                k0 += m
            st.link(nc.vector.tensor_tensor(ssc[:], ssc[:], sbias[:], ALU.add))
            nc.vector.tensor_reduce(sm[0:SAMPLES, 1, :], self_s[:].rearrange("b g h -> b h g"), AX.X, ALU.max)
            mark(nc.vector.tensor_reduce(sm[:, 0, :], ssc[:].rearrange("p k h -> p h k"), AX.X, ALU.max))
            dve.wait_ge(samp_pe, 3)
            m48 = sm[0:4, 2:4, :].rearrange("p a c -> p (a c)")
            n48 = sm[0:4, 4:6, :].rearrange("p a c -> p (a c)")
            st.link(nc.vector.tensor_reduce(m48, B7[0:4, 0:P].rearrange("p (b c) -> p b c", c=16), AX.X, ALU.max))
            mark(nc.vector.tensor_tensor(n48, B7[0:4, P:P + SAMPLES], m48, ALU.max))
            dve.wait_ge(samp_pe, 4)
            mark(nc.vector.tensor_copy(sm[0:SAMPLES, 6, :], B34[0:SAMPLES, 0, 0:4]))
            dve.wait_ge(samp_pe, 5)
            dve.wait_ge(samp_dve, 3)
            st.link(nc.vector.tensor_copy(sm[:, 8, :], B56[:, 0, 0:4]))
            st.link(nc.vector.tensor_tensor(ssc[:], ssc[:], sm[:, 8, :].unsqueeze(1).to_broadcast([P, SK, 4]),
                                            ALU.subtract))
            st.link(nc.vector.tensor_tensor(self_s[:], self_s[:], sm[0:SAMPLES, 6, :].unsqueeze(1).to_broadcast(
                [SAMPLES, 3, 4]), ALU.subtract))
            assert st.n == SMALL_S
            dve.wait_ge(samp_act, 4)
            st.link(nc.vector.tensor_reduce(sm[:, 7, :], ssc[:].rearrange("p k h -> p h k"), AX.X, ALU.add))
            k0 = 0
            for n, g in enumerate((0, 2, 1)):
                m = SKEYS[g]
                st.link(nc.vector.tensor_tensor(prod[:, 0:m], kvc[:, k0:k0 + m, 1, :].rearrange(
                    "p j (h e) -> p j h e", e=HD), wide(ssc[:, k0:k0 + m, :], HD), ALU.mult))
                st.link(nc.vector.tensor_reduce(og[:, n, :], prod[:, 0:m].rearrange("p j h e -> p (h e) j"), AX.X,
                                                ALU.add))
                k0 += m
            mark(nc.vector.tensor_tensor(self_p[:].rearrange("b g (h e) -> b g h e", e=HD),
                                         sq[:, :, 2, :].rearrange("b g (h e) -> b g h e", e=HD),
                                         wide(self_s[:], HD), ALU.mult))
            dve.wait_ge(samp_pe, 6)
            st.link(nc.vector.reciprocal(sm[0:SAMPLES, 9, :], B7[0:SAMPLES, 256:260]))
            mark(nc.vector.tensor_tensor(o8[:].rearrange("b (h e) -> b h e", e=HD),
                                         B7[0:SAMPLES, 0:256].rearrange("b (h e) -> b h e", e=HD),
                                         sm[0:SAMPLES, 9, :].unsqueeze(2).to_broadcast([SAMPLES, 4, HD]), ALU.mult))
            dve.wait_ge(ao_high, 1)
            nc.vector.tensor_tensor(ol[:, 0:2, SEQ:TOK], B34[:, 1, 0:2 * SAMPLES].rearrange("p (n b) -> p n b", n=2),
                                    oh[:, 0:2, SEQ:TOK].bitcast(F32), ALU.subtract).then_inc(ao_low, 1)

            dve.wait_ge(ao_low, 1)
            dve.wait_ge(cf_act, 1)
            st.link(nc.vector.tensor_copy(cf[:, 0, :], B7[:, 0:32]))
            nc.vector.tensor_tensor(cf[:, 3, :], B7[:, 32:64], cf[:, 0, :], ALU.subtract).then_inc(cf_dve, 1)
            nc.vector.memset(S[:], 0.0).then_inc(s_ready, 1)
            dve.wait_ge(cf_act, 3)
            dve.wait_ge(dcst_in, 16)
            dn = Steps(dve, dn_step)
            heads4 = lambda ap: ap.rearrange("p (h k) -> p h k", h=DN_H)
            per_head = lambda ap: ap.unsqueeze(2).to_broadcast([P, DN_H, P])
            same = lambda ap: ap.unsqueeze(1).to_broadcast([P, DN_H, P])
            q4, k4, v4, G4 = (heads4(x) for x in (B34[:, 0, :], B34[:, 1, :], B56[:, 0, :], B56[:, 1, :]))

            def stage_g(t):
                nc.vector.tensor_scalar(gB, per_head(babuf[:, 1, bass.ds(t, 1), :].squeeze(1)), 1.0, None,
                                        ALU.mult).then_inc(g_staged, 1)

            def norm_sums(t, steps):
                dve.wait_ge(squared, t + 1)
                steps.link(nc.vector.tensor_reduce(rn[:, 0, :], sq2[:], AX.X, ALU.add))
                nc.vector.tensor_scalar(rn[:, 1, :], rn[:, 0, :], RMS_EPS, None, ALU.add).then_inc(ss_ready, 1)

            def normed(t, steps):
                dve.wait_ge(rs_ready, t * 2 + 1)
                nc.vector.tensor_scalar(rn[:, 2, 0:4], rn[:, 1, 0:4], 0.5 * DN_D ** -0.5, None, ALU.mult)
                steps.link(nc.vector.tensor_scalar(rn[:, 2, 4:8], rn[:, 1, 4:8], 0.5, None, ALU.mult))
                nc.vector.tensor_tensor(qn[:], q4, per_head(rn[:, 2, 0:4]), ALU.mult)
                nc.vector.tensor_tensor(kn[:], k4, per_head(rn[:, 2, 4:8]), ALU.mult).then_inc(qkn_ready, 1)

            stage_g(0)
            norm_sums(0, st)
            normed(0, st)
            with dve.Fori(0, TILES) as t:
                dn.item(t, DN_STEPS)
                th = bass.ds(t * DN_H, DN_H)
                gc, eg, egt, ekd = (cf[:, n, th] for n in range(4))
                beta = babuf[:, 0, bass.ds(t, 1), :].squeeze(1)
                dve.wait_ge(qkn_ready, t + 1)
                dn.link(nc.vector.tensor_tensor(kb[:], kn[:], per_head(beta), ALU.mult))
                nc.vector.tensor_tensor(qd[:], qn[:], per_head(eg), ALU.mult).then_inc(kbqd_ready, 1)
                dve.wait_ge(tv_done, t + 1)
                nc.vector.scalar_tensor_tensor(vb[:], v4, 0.5, per_head(beta), ALU.mult, ALU.mult).then_inc(v_ready, 1)
                dve.wait_ge(g_done, t + 1)
                nc.vector.tensor_tensor(ET[:], G4, same(dcst[:, D_NEG:D_NEG + P]), ALU.add).then_inc(g_read, 1)
                dve.wait_ge(g_read, t + 1)
                nc.vector.tensor_tensor(ET[:], ET[:], per_head(gc), ALU.subtract).then_inc(decay_sum, 1)
                nc.vector.tensor_tensor(kbe[:], kb[:], per_head(eg), ALU.mult)
                dve.wait_ge(decay_exp, t + 1)
                dn.link(nc.vector.tensor_tensor(ETs[:], ET[:], same(dcst[:, D_STR:D_STR + P]), ALU.mult))
                dve.wait_ge(la_done, t + 1)
                lev = lambda n: same(dcst[:, D_LEV + n * P:D_LEV + (n + 1) * P])
                dn.link(nc.vector.tensor_tensor(heads4(LTm[:]), q4, ETs[:], ALU.mult))
                dn.link(nc.vector.tensor_tensor(heads4(XT[:]), heads4(LTm[:]), lev(0), ALU.mult))
                nc.vector.tensor_tensor(heads4(XT[:]), heads4(XT[:]), same(ident), ALU.add).then_inc(xt_ready, 1)
                nc.vector.tensor_tensor(heads4(Lb[:, 1]), heads4(LTm[:]), lev(1), ALU.mult).then_inc(lb_ready, 1)
                dn.link(nc.vector.tensor_tensor(heads4(ATm[:]), k4, ET[:], ALU.mult))
                nc.vector.tensor_tensor(kd[:], kn[:], per_head(ekd), ALU.mult)
                for lv in range(LEVELS):
                    if lv + 2 < LEVELS + 1:
                        after(dve, y_done, t * LEVELS + lv)
                        dn.link(nc.vector.tensor_tensor(heads4(Lb[:, lv % 2]), heads4(LTm[:]), lev(lv + 2), ALU.mult))
                    if lv == 0:
                        dve.wait_ge(att_in, t * 16 + 16)
                        dve.wait_ge(ao_low, t + 1)
                        dn.link(nc.vector.tensor_tensor(amx[:, 0, :], abuf[:, 0, :, 65], abuf[:, 1, :, 65], ALU.max))
                        dn.link(nc.vector.tensor_tensor(amx[:, 0, :], amx[:, 0, :], abuf[:, 2, :, 65], ALU.max))
                        nc.vector.tensor_tensor(amx[:, 1:4, :], abuf[:, :, :, 65], amx[:, 0, :].unsqueeze(1)
                                                .to_broadcast([P, 3, 4]), ALU.subtract).then_inc(ae_ready, 1)
                    if lv < LEVELS - 1:
                        dve.wait_ge(z_done, t * (LEVELS - 1) + (lv + 1))
                        nc.vector.tensor_tensor(X[:], X[:], B56[:, 0, :], ALU.add).then_inc(x_added, 1)
                    dve.wait_ge(zt_done, t * LEVELS + (lv + 1))
                    nc.vector.tensor_tensor(XT[:], XT[:], B7[:, :], ALU.add).then_inc(xt_ready, 1)
                    if lv == 1:
                        dve.wait_ge(ae_exp, t + 1)
                        w3 = amx[:, 1:4, :].unsqueeze(3).to_broadcast([P, 3, 4, 65])
                        dn.link(nc.vector.tensor_tensor(abuf[:, :, :, 0:65], abuf[:, :, :, 0:65], w3, ALU.mult))
                        dn.link(nc.vector.tensor_tensor(abuf[:, 0, :, 0:65], abuf[:, 0, :, 0:65], abuf[:, 1, :, 0:65],
                                                        ALU.add))
                    if lv == 2:
                        dn.link(nc.vector.tensor_tensor(abuf[:, 0, :, 0:65], abuf[:, 0, :, 0:65], abuf[:, 2, :, 0:65],
                                                        ALU.add))
                        dn.link(nc.vector.reciprocal(amx[:, 4, :], abuf[:, 0, :, 64]))
                        nc.vector.tensor_tensor(ao[:], abuf[:, 0, :, 0:64], amx[:, 4, :].unsqueeze(2).to_broadcast(
                            [P, 4, 64]), ALU.mult).then_inc(ao_ready, 1)
                    if lv == 4:
                        dve.wait_ge(ao_high, t + 2)
                        nc.vector.tensor_tensor(ol[:, 0:2, bass.ds(t * P, P)], B34[:, 1, 0:256].rearrange(
                            "p (n k) -> p n k", n=2), oh[:, 0:2, bass.ds(t * P, P)].bitcast(F32),
                            ALU.subtract).then_inc(ao_low, 1)
                dve.wait_ge(od_done, t + 1)
                dve.wait_ge(s_ready, t + 1)
                dn.link(nc.vector.tensor_tensor(heads4(S[:]), heads4(S[:]), per_head(egt), ALU.mult))
                nc.vector.tensor_tensor(S[:], S[:], B56[:, 1, :], ALU.add).then_inc(s_ready, 1)
                dve.wait_ge(o_squared, t + 1)
                dn.link(nc.vector.tensor_reduce(rn[:, 3, 0:4], heads4(X[:]), AX.X, ALU.add))
                nc.vector.tensor_scalar(rn[:, 3, 4:8], rn[:, 3, 0:4], 1.0 / DN_D, RMS_EPS, ALU.mult, ALU.add).then_inc(
                    ss_ready, 1)
                norm_sums(t + 1, dn)
                stage_g(t + 1)
                dve.wait_ge(rs_ready, t * 2 + 2)
                nc.vector.tensor_tensor(of[:], v4, per_head(rn[:, 3, 4:8]), ALU.mult).then_inc(on_ready, 1)
                normed(t + 1, dn)
                dve.wait_ge(on_done, t + 1)
                dve.wait_ge(z_in, t * 16 + 16)
                nc.vector.scalar_tensor_tensor(of[:], heads4(B7[:, :]), onh[:], zin[:], ALU.mult, ALU.mult).then_inc(
                    of_ready, 1)
                dve.wait_ge(of_high, t + 1)
                nc.vector.tensor_tensor(ol[:, 2:6, bass.ds(t * P, P)], of[:], oh[:, 2:6, bass.ds(t * P, P)].bitcast(F32),
                                        ALU.subtract).then_inc(of_low, 1)
                assert dn.n == DN_STEPS, dn.n

            dve.wait_ge(of_low, TILES)
            dve.wait_ge(ds_in, 32)
            dve.wait_ge(ds_act, 2)
            by_b = lambda ap: ap.unsqueeze(1).to_broadcast([SAMPLES, SAMPLES, DN_H])
            eye8 = ident[0:SAMPLES, 0:SAMPLES].unsqueeze(2).to_broadcast([SAMPLES, SAMPLES, DN_H])
            nc.vector.tensor_tensor(sdiag[:, 0], eye8, by_b(babuf[0:SAMPLES, 0, TILES, :]), ALU.mult)
            nc.vector.tensor_tensor(sdiag[:, 1], eye8, by_b(babuf[0:SAMPLES, 6, TILES, :]), ALU.mult).then_inc(ds_dve, 1)
            dve.wait_ge(ds_pe, 2)
            nc.vector.tensor_scalar(s64[0:64, 1, 0:1], B34[0:64, 1, 0:1], RMS_EPS, None, ALU.add).then_inc(ss_ready, 1)
            st.link(nc.vector.tensor_scalar(s64[:, 3, :].rearrange("p (x h b) -> p x b h", x=2, h=DN_H),
                                            B34[:, 0, 0:64].rearrange("p (x b h) -> p x b h", x=2, h=DN_H), 1.0, None,
                                            ALU.mult))
            dve.wait_ge(ds_pe, 3)
            qk = sin[:, 0:8, :].rearrange("p h b -> p (h b)")
            st.link(nc.vector.scalar_tensor_tensor(s64[:, 2, :], qk, 0.5, B34[:, 1, 64:128], ALU.mult, ALU.mult))
            nc.vector.tensor_scalar(s64[:, 4, 0:32], s64[:, 2, 32:64], -1.0, None, ALU.mult)
            nc.vector.tensor_tensor(s64[:, 4, 32:64], s64[:, 2, 32:64], s64[:, 3, 0:32], ALU.mult)
            nc.vector.tensor_scalar(s64[:, 5, 0:32], sin[:, 8:12, :].rearrange("p h b -> p (h b)"), 0.5, None, ALU.mult)
            nc.vector.tensor_scalar(s64[:, 2, 0:32], s64[:, 2, 0:32], DN_D ** -0.5, None, ALU.mult).then_inc(ds_dve, 1)
            dve.wait_ge(ds_dve, 2)
            across = lambda ap: ap.unsqueeze(2).to_broadcast([P, 4, P])

            def group_of(n):
                h, b0 = n // 2, n % 2 * 4
                col = h * SAMPLES + b0
                return sS[:, h, b0:b0 + 4, :], lambda part, base: across(s64[:, part, base + col:base + col + 4])

            def decayed(n):
                state, by = group_of(n)
                st.link(nc.vector.tensor_tensor(state, state, by(3, 32), ALU.mult))
                nc.vector.tensor_tensor(sdv[:, n % 2], same(ident), by(5, 0), ALU.mult).then_inc(ds_scaled, 1)

            decayed(0)
            for n in range(8):
                if n < 7:
                    decayed(n + 1)
                state, by = group_of(n)
                dve.wait_ge(ds_prod, n + 1)
                st.link(nc.vector.tensor_tensor(sdv[:, n % 2], heads4(B56[:, n % 2, :]), by(4, 32), ALU.mult))
                nc.vector.tensor_tensor(state, state, sdv[:, n % 2], ALU.add).then_inc(ds_new, 1)
                dve.wait_ge(ds_new, n + 1)
            dve.wait_ge(ds_pe, 4)
            nc.vector.tensor_scalar(s64[0:32, 1, 1:2], B34[0:32, 1, 0:1], 1.0 / DN_D, RMS_EPS, ALU.mult, ALU.add).then_inc(
                ss_ready, 1)
            dve.wait_ge(ds_pe, 5)
            st.link(nc.vector.tensor_copy(s64[:, 5, 32:64], B34[:, 1, 64:96]))
            hb = lambda ap: ap.rearrange("p (h b) -> p h b", h=DN_H)
            st.link(nc.vector.tensor_tensor(sof[:], hb(B7[:, 0:32]), hb(s64[:, 5, 32:64]), ALU.mult))
            nc.vector.scalar_tensor_tensor(sof[:], sof[:], onh[:], sin[:, 12:16, :], ALU.mult, ALU.mult).then_inc(
                of_ready, 1)
            dve.wait_ge(of_high, TILES + 1)
            nc.vector.tensor_tensor(ol[:, 2:6, SEQ:TOK], sof[:], oh[:, 2:6, SEQ:TOK].bitcast(F32),
                                    ALU.subtract).then_inc(of_low, 1)

            dbank = (B34[:, 0, :], B34[:, 1, :], B56[:, 0, :])
            dve.wait_ge(fstate_in, 16)
            dve.wait_ge(of_low, TILES + 1)
            for f, par, i in pairs(dve, 0, KT):
                dve.wait_ge(gates_in[par], (f - par) * 8 + 16)
                after(dve, m_low, f * 3)
                for j in range(THIRDS):
                    dve.wait_ge(slice_done, (f + U_BRANCH) * 3 + (j + 1))
                    nc.vector.scalar_tensor_tensor(cc[:, third(j)], gates[:, par, 0, third(j)], 1.0,
                                                   U[:, j, 0:TW], ALU.add, ALU.mult)
                    dve.wait_ge(merged, f * 3 + j)
                    nc.vector.scalar_tensor_tensor(mt, gates[:, par, 1, third(j)], 1.0,
                                                   dbank[j][:, 0:TW], ALU.add, ALU.mult).then_inc(used, 1)
                    dve.wait_ge(used, f * 3 + (j + 1))
                    nc.vector.tensor_tensor(cc[:, third(j)], cc[:, third(j)], mt, ALU.add).then_inc(merged, 1)
                for j in range(THIRDS):
                    dve.wait_ge(m_high, f * 3 + (j + 1))
                    x = (slice(None), bass.ds(f, 1), third(j))
                    nc.vector.scalar_tensor_tensor(xl[x].squeeze(1), cc[:, third(j)], 0.5, xh[x].squeeze(1).bitcast(F32),
                                                   ALU.mult, ALU.subtract).then_inc(m_low, 1)
            dve.wait_ge(acc_in, 16)
            for f, par, i in pairs(dve, 0, KT):
                for j in range(THIRDS):
                    dve.wait_ge(slice_done, (f + U_MIX) * 3 + (j + 1))
                    a = acc[:, bass.ds(f, 1), third(j)].squeeze(1)
                    nc.vector.scalar_tensor_tensor(a, a, ALPHA, U[:, j, 0:TW], ALU.mult, ALU.add).then_inc(used, 1)
            nc.vector.memset(ab[:, 0:2], 0.0).then_inc(f_zero, 1)

            def moments(t, first):
                par, win, m = window(t)
                n = first + t
                dve.wait_ge(ln_in, n + 1)
                after(dve, ln_norm, n - 1)
                for a in range(2):
                    ins = nc.vector.bn_stats(stats[0:m, par, a, :], (B34, B56)[par][0:m, a, :])
                ins.then_inc(ln_step, 1)
                dve.wait_ge(ln_step, 2 * n + 1)
                nc.vector.bn_aggr(mv[0:m, par, 0:2], stats[0:m, par].rearrange("p a s -> p (a s)")).then_inc(ln_step, 1)
                dve.wait_ge(ln_step, 2 * n + 2)
                nc.vector.tensor_scalar(mv[0:m, par, 1:2], mv[0:m, par, 1:2], LN_EPS, None, ALU.add).then_inc(ln_var, 1)

            def shift(t, first):
                par, win, m = window(t)
                dve.wait_ge(ln_root, first + t + 1)
                nc.vector.scalar_tensor_tensor(mv[0:m, par, 3:4], mv[0:m, par, 0:1], -1.0, mv[0:m, par, 2:3], ALU.mult,
                                               ALU.mult).then_inc(ln_shift, 1)

            for t in range(WINDOWS + 2):
                if t < WINDOWS:
                    moments(t, 0)
                if t >= 2:
                    par, win, m = window(t - 2)
                    row = lambda c: cst[:, c:c + 4].unsqueeze(2).to_broadcast([P, 4, m])
                    src = U[:, 2 * par, :].rearrange("p (k t) -> p k t", k=4)[:, :, 0:m]
                    dve.wait_ge(ln_back, t - 1)
                    nc.vector.tensor_tensor(acc[:, 0:4, win], src, row(C_G1), ALU.mult).then_inc(ln_mul, 1)
                    dve.wait_ge(ln_mul, t - 1)
                    nc.vector.tensor_tensor(acc[:, 0:4, win], acc[:, 0:4, win], row(C_B1), ALU.add).then_inc(
                        ln_front, 1)
                if t < WINDOWS:
                    shift(t, 0)
            fs = Steps(dve, f_step)
            dve.wait_ge(f_zero, 1)
            for n, f0, u0, before in pieces():
                for p, par, i in pairs(dve, 0, n):
                    u, F = p * 2 + u0, p + f0
                    fs.item(F, FFN_STEPS)
                    w3 = [cst[:, bass.ds(F * 3 + (C_FFW + k), 1)] for k in range(3)]
                    after(dve, f_low, F)
                    for j in range(THIRDS):
                        dve.wait_ge(a_taken, F * 3 + (j + 1))
                        a, w = j * TW, (TW if j < 2 else SEQ - 2 * TW)
                        fs.link(nc.vector.tensor_scalar(cc[:, a:a + w], ab[:, a + 2:a + 2 + w], w3[2], None, ALU.mult))
                        for k in (1, 0):
                            fs.link(nc.vector.scalar_tensor_tensor(cc[:, a:a + w], ab[:, a + k:a + k + w], w3[k],
                                                                   cc[:, a:a + w], ALU.mult, ALU.add))
                    fs.link(nc.vector.tensor_scalar(cc[:, SEQ:TOK], ab[:, SEQ + 2:TOK + 2], w3[2], None, ALU.mult))
                    fs.link(nc.vector.scalar_tensor_tensor(cc[:, SEQ:TOK], fstate[:, bass.ds(F, 1), :, 1].squeeze(1),
                                                           w3[1], cc[:, SEQ:TOK], ALU.mult, ALU.add))
                    nc.vector.tensor_scalar(ftails[:, bass.ds(F, 1), :].squeeze(1), ab[:, SEQ:SEQ + 10], 1.0, None,
                                            ALU.mult)
                    fs.link(nc.vector.scalar_tensor_tensor(cc[:, SEQ:TOK], fstate[:, bass.ds(F, 1), :, 0].squeeze(1),
                                                           w3[0], cc[:, SEQ:TOK], ALU.mult, ALU.add))
                    dve.wait_ge(f_gelu, F + 1)
                    for j in range(THIRDS):
                        dve.wait_ge(slice_done, u * 3 + (3 + j + 1))
                        nc.vector.tensor_tensor(cc[:, third(j)], gl[:, third(j)], U[:, j, 0:TW],
                                                ALU.mult).then_inc(f_prod, 1)
                    dve.wait_ge(f_high, F * 3 + 3)
                    x = (slice(None), bass.ds(p, 1), slice(None))
                    nc.vector.tensor_tensor(xl[x].squeeze(1), cc[:], xh[x].squeeze(1).bitcast(F32),
                                            ALU.subtract).then_inc(f_low, 1)
                for f, par, i in pairs(dve, 0, KT):
                    for j in range(THIRDS):
                        dve.wait_ge(slice_done, (f + (u0 + 2 * n)) * 3 + (j + 1))
                        a = acc[:, bass.ds(f, 1), third(j)].squeeze(1)
                        nc.vector.scalar_tensor_tensor(a, a, ALPHA if f0 == 0 else 1.0, U[:, j, 0:TW], ALU.mult,
                                                       ALU.add).then_inc(used, 1)
                dve.wait_ge(used, before + 3 * KT)
            dve.wait_ge(rows2_in, 32)
            for t in range(WINDOWS + 1):
                if t < WINDOWS:
                    moments(t, WINDOWS)
                if t >= 1:
                    par, win, m = window(t - 1)
                    dve.wait_ge(ln_norm, WINDOWS + t)
                    after(dve, y_stored[par], (t - 1) // 2 * 16)
                    nc.vector.tensor_tensor(yt[0:m, par, :], xn[par][0:m], g2r[0:m], ALU.mult).then_inc(ln_mul, 1)
                    dve.wait_ge(ln_mul, WINDOWS + t)
                    nc.vector.tensor_tensor(yt[0:m, par, 0:512], yt[0:m, par, 0:512], b2r[0:m, 0:512], ALU.add).then_inc(
                        y_ready, 1)
                if t < WINDOWS:
                    shift(t, WINDOWS)


def layout(x):
    f = np.float32
    g = lambda n: np.asarray(x[n])
    out = {}
    xs = np.concatenate([g("x_prompt")[0], g("x_sample")[:, 0]], 0)
    out["xT"] = np.ascontiguousarray(xs.T.reshape(KT, P, TOK).transpose(1, 0, 2))
    win, wup, wo, wdn = g("w_in")[0], g("w_up")[0], g("w_o")[0], g("w_down")[0]
    wad = np.concatenate([g("w_att_out")[0], g("w_dn_out")[0]], 0)
    wu = np.zeros((UNITS, P, KT, P), f)
    n = 0

    def put(w, k0, ks, c0):
        nonlocal n
        wu[n, :, 0:ks] = w[k0 * P:(k0 + ks) * P, c0:c0 + P].reshape(ks, P, P).transpose(1, 0, 2)
        n += 1

    for grp, kinds in ((0, (0, 1, 2)), (2, (0, 1, 2)), (1, (0, 1, 2))):
        for kind in kinds:
            for j in range(2):
                put(win, 0, KT, kind * ATT_W + grp * 256 + j * P)
    for i in range(12):
        put(win, 0, KT, OFF_DN + i * P)
    for i in range(DN_H):
        put(win, 0, KT, OFF_Z + i * P)
    for i in range(KT):
        put(win, 0, KT, OFF_GATE + i * P)
        put(win, 0, KT, OFF_GATE + D_MODEL + i * P)
    for i in range(KT):
        put(wad, 0, 6, i * P)
    for i in range(KT):
        put(wo, 0, KT, i * P)
    f0 = 0
    for m in PIECES:
        for i in range(m):
            put(wup, 0, KT, (f0 + i) * P)
            put(wup, 0, KT, D_FF + (f0 + i) * P)
        for i in range(KT):
            put(wdn, f0, m, i * P)
        f0 += m
    assert n == UNITS and f0 == FT
    out["wu"] = wu.reshape(UNITS, P, KT * P)
    out["wba"] = np.ascontiguousarray(win[:, OFF_BA:OFF_GATE].reshape(KT, P, 8).transpose(1, 0, 2))
    out["bac"] = np.stack([g("dn_a_log")[0], g("dn_dt_bias")[0]])[None]
    cst = np.zeros((P, C_END), f)
    cst[:, C_ID:C_DNW] = np.eye(P, dtype=f)
    cst[:, C_DNW:C_FFW] = g("w_dn_conv")[0].reshape(4, 12, P).transpose(2, 1, 0).reshape(P, 48)
    cst[:, C_FFW:C_FFB] = g("w_ffn_conv")[0].reshape(3, FT, P).transpose(2, 1, 0).reshape(P, 3 * FT)
    cst[:, C_FFB:C_G1] = g("b_ffn_conv")[0].reshape(FT, P).T
    cst[:, C_G1:C_B1] = g("ln1_g")[0].reshape(KT, P).T
    cst[:, C_B1:C_ON] = g("ln1_b")[0].reshape(KT, P).T
    cst[:, C_ON:C_R] = g("dn_onorm_w")[0][:, None]
    cst[0:SAMPLES, C_R:C_END] = (np.arange(P)[None] // 16 == np.arange(SAMPLES)[:, None]).astype(f)
    out["cst"] = cst
    out["sconv"] = np.ascontiguousarray(g("state_dn_conv")[0].reshape(SAMPLES, 3, 12, P).transpose(3, 2, 0, 1))
    slopes = np.exp2(np.float32(-8.0) * np.arange(1, 13, dtype=f) / np.float32(12)).astype(f).reshape(3, 4)
    q, k = np.arange(P)[:, None], np.arange(P)[None]
    bias = np.full((3, P, 4, 2, P), NEG, f)
    for grp, (win_, d) in enumerate(DIL):
        for slot in range(4):
            h = (slot % 2) * 2 + slot // 2
            if grp < 2:
                own, ok = q - k, q >= k
                pv, okp = P + q - k, k >= q
                bias[grp, :, slot, 1] = np.where(okp, -slopes[grp, h] * (d * pv).astype(f), f(NEG))
            else:
                own, ok = q - k, (q >= k) & (q // 64 == k // 64)
            bias[grp, :, slot, 0] = np.where(ok, -slopes[grp, h] * (d * own).astype(f), f(NEG))
    out["bias"] = bias
    for grp, name in enumerate(("cache_kv_w128", "cache_kv_w512", "cache_kv_w2048")):
        out[f"cache{grp}"] = g(name)[0].reshape(SAMPLES, PAST[grp], 2 * HPG * HD)
    sbias, k0 = np.zeros((P, SK, 4), f), 0
    for grp in (0, 2, 1):
        m, d = SKEYS[grp], DIL[grp][1]
        back = 16 * m - (np.arange(P)[:, None] % 16 * m + np.arange(m)[None])
        sbias[:, k0:k0 + m] = -slopes[grp][None, None] * (d * back).astype(f)[:, :, None]
        k0 += m
    out["sbias"] = sbias
    out["rt"] = np.ascontiguousarray(cst[0:SAMPLES, C_R:C_END].T)
    dc = np.zeros((P, D_END), f)
    dc[:, D_TRI:D_NEG] = q <= k
    dc[:, D_NEG:D_STR] = np.where(q <= k, f(0), f(NEG))
    dc[:, D_STR:D_ONE] = np.where(q < k, f(-1), f(0))
    dc[:, D_ONE:D_LEV] = 1
    for i in range(7):
        n = 1 << i
        dc[:, D_LEV + i * P:D_LEV + (i + 1) * P] = (q // (2 * n) == k // (2 * n)) & (k // n % 2 == 1) & (q // n % 2 == 0)
    out["dcst"] = dc
    out["dnrows"], out["ffnrows"] = g("state_dn_conv")[0], g("state_ffn_conv")[0]
    out["fstate"] = np.ascontiguousarray(g("state_ffn_conv")[0].reshape(SAMPLES, 2, FT, P).transpose(3, 2, 0, 1))
    out["g2"], out["b2"] = g("ln2_g"), g("ln2_b")
    out["sS"] = np.ascontiguousarray(g("state_dn_S")[0].transpose(2, 1, 0, 3))
    return out


OUTS = {"kv0": (P, 4, 136), "kv1": (P, 4, 520), "kv2": (P, 4, TOK), "dnconv": (P, 12, 11), "shift0": (SAMPLES, 127, 512),
        "shift1": (SAMPLES, 511, 512), "shift2": (SAMPLES, 1023, 512), "pS": (P, DN_H * P), "sS": (P, DN_H, SAMPLES, P),
        "dnrows": (SAMPLES, 2, 12 * P), "ffnrows": (SAMPLES, 1, D_FF), "ffnconv": (P, FT, 10), "y": (TOK, D_MODEL)}


def gather(r):
    y = r["y"]
    heads = (2, HPG, HD)
    kv_p, kv_s = [], []
    for grp in range(GROUPS):
        rows = r[f"kv{grp}"].transpose(2, 1, 0).reshape(-1, *heads)
        kv_p.append(rows[None, None, :-SAMPLES])
        old = r[f"shift{grp}"].reshape(SAMPLES, -1, *heads)
        kv_s.append(np.concatenate([old, rows[-SAMPLES:, None]], 1)[None])
    dn = r["dnconv"].transpose(2, 1, 0).reshape(3 + SAMPLES, 12 * P)
    ffn = r["ffnconv"].transpose(2, 1, 0).reshape(2 + SAMPLES, D_FF)
    return (y[None, :SEQ], y[SEQ:, None], *kv_p,
            dn[None, None, :3], r["pS"].reshape(P, DN_H, P).transpose(1, 0, 2)[None, None], ffn[None, None, :2],
            *kv_s,
            np.concatenate([r["dnrows"], dn[3:, None]], 1)[None], r["sS"].transpose(2, 1, 0, 3)[None],
            np.concatenate([r["ffnrows"], ffn[2:, None]], 1)[None])


def kernel(**inputs):
    import concourse.bacc as bacc
    from concourse.bass_utils import run_bass_kernel_spmd

    nc = bacc.Bacc("TRN2", target_bir_lowering=False, num_devices=1)
    arrays = {"in_" + name: np.ascontiguousarray(a) for name, a in layout(inputs).items()}
    ins = {name[3:]: nc.dram_tensor(name, a.shape, mybir.dt.from_np(a.dtype), kind="ExternalInput").ap()
           for name, a in arrays.items()}
    outs = {name: nc.dram_tensor("out_" + name, shape, F32, kind="ExternalOutput").ap() for name, shape in OUTS.items()}
    build(nc, ins, outs)
    r = run_bass_kernel_spmd(nc, [arrays], core_ids=[0])
    r = {name: r.results[0]["out_" + name] for name in OUTS}
    return tuple(np.ascontiguousarray(a) for a in gather(r))
```

```python
import numpy as np

import concourse.bass as bass
from concourse import mybir
from contextlib import ExitStack

F32 = mybir.dt.float32
F32R = mybir.dt.float32r
ALU = mybir.AluOpType
ACT = mybir.ActivationFunctionType
AX = mybir.AxisListType

P = 128
D_MODEL, SEQ, SAMPLES = 1024, 1024, 8
D_FF = 2816
DIL = ((128, 1), (512, 4), (2048, 16))
GROUPS, HPG, HD = 3, 4, 64
ATT_W = GROUPS * HPG * HD
DN_H, DN_D = 4, 128
TOK = SEQ + SAMPLES
THIRDS = 3
TW = TOK // THIRDS
KT = D_MODEL // P
FT = D_FF // P
OFF_DN = 3 * ATT_W
OFF_Z = OFF_DN + 3 * DN_H * DN_D
OFF_BA = OFF_Z + DN_H * DN_D
OFF_GATE = OFF_BA + 2 * DN_H
ALPHA = 2.0 ** 0.25
LN_EPS, RMS_EPS = 1e-5, 1e-6
NEG = -1e30
N_CONSTS = 4
CONV_STEPS = 16
FFN_STEPS = 12
SMALL_0, SMALL_S, DN_STEPS = 5, 17, 19
BLOCKS = 8
TILES = SEQ // P
PAST = (128, 512, 1024)
SKEYS = (8, 8, 4)
SK = sum(SKEYS)

U_BLK = 10
U_DN = 18
U_Z = U_DN + 12
U_GATE = U_Z + DN_H
U_BRANCH = U_GATE + 16
EARLY = 4
SINGLE = 4
U_MIX = U_BRANCH + KT
U_FFN = U_MIX + KT
PIECES = (8, 8, 6)
WINDOWS = TILES + 1
LAST_USED = 3 * (U_FFN - U_BRANCH + len(PIECES) * KT)
UNITS = U_FFN + sum(2 * n + KT for n in PIECES)
U_LAST = UNITS - KT

C_ID, C_DNW, C_FFW, C_FFB, C_G1, C_B1, C_ON, C_R, C_END = np.cumsum(
    [0, P, 12 * 4, FT * 3, FT, KT, KT, 1, P]).tolist()
D_TRI, D_NEG, D_STR, D_ONE, D_LEV, D_END = np.cumsum([0, P, P, P, P, 7 * P]).tolist()


def third(j):
    return slice(j * TW, (j + 1) * TW)


def build(nc, I, O):
    ctx = ExitStack()
    with ctx:
        def sem(name):
            return ctx.enter_context(nc.semaphore(name))

        def held(stack, name, shape, dt=F32):
            return stack.enter_context(nc.sbuf_tensor(name, shape, dt))

        att_scr = nc.dram_tensor("att_scr", [GROUPS, SEQ, HPG * 66], F32).ap()
        dn_scr = nc.dram_tensor("dn_scr", [16, P, SEQ + P], F32).ap()
        gate_scr = nc.dram_tensor("gate_scr", [16, P, TOK], F32).ap()

        xh = held(ctx, "xh", [P, KT, TOK], F32R)
        xl = held(ctx, "xl", [P, KT, TOK], F32R)
        stage = held(ctx, "stage", [P, 2, KT * P])
        wh = held(ctx, "wh", [P, 2, KT * P], F32R)
        wl = held(ctx, "wl", [P, 2, KT * P], F32R)
        cst = held(ctx, "cst", [P, C_END])
        ident = cst[:, C_ID:C_ID + P]
        mhalf = held(ctx, "mhalf", [P, 64])
        babuf = held(ctx, "babuf", [P, 8, 9, DN_H])

        early = ExitStack()
        with early:
            qkv = held(early, "qkv", [P, 18, TOK])
            q_st = held(early, "q_st", [P, 2, P])
            k_st = held(early, "k_st", [P, 2, 2, P])
            v_st = held(early, "v_st", [P, 2, P])
            bias = held(early, "bias", [P, 4, 2, P])
            sb = held(early, "sb", [P, 4, 2, P])
            pb = held(early, "pb", [P, 4, 2, P])
            pts = held(early, "pts", [P, 8, P])
            vtok = held(early, "vtok", [P, 2, 256])
            obuf = held(early, "obuf", [P, 2, 4, 66])
            nmax = held(early, "nmax", [P, 4])
            pre = held(early, "pre", [P, 2, 3 + TOK])
            cb = held(early, "cb", [P, TOK])
            thb = held(early, "thb", [P, TOK])
            tails = held(early, "tails", [P, 12, 11])
            sconv = held(early, "sconv", [P, 12, SAMPLES, 3])
            wba = held(early, "wba", [P, KT, 8])
            bac = held(early, "bac", [P, 2, DN_H])
        xraw = qkv[:, 10:18, :]

        middle = ExitStack()
        with middle:
            oh = held(middle, "oh", [P, 6, TOK], F32R)
            ol = held(middle, "ol", [P, 6, TOK], F32R)
            with ExitStack() as part:
                gates = held(part, "gates", [P, 2, 2, TOK])
            gth = held(middle, "gth", [P, 2, TOK])
            with ExitStack() as part:
                sq = held(part, "sq", [SAMPLES, 3, 3, 256])
                qb = held(part, "qb", [P, 3, 256])
                ssc = held(part, "ssc", [P, SK, 4])
                sbias = held(part, "sbias", [P, SK, 4])
                og = held(part, "og", [P, 3, 256])
                rt = held(part, "rt", [P, SAMPLES])
                sm = held(part, "sm", [P, 16, 4])
                self_s = held(part, "self_s", [SAMPLES, 3, 4])
                self_p = held(part, "self_p", [SAMPLES, 3, 256])
                o8 = self_p[:, 0, :]
                kvc = held(part, "kvc", [P, SK, 2, 256])
            dnin = held(middle, "dnin", [P, 12, P])
            zin = held(middle, "zin", [P, 4, P])
            rn = held(middle, "rn", [P, 4, 8])
            dcst = held(middle, "dcst", [P, D_END])
            cf = held(middle, "cf", [P, 4, DN_H * (TILES + 1)])
            onh = held(middle, "onh", [P, 1])
            part = ExitStack()
            with part:
                abuf = held(part, "abuf", [P, 3, 4, 66])
                amx = held(part, "amx", [P, 8, 4])
                ao = held(part, "ao", [P, 4, 64])
                of = held(part, "of", [P, 4, P])
                ET = held(part, "ET", [P, 4, P])
                ETs = held(part, "ETs", [P, 4, P])
                sq2 = held(part, "sq2", [P, 8, P])
                qn, kn, kb, qd, kbe, kd, vb = (held(part, n, [P, 4, P]) for n in
                                               ("qn", "kn", "kb", "qd", "kbe", "kd", "vb"))
                kqT = held(part, "kqT", [P, 2, 4 * P])
                kbT, qdT, ATm, LTm, XT, S = (held(part, n, [P, 4 * P]) for n in (
                    "kbT", "qdT", "ATm", "LTm", "XT", "S"))
                flat4 = lambda ap: ap.rearrange("p h k -> p (h k)")
                X, Lb, Y = kbT, kqT, flat4(sq2[:, 4:8, :])
                wkT, us = flat4(qn[:]), flat4(kb[:])
                gB = ATm[:].rearrange("p (h k) -> p h k", h=4)
            part = ExitStack()
            with part:
                sS = held(part, "sS", [P, DN_H, SAMPLES, P])
                sin = held(part, "sin", [P, 16, SAMPLES])
                s64 = held(part, "s64", [P, 6, 64])
                sdv = held(part, "sdv", [P, 2, 4, P])
                sdiag = held(part, "sdiag", [SAMPLES, 2, SAMPLES, DN_H])
                sof = held(part, "sof", [P, DN_H, SAMPLES])

        late = ExitStack()
        with late:
            hh = held(late, "hh", [P, KT, TOK], F32R)
            hl = held(late, "hl", [P, KT, TOK], F32R)
            acc = held(late, "acc", [P, KT, TOK])
            ab = held(late, "ab", [P, 2 + TOK])
            cc = held(late, "cc", [P, TOK])
            gl = held(late, "gl", [P, TOK])
            fstate = held(late, "fstate", [P, FT, SAMPLES, 2])
            ftails = held(late, "ftails", [P, FT, 10])
            stats = held(late, "stats", [P, 2, 2, 6])
            mv = held(late, "mv", [P, 2, 4])
            mt = ab[:, 0:TW]
            xn = (gl[:, 0:D_MODEL], cc[:, 0:D_MODEL])
        with ExitStack() as part:
            g2r = held(part, "g2r", [P, D_MODEL])
            b2r = held(part, "b2r", [P, D_MODEL])
            yt = held(part, "yt", [P, 2, D_MODEL])
            dwh = held(part, "dwh", [P, KT - 1, PIECES[-1] * P], F32R)
            dwl = held(part, "dwl", [P, KT - 1, PIECES[-1] * P], F32R)

        U = ctx.enter_context(nc.psum_tensor("U", [P, 3, 512], F32))
        B34 = ctx.enter_context(nc.psum_tensor("B34", [P, 2, 512], F32))
        B56 = ctx.enter_context(nc.psum_tensor("B56", [P, 2, 512], F32))
        B7 = ctx.enter_context(nc.psum_tensor("B7", [P, 512], F32))

        consts_in = sem("consts_in")
        x_in = [sem(f"x_in{i}") for i in range(4)]
        x_hi, x_lo, conv_in = sem("x_hi"), sem("x_lo"), sem("conv_in")
        zeroed = sem("zeroed")
        w_in = [sem("w_in0"), sem("w_in1")]
        w_hi, w_lo = sem("w_hi"), sem("w_lo")
        slice_done = sem("slice_done")
        taken = sem("taken")
        ba_rows, ba_staged = sem("ba_rows"), sem("ba_staged")
        ba_done, ba_raw, ba_act, ba_dve = sem("ba_done"), sem("ba_raw"), sem("ba_act"), sem("ba_dve")
        bias_in = sem("bias_in")
        qk_staged, v_staged = sem("qk_staged"), sem("v_staged")
        s_done, biased, maxed, exped = sem("s_done"), sem("biased"), sem("maxed"), sem("exped")
        pt_done, pt_taken = sem("pt_done"), sem("pt_taken")
        v_done, v_taken = sem("v_done"), sem("v_taken")
        pv_done, o_taken = sem("pv_done"), sem("o_taken")
        o_stored = [sem("o_stored0"), sem("o_stored1")]
        kv_stored = sem("kv_stored")
        conv_step, conv_tanh, conv_out, conv_stored, tail_stored = (
            sem("conv_step"), sem("conv_tanh"), sem("conv_out"), sem("conv_stored"), sem("tail_stored"))
        small_step = sem("small_step")
        samp_in, samp_pe, samp_act, samp_dve = sem("samp_in"), sem("samp_pe"), sem("samp_act"), sem("samp_dve")
        dcst_in, dn_in, z_in, att_in = sem("dcst_in"), sem("dn_in"), sem("z_in"), sem("att_in")
        used = sem("used")
        gates_in = [sem("gates_in0"), sem("gates_in1")]
        merged, m_high, m_low, acc_in = sem("merged"), sem("m_high"), sem("m_low"), sem("acc_in")
        ln_in, ln_var, ln_root, ln_shift, ln_norm, ln_back, ln_front, ln_rear, h_high, h_low, ln_step, ln_mul = (
            sem(n) for n in ("ln_in", "ln_var", "ln_root", "ln_shift", "ln_norm", "ln_back", "ln_front", "ln_rear",
                             "h_high", "h_low", "ln_step", "ln_mul"))
        y_rear = sem("y_rear")
        fstate_in, f_zero, a_taken, f_step, f_gelu, f_prod, f_high, f_low = (
            sem(n) for n in ("fstate_in", "f_zero", "a_taken", "f_step", "f_gelu", "f_prod", "f_high", "f_low"))
        rows2_in, y_ready, y_stored, ftail_stored = sem("rows2_in"), sem("y_ready"), [sem("y_s0"), sem("y_s1")], sem("ftail_stored")
        ds_in, ds_pe, ds_act, ds_dve, ds_scaled, ds_prod, ds_new, ds_o = (
            sem(n) for n in ("ds_in", "ds_pe", "ds_act", "ds_dve", "ds_scaled", "ds_prod", "ds_new", "ds_o"))
        half_set = sem("half_set")
        state_in = [sem(f"state_in{h}") for h in range(DN_H)]
        values_in, samp_pool = sem("values_in"), sem("samp_pool")
        ss_ready, rs_ready = sem("ss_ready"), sem("rs_ready")
        cf_pe, cf_dve, cf_act = sem("cf_pe"), sem("cf_dve"), sem("cf_act")
        g_staged, g_done, decay_sum, decay_exp = sem("g_staged"), sem("g_done"), sem("decay_sum"), sem("decay_exp")
        lb_ready = sem("lb_ready")
        tv_done, g_read, x_added, z_done = sem("tv_done"), sem("g_read"), sem("x_added"), sem("z_done")
        tr1_done, squared, qkn_ready, kbqd_ready = sem("tr1_done"), sem("squared"), sem("qkn_ready"), sem("kbqd_ready")
        v_ready, tr2_done, kqT_taken, tr3_done, kbqd_taken = (
            sem("v_ready"), sem("tr2_done"), sem("kqT_taken"), sem("tr3_done"), sem("kbqd_taken"))
        la_done, y_done, y_taken, zt_done, xt_ready, x_done, x_taken = (
            sem("la_done"), sem("y_done"), sem("y_taken"), sem("zt_done"), sem("xt_ready"), sem("x_done"),
            sem("x_taken"))
        wk_done, wk_taken, u_done, u_taken, od_done, s_ready = (
            sem("wk_done"), sem("wk_taken"), sem("u_done"), sem("u_taken"), sem("od_done"), sem("s_ready"))
        o_squared, on_ready, on_done, of_ready, of_high, of_low = (
            sem("o_squared"), sem("on_ready"), sem("on_done"), sem("of_ready"), sem("of_high"), sem("of_low"))
        ae_ready, ae_exp, ao_ready, ao_done, ao_high, ao_low = (
            sem("ae_ready"), sem("ae_exp"), sem("ao_ready"), sem("ao_done"), sem("ao_high"), sem("ao_low"))
        gate_stored, dn_step, shifted, state_stored, pad_stored = (
            [sem("gate_stored0"), sem("gate_stored1")], sem("dn_step"), sem("shifted"), sem("state_stored"), sem("pad_stored"))


        GT = (0, 12, 6)
        ALL_QKV = 3 * U_DN

        def pairs(eng, first, count):
            with eng.Fori(0, count // 2) as i:
                for half in (0, 1):
                    yield i * 2 + (first + half), half, i

        def peeled(first, count):
            for n in range(first, first + count):
                yield n, n % 2, None

        def after(eng, s, n):
            if not (isinstance(n, int) and n <= 0):
                eng.wait_ge(s, n)

        def bulk(eng):
            yield from peeled(0, 2)
            yield from pairs(eng, 2, U_BLK - 2)

        class Steps:

            def __init__(self, eng, s):
                self.eng, self.s, self.base, self.n = eng, s, 0, 0

            def item(self, index, per):
                self.base, self.n, self.per = index * per, 0, per

            def link(self, ins):
                self.n += 1
                ins.then_inc(self.s, 1)
                self.eng.wait_ge(self.s, self.base + self.n)

        def blocks_of(eng, before_group=None):
            for b, par, _ in peeled(0, 2):
                yield b, par, 0, b, b > 0, "att"
            for b, par, i in pairs(eng, 2, 6):
                yield b, par, 0, b, True, "att"
            if before_group:
                before_group(1)
            for b, par, _ in peeled(BLOCKS, 2):
                yield b, par, 1, (0, par), par == 1, "dn"
            for b, par, i in pairs(eng, BLOCKS + 2, BLOCKS - 2):
                yield b, par, 1, (i + 1, par), par == 1, "dn"
            if before_group:
                before_group(2)
            for b, par, i in pairs(eng, 2 * BLOCKS, 4):
                yield b, par, 2, i * 2 + par, False, "dn"
            for b, par, _ in peeled(2 * BLOCKS + 4, 2):
                yield b, par, 2, b - 2 * BLOCKS, False, "z"
            for b, par, i in pairs(eng, 2 * BLOCKS + 6, 2):
                yield b, par, 2, i * 2 + (6 + par), False, "z"

        def cols(tiles, g, n):
            if g == 0:
                return tiles[:, :, bass.ds(n * P, P)]
            v = tiles.rearrange("p j (i d) -> p j d i", d=DIL[g][1])
            if g == 1:
                return v[:, :, bass.ds(n[0], 1), n[1] * P:(n[1] + 1) * P].squeeze(2)
            return v[:, :, bass.ds(n * 2, 2), :]

        def packed(t, g):
            return t.rearrange("p j (d i) -> p j d i", d=2) if g == 2 else t

        def stored_before(b, par, g, n):
            if g == 0:
                return (b - par) * 8
            if g == 1:
                return n[0] * 16 + 64
            return (n - par) * 16 + 128

        QUARTERS = 18
        LEVELS = 6

        class Beside:

            def __init__(self, u, par, units, quarter, start_unit):
                self.u, self.par, self.units, self.quarter, self.start_unit, self.c = (
                    u, par, units, quarter, start_unit, 0)

            def run(self, n):
                end = min(self.c + n, QUARTERS * self.units)
                for c in range(self.c, end):
                    x, q = c // QUARTERS, c % QUARTERS
                    if q == 0:
                        self.start_unit(self.u + x, (self.par + x) % 2)
                    self.quarter(self.u + x, (self.par + x) % 2, q // 6, q % 6)
                self.c = end

            def some(self, two, one):
                self.run(two if self.units == 2 else one)

            def rest(self):
                self.run(QUARTERS * self.units)

        def tiles(eng):
            with eng.Fori(0, SINGLE // 2) as i:
                for half in (0, 1):
                    yield i * 2 + half, i * 2 + (U_GATE + EARLY + half), half, 1
            with eng.Fori(0, TILES - SINGLE) as i:
                yield i + SINGLE, i * 2 + (U_GATE + EARLY + SINGLE), 0, 2

        def window(t):
            return t % 2, slice(t * P, min((t + 1) * P, TOK)), min(P, TOK - t * P)

        BESIDE_LAST = 5

        def last_slices():
            follows = {(1, 1): 0, (1, 5): 1, (2, 0): 2, (2, 3): 3, (2, 6): 4}
            for j in range(THIRDS):
                for f in range(KT):
                    yield j, f, j * KT + f, follows.get((j, f))

        def pieces():
            f0, u0, before = 0, U_FFN, 3 * (U_FFN - U_BRANCH)
            for n in PIECES:
                yield n, f0, u0, before
                f0, u0, before = f0 + n, u0 + 2 * n + KT, before + 3 * KT

        block = ctx.enter_context(nc.Block())

        @block.sync
        def _(sp):
            for i in range(4):
                sp.dma_start(xraw[:, 2 * i:2 * i + 2, :], I["xT"][:, 2 * i:2 * i + 2, :]).then_inc(x_in[i], 16)
                if i < 2:
                    sp.dma_start(stage[:, i, :], I["wu"][i]).then_inc(w_in[i], 16)

            def load(u, par):
                sp.wait_ge(w_lo, u - 1)
                sp.dma_start(stage[:, par, :], I["wu"][bass.ds(u, 1)].squeeze(0)).then_inc(w_in[par], 16)

            sp.dma_start(dn_scr[0:12, :, TOK:SEQ + P], I["wu"][0:12, :, 0:SEQ + P - TOK]).then_inc(pad_stored, 16)
            sp.dma_start(O["dnrows"], I["dnrows"][:, 1:3, :]).then_inc(shifted, 16)
            sp.dma_start(O["ffnrows"], I["ffnrows"][:, 1:2, :]).then_inc(shifted, 16)
            for u, par, _ in bulk(sp):
                load(u + 2, par)

            def next_bias(g):
                sp.wait_ge(biased, g * BLOCKS)
                sp.dma_start(bias[:], I["bias"][g]).then_inc(bias_in, 16)
                if g == 2:
                    sp.wait_ge(taken, ALL_QKV)
                    for grp in range(GROUPS):
                        keep = min(DIL[grp][0], SEQ)
                        sp.dma_start(O[f"kv{grp}"], qkv[:, GT[grp] + 2:GT[grp] + 6, SEQ - keep:TOK]).then_inc(
                            kv_stored, 16)

            def rows_out(f):
                sp.wait_ge(conv_out, f + 2)
                sp.dma_start(dn_scr[bass.ds(f, 1), :, 0:TOK].squeeze(0), thb[:]).then_inc(conv_stored, 16)

            for b, par, g, n, prev, kind in blocks_of(sp, next_bias):
                load(b + (U_BLK + 2), par)
                if kind != "att" and not (isinstance(b, int) and b == BLOCKS):
                    rows_out(b - (BLOCKS + 1))
                sp.wait_ge(o_taken, b + 1)
                src = obuf[:, par, :, :].rearrange("p h c -> p (h c)")
                if g == 0:
                    sp.dma_start(att_scr[0][bass.ds(b * P, P), :], src).then_inc(o_stored[par], 16)
                elif g == 1:
                    dst = att_scr[1].rearrange("(i d) c -> d i c", d=4)
                    sp.dma_start(dst[bass.ds(n[0], 1), par * P:(par + 1) * P, :].squeeze(0), src).then_inc(
                        o_stored[par], 16)
                else:
                    dst = att_scr[2].rearrange("(i d) c -> d i c", d=16)
                    for r in range(2):
                        sp.dma_start(dst[bass.ds(n * 2 + r, 1)].squeeze(0), src[64 * r:64 * r + 64, :]).then_inc(
                            o_stored[par], 16)
            rows_out(2 * BLOCKS - 1)
            sp.dma_start(O["dnconv"], tails[:]).then_inc(tail_stored, 16)
            sp.wait_ge(conv_stored, 16 * 16)
            sp.wait_ge(tail_stored, 16)
            for par in (0, 1):
                sp.wait_ge(o_stored[par], 16 * (4 + 4 + 8))
            sp.wait_ge(pv_done, 24)
            sp.wait_ge(conv_out, 17)
            k0 = 0
            for g in (0, 2, 1):
                src = I[f"cache{g}"].rearrange("b (c j d) e -> (b c) j d e", c=16, d=DIL[g][1])
                sp.dma_start(kvc[:, k0:k0 + SKEYS[g], 0, :], src[:, :, 0, 0:256]).then_inc(samp_in, 16)
                k0 += SKEYS[g]
            sp.wait_ge(kv_stored, 48)
            sp.wait_ge(samp_act, 1)
            sp.dma_start(sbias[:], I["sbias"]).then_inc(samp_in, 16)
            sp.dma_start(rt[:], I["rt"]).then_inc(samp_in, 16)
            load(U_GATE + 2, 0)
            k0 = 0
            for g in (0, 2, 1):
                src = I[f"cache{g}"].rearrange("b (c j d) e -> (b c) j d e", c=16, d=DIL[g][1])
                sp.dma_start(kvc[:, k0:k0 + SKEYS[g], 1, :], src[:, :, 0, 256:512]).then_inc(values_in, 16)
                k0 += SKEYS[g]

            def gate_out(u, par):
                sp.wait_ge(taken, (u + 1) * 3)
                sp.dma_start(gate_scr[bass.ds(u - U_GATE, 1)].squeeze(0), gth[:, par, :]).then_inc(gate_stored[par], 16)

            for x in range(EARLY - 1):
                load(U_GATE + 3 + x, (x + 1) % 2)
                gate_out(U_GATE + x, x % 2)
            sp.wait_ge(samp_pe, 6)
            sp.dma_start(dcst[:], I["dcst"]).then_inc(dcst_in, 16)

            def rows_in(t):
                sp.dma_start(dnin[:], dn_scr[0:12, :, bass.ds(t * P, P)].rearrange("f p t -> p f t")).then_inc(
                    dn_in, 16)

            sp.wait_ge(pad_stored, 16)
            rows_in(0)
            gate_out(U_GATE + EARLY - 1, (EARLY - 1) % 2)
            for t, u, par, units in tiles(sp):
                load(u + 2, par)
                after(sp, of_low, t)
                sp.dma_start(zin[:], dn_scr[12:16, :, bass.ds(t * P, P)].rearrange("f p t -> p f t")).then_inc(z_in, 16)
                sp.wait_ge(ao_low, t + 1)
                sp.dma_start(abuf[:].rearrange("p g h c -> p g (h c)"),
                             att_scr[:, bass.ds(t * P, P), :].rearrange("g t c -> t g c")).then_inc(att_in, 16)
                for g in range(GROUPS):
                    sp.dma_start(O[f"shift{g}"][bass.ds(t, 1)], I[f"cache{g}"][bass.ds(t, 1), 1:, :]).then_inc(
                        shifted, 16)
                sp.wait_ge(v_ready, t + 1)
                sp.dma_start(dnin[:], dn_scr[0:12, :, bass.ds((t + 1) * P, P)].rearrange("f p t -> p f t")).then_inc(
                    dn_in, 16)
                if units == 2:
                    load(u + 3, 1 - par)
                for x in range(units):
                    gate_out(u + x, (par + x) % 2)
            sp.wait_ge(s_ready, TILES + 1)
            sp.dma_start(O["pS"], S[:]).then_inc(state_stored, 16)
            sp.wait_ge(of_low, TILES)
            sp.dma_start(sin[:], dn_scr[:, :, SEQ:TOK].rearrange("f p b -> p f b")).then_inc(ds_in, 16)
            for h in range(DN_H):
                sp.dma_start(sS[:, h], I["sS"][:, h]).then_inc(state_in[h], 16)
            for par in (0, 1):
                sp.wait_ge(gate_stored[par], 16 * TILES)
            sp.wait_ge(qkn_ready, TILES + 1)

            def gates_of(f, par):
                sp.dma_start(gates[:, par, :, :], gate_scr[bass.ds(f * 2, 2)].rearrange("g p t -> p g t")).then_inc(
                    gates_in[par], 16)

            gates_of(0, 0)
            gates_of(1, 1)
            sp.wait_ge(ds_new, 8)
            sp.dma_start(O["sS"], sS[:]).then_inc(state_stored, 16)
            sp.wait_ge(of_low, TILES + 1)
            sp.wait_ge(state_stored, 32)
            sp.wait_ge(shifted, 16 * 26)
            sp.dma_start(fstate[:], I["fstate"]).then_inc(fstate_in, 16)

            def x_of(f, n):
                sp.dma_start(acc[:, bass.ds(f, n), :], I["xT"][:, bass.ds(f, n), :]).then_inc(acc_in, 16)

            for f, par, _ in pairs(sp, 0, KT - 2):
                load(f + (U_BRANCH + 2), par)
                sp.wait_ge(used, f * 3 + 3)
                gates_of(f + 2, par)
                x_of(f, 1)
            for f in range(KT - 2, KT):
                load(f + (U_BRANCH + 2), f % 2)
            x_of(KT - 2, 2)
            for u, par, _ in pairs(sp, U_MIX + 2, U_LAST - U_MIX - 2):
                load(u, par)
            for u in range(U_LAST, UNITS):
                sp.wait_ge(w_lo, u - 1)
                sp.dma_start(stage[:, u % 2, 0:PIECES[-1] * P], I["wu"][u][:, 0:PIECES[-1] * P]).then_inc(w_in[u % 2], 16)
            sp.wait_ge(f_low, FT)
            sp.wait_ge(slice_done, 3 * U_LAST)
            sp.dma_start(O["ffnconv"], ftails[:]).then_inc(ftail_stored, 16)
            sp.dma_start(g2r[:], I["g2"].to_broadcast([P, D_MODEL])).then_inc(rows2_in, 16)
            sp.dma_start(b2r[:], I["b2"].to_broadcast([P, D_MODEL])).then_inc(rows2_in, 16)
            for t in range(WINDOWS):
                par, win, m = window(t)
                sp.wait_ge(y_ready, t + 1)
                sp.wait_ge(y_rear, t + 1)
                sp.dma_start(O["y"][win, :], yt[0:m, par, :]).then_inc(y_stored[par], 16)
            sp.wait_ge(y_stored[0], 16 * 5)
            sp.wait_ge(y_stored[1], 16 * 4)
            sp.wait_ge(ftail_stored, 16)

        @block.gpsimd
        def _(pool):
            def low(u, par):
                pool.wait_ge(w_hi, u + 1)
                nc.gpsimd.tensor_tensor(wl[:, par, :], stage[:, par, :], wh[:, par, :].bitcast(F32),
                                        ALU.subtract).then_inc(w_lo, 1)

            def inverse_root(x, n):
                pool.wait_ge(ss_ready, n)
                nc.gpsimd.tensor_tensor(x, x, mhalf[0:x.shape[0], 0:x.shape[1]], ALU.pow).then_inc(rs_ready, 1)

            nc.gpsimd.memset(mhalf[:], -0.5).then_inc(half_set, 1)
            for u, par, _ in pairs(pool, 0, U_GATE):
                low(u, par)
            pool.wait_ge(half_set, 1)
            low(U_GATE, 0)
            low(U_GATE + 1, 1)
            k0, m = SK - SKEYS[1], SKEYS[1]
            pool.wait_ge(samp_in, 16 * 5)
            pool.wait_ge(samp_act, 3)
            keys = kvc[:, k0:SK, 0, :]
            nc.gpsimd.tensor_tensor(keys, keys, qb[:, 2, :].unsqueeze(1).to_broadcast([P, m, 256]), ALU.mult).then_inc(
                samp_pool, 1)
            low(U_GATE + 2, 0)
            low(U_GATE + 3, 1)
            pool.wait_ge(values_in, 16 * 3)
            pool.wait_ge(samp_act, 4)
            vals = kvc[:, k0:SK, 1, :].rearrange("p j (h e) -> p j h e", e=HD)
            nc.gpsimd.tensor_tensor(vals, vals, ssc[:, k0:SK, :].unsqueeze(3).to_broadcast([P, m, HPG, HD]),
                                    ALU.mult).then_inc(samp_pool, 1)
            low(U_GATE + EARLY, 0)
            inverse_root(rn[:, 1, :], 1)
            for t, u, par, units in tiles(pool):
                for x in range(units):
                    low(u + (x + 1), (par + x + 1) % 2)
                inverse_root(rn[:, 3, 4:8], t * 2 + 2)
                inverse_root(rn[:, 1, :], t * 2 + 3)
            inverse_root(s64[0:64, 1, 0:1], 2 * TILES + 2)
            inverse_root(s64[0:32, 1, 1:2], 2 * TILES + 3)

            def root(t, first):
                par, win, m = window(t)
                pool.wait_ge(ln_var, first + t + 1)
                nc.gpsimd.tensor_tensor(mv[0:m, par, 2:3], mv[0:m, par, 1:2], mhalf[0:m, 0:1], ALU.pow).then_inc(
                    ln_root, 1)

            for u, par, _ in pairs(pool, U_BRANCH + 1, U_FFN - U_BRANCH):
                low(u, 1 - par)
            for t in range(WINDOWS + 2):
                if t < WINDOWS:
                    root(t, 0)
                if t >= 2:
                    win = window(t - 2)[1]
                    pool.wait_ge(h_high, t - 1)
                    nc.gpsimd.tensor_tensor(hl[:, :, win], acc[:, :, win], hh[:, :, win].bitcast(F32),
                                            ALU.subtract).then_inc(h_low, 1)
            for u, par, _ in pairs(pool, U_FFN + 1, U_LAST - U_FFN):
                low(u, 1 - par)
            for u in range(U_LAST + 1, UNITS):
                pool.wait_ge(w_hi, u + 1)
                nc.gpsimd.tensor_tensor(dwl[:, u - U_LAST - 1, :], stage[:, u % 2, 0:PIECES[-1] * P],
                                        dwh[:, u - U_LAST - 1, :].bitcast(F32), ALU.subtract).then_inc(w_lo, 1)
            pool.wait_ge(rows2_in, 32)
            for t in range(WINDOWS + 1):
                if t < WINDOWS:
                    root(t, WINDOWS)
                if t >= 1:
                    par, win, m = window(t - 1)
                    pool.wait_ge(ln_mul, WINDOWS + t)
                    nc.gpsimd.tensor_tensor(yt[0:m, par, 512:], yt[0:m, par, 512:], b2r[0:m, 512:], ALU.add).then_inc(
                        y_rear, 1)

        @block.tensor
        def _(pe):
            def products(dst, par, j, ks, x=None, first=True, last=True):
                hi, lo = x or (xh, xl)
                for n, (k, xk) in enumerate(ks):
                    w = slice(k * P, (k + 1) * P)
                    for m, (a, b) in enumerate(((wh, hi), (wl, hi), (wh, lo))):
                        ins = nc.tensor.matmul(dst, a[:, par, w], b[:, xk, third(j)],
                                               start=first and n == 0 and m == 0,
                                               stop=last and n == len(ks) - 1 and m == 2)
                return ins

            def slice_start(u, par, j, n=KT):
                after(pe, taken, u * 3 + (j - 2))
                pe.wait_ge(w_lo, u + 1)
                return products(U[:, j, 0:TW], par, j, [(k, k) for k in range(n)], last=n == KT)

            def slice_rest(par, j, n):
                products(U[:, j, 0:TW], par, j, [(k, k) for k in range(n, KT)], first=False).then_inc(slice_done, 1)

            def unit_slice(u, par, j):
                slice_start(u, par, j).then_inc(slice_done, 1)

            pe.wait_ge(consts_in, 16 * N_CONSTS)
            for k in range(KT):
                pe.wait_ge(x_in[k // 2], 16)
                for j in range(THIRDS):
                    dst = (B34[0:8, 0, 0:TW], B34[0:8, 1, 0:TW], B56[0:8, 0, 0:TW])[j]
                    ins = nc.tensor.matmul(dst, wba[:, k, :], xraw[:, k, third(j)], start=k == 0, stop=k == KT - 1)
            ins.then_inc(ba_rows, 1)
            for u, par, _ in bulk(pe):
                if isinstance(u, int) and u == 0:
                    for k in range(KT):
                        pe.wait_ge(x_lo, k + 1)
                for j in range(THIRDS):
                    unit_slice(u, par, j)
                if isinstance(u, int) and u == 0:
                    pe.wait_ge(ba_staged, 1)
                    for t in range(TILES + 1):
                        m = P if t < TILES else SAMPLES
                        ins = nc.tensor.transpose(B7[0:m, 8 * t:8 * t + 8], cb[0:8, t * P:t * P + m], ident[0:8, 0:8])
                    ins.then_inc(ba_done, 1)
            pe.wait_ge(ba_raw, 1)
            for b, par, g, n, prev, kind in blocks_of(pe):
                u = b + U_BLK
                parts = 2 if prev else 1
                unit_slice(u, par, 0)
                pe.wait_ge(qk_staged, b + 1)
                after(pe, biased, b)
                for h in range(HPG):
                    hp, j = h % 2, h // 2
                    rows = slice(64 * hp, 64 * hp + 64)
                    for part in range(parts):
                        ins = nc.tensor.matmul(B34[:, hp, j * 256 + part * P:j * 256 + (part + 1) * P],
                                               q_st[rows, j, :], k_st[rows, (par + part) % 2, j, :],
                                               start=True, stop=True)
                ins.then_inc(s_done, 1)
                pe.wait_ge(v_staged, b + 1)
                after(pe, v_taken, b)
                after(pe, o_taken, b)
                for j in range(2):
                    ins = nc.tensor.transpose(B7[:, j * P:(j + 1) * P], v_st[:, j, :], ident)
                ins.then_inc(v_done, 1)
                unit_slice(u, par, 1)
                slice_start(u, par, 2, 3)
                pe.wait_ge(exped, b + 1)
                after(pe, pt_taken, b)
                for slot in range(HPG):
                    for part in range(parts):
                        c = ((slot % 2) * 2 + part) * P
                        ins = nc.tensor.transpose(B56[:, slot // 2, c:c + P], pb[:, slot, part, :], ident)
                ins.then_inc(pt_done, 1)
                slice_rest(par, 2, 3)
                pe.wait_ge(pt_taken, b + 1)
                pe.wait_ge(v_taken, b + 1)
                for h in range(HPG):
                    slot = (h % 2) * 2 + h // 2
                    for part in range(parts):
                        ins = nc.tensor.matmul(B7[:, 256 + 64 * h:256 + 64 * h + 64], pts[:, 2 * slot + part, :],
                                               vtok[:, (par + part) % 2, 64 * h:64 * h + 64],
                                               start=part == 0, stop=part == parts - 1)
                ins.then_inc(pv_done, 1)

            def start_unit(u, par):
                pe.wait_ge(w_lo, u + 1)

            def quarter(u, par, j, c):
                if c == 0:
                    pe.wait_ge(taken, u * 3 + (j - 2))
                for m in range(4 * c, 4 * c + 4):
                    a, x = ((wh, xh), (wl, xh), (wh, xl))[m % 3]
                    k = m // 3
                    ins = nc.tensor.matmul(U[:, j, 0:TW], a[:, par, k * P:(k + 1) * P], x[:, k, third(j)],
                                           start=m == 0, stop=m == 3 * KT - 1)
                if c == 5:
                    ins.then_inc(slice_done, 1)

            beside = Beside(U_GATE, 0, EARLY, quarter, start_unit)

            def step(ins):
                ins.then_inc(samp_pe, 1)

            pe.wait_ge(o_taken, 24)
            pe.wait_ge(pt_taken, 24)
            pe.wait_ge(biased, 24)
            pe.wait_ge(v_taken, 24)
            for n in range(18):
                dst = (B34, B56, B7)[n // 8]
                dst = dst[0:SAMPLES, n % 8 // 4, n % 4 * P:(n % 4 + 1) * P] if n < 16 else \
                    B7[0:SAMPLES, (n - 16) * P:(n - 15) * P]
                ins = nc.tensor.matmul(dst, qkv[:, n, SEQ:TOK], ident, start=True, stop=True)
            step(ins)
            beside.run(8)
            pe.wait_ge(samp_act, 2)
            for n in range(3):
                ins = nc.tensor.matmul(B34[:, n // 2, n % 2 * 256:n % 2 * 256 + 256], cst[0:SAMPLES, C_R:C_END],
                                       sq[:, n, 0, :], start=True, stop=True)
            step(ins)
            beside.run(30)
            pe.wait_ge(samp_dve, 1)
            nc.tensor.matmul(B7[0:4, 0:P], sm[:, 0, :], ident, start=True, stop=True)
            ins = nc.tensor.matmul(B7[0:4, P:P + SAMPLES], sm[0:SAMPLES, 1, :], ident[0:SAMPLES, 0:SAMPLES],
                                   start=True, stop=True)
            step(ins)
            pe.wait_ge(samp_dve, 2)
            step(nc.tensor.matmul(B34[0:SAMPLES, 0, 0:4], sm[0:4, 4:6, :].rearrange("p a c -> p (a c)"),
                                  ident[0:4, 0:4], start=True, stop=True))
            pe.wait_ge(samp_dve, 3)
            step(nc.tensor.matmul(B56[:, 0, 0:4], cst[0:SAMPLES, C_R:C_END], sm[0:SAMPLES, 6, :],
                                  start=True, stop=True))
            beside.run(22)
            pe.wait_ge(samp_dve, 4)
            pe.wait_ge(samp_in, 16 * 5)
            for n in range(3):
                nc.tensor.matmul(B7[0:SAMPLES, 0:256], rt[:], og[:, n, :], start=n == 0, stop=False)
            for n in range(3):
                nc.tensor.matmul(B7[0:SAMPLES, 0:256], ident[0:SAMPLES, 0:SAMPLES], self_p[:, n, :], start=False,
                                 stop=n == 2)
            nc.tensor.matmul(B7[0:SAMPLES, 256:260], rt[:], sm[:, 7, :], start=True, stop=False)
            for n in range(3):
                ins = nc.tensor.matmul(B7[0:SAMPLES, 256:260], ident[0:SAMPLES, 0:SAMPLES], self_s[:, n, :],
                                       start=False, stop=n == 2)
            step(ins)
            beside.run(4)
            pe.wait_ge(samp_dve, 5)
            for n in range(2):
                ins = nc.tensor.matmul(B34[:, 1, n * SAMPLES:(n + 1) * SAMPLES], o8[:, n * P:(n + 1) * P],
                                       ident[0:SAMPLES, 0:SAMPLES], start=True, stop=True)
            step(ins)

            pe.wait_ge(ao_low, 1)
            pe.wait_ge(dcst_in, 16)
            gall = babuf[:, 1, 0:TILES, :]
            tri = dcst[:, D_TRI:D_TRI + P]
            nc.tensor.matmul(B7[:, 0:32], tri, gall, start=True, stop=True)
            nc.tensor.matmul(B7[:, 32:64], dcst[:, D_ONE:D_ONE + P], gall, start=True, stop=True).then_inc(cf_pe, 1)
            beside.rest()
            pe.wait_ge(cf_act, 3)

            def heads():
                return [(h, slice(h * P, (h + 1) * P)) for h in range(DN_H)]

            def turn_qk(t):
                pe.wait_ge(dn_in, t * 16 + 16)
                for n in range(8):
                    ins = nc.tensor.transpose(B34[:, n // 4, n % 4 * P:(n % 4 + 1) * P], dnin[:, n, :], ident)
                ins.then_inc(tr1_done, 1)

            turn_qk(0)
            for t, u, par, units in tiles(pe):
                beside = Beside(u, par, units, quarter, start_unit)
                pe.wait_ge(s_ready, t + 1)
                for h, c in heads():
                    ins = nc.tensor.transpose(B56[:, 0, c], dnin[:, 8 + h, :], ident)
                ins.then_inc(tv_done, 1)
                pe.wait_ge(g_staged, t + 1)
                for h, c in heads():
                    ins = nc.tensor.matmul(B56[:, 1, c], gB[:, h, :], tri, start=True, stop=True)
                ins.then_inc(g_done, 1)
                beside.some(3, 1)
                pe.wait_ge(qkn_ready, t + 1)
                for src, dst in ((kn, B34[:, 0, :]), (qn, B34[:, 1, :])):
                    for h, c in heads():
                        ins = nc.tensor.transpose(dst[:, c], src[:, h, :], ident)
                ins.then_inc(tr2_done, 1)
                beside.some(2, 1)
                pe.wait_ge(kbqd_ready, t + 1)
                pe.wait_ge(v_ready, t + 1)
                pe.wait_ge(of_ready, t)
                for src, dst in ((kb, B56[:, 0, :]), (qd, B7[:, :])):
                    for h, c in heads():
                        ins = nc.tensor.transpose(dst[:, c], src[:, h, :], ident)
                ins.then_inc(tr3_done, 1)
                beside.some(3, 1)
                pe.wait_ge(kqT_taken, t + 1)
                pe.wait_ge(kbqd_taken, t + 1)
                for rhs, dst in ((kbT, B34[:, 0, :]), (kqT[:, 1, :], B34[:, 1, :])):
                    for h, c in heads():
                        ins = nc.tensor.matmul(dst[:, c], kqT[:, 0, c], rhs[:, c], start=True, stop=True)
                ins.then_inc(la_done, 1)
                beside.some(4, 2)
                pe.wait_ge(xt_ready, t * (LEVELS + 1) + 1)
                for h, c in heads():
                    ins = nc.tensor.transpose(B56[:, 0, c], XT[:, c], ident)
                ins.then_inc(x_done, 1)
                beside.some(2, 1)
                for lv in range(LEVELS):
                    if lv == 0:
                        pe.wait_ge(x_taken, t + 1)
                        pe.wait_ge(lb_ready, t + 1)
                        pe.wait_ge(g_read, t + 1)
                    else:
                        pe.wait_ge(x_added, t * (LEVELS - 1) + lv)
                    for h, c in heads():
                        ins = nc.tensor.matmul(B56[:, 1, c], Lb[:, (lv + 1) % 2, c], X[:, c], start=True, stop=True)
                    ins.then_inc(y_done, 1)
                    beside.some(2, 1)
                    pe.wait_ge(y_taken, t * LEVELS + (lv + 1))
                    pe.wait_ge(xt_ready, t * (LEVELS + 1) + (lv + 1))
                    if lv < LEVELS - 1:
                        for h, c in heads():
                            ins = nc.tensor.matmul(B56[:, 0, c], XT[:, c], Y[:, c], start=True, stop=True)
                        ins.then_inc(z_done, 1)
                    for h, c in heads():
                        ins = nc.tensor.matmul(B7[:, c], Y[:, c], XT[:, c], start=True, stop=True)
                    ins.then_inc(zt_done, 1)
                    if lv == 3:
                        pe.wait_ge(ao_ready, t + 1)
                        for n in range(2):
                            ins = nc.tensor.transpose(B34[:, 1, n * P:(n + 1) * P], ao[:].rearrange(
                                "p h e -> p (h e)")[:, n * P:(n + 1) * P], ident)
                        ins.then_inc(ao_done, 1)
                pe.wait_ge(xt_ready, t * (LEVELS + 1) + (LEVELS + 1))
                for h, c in heads():
                    ins = nc.tensor.matmul(B34[:, 0, c], kbe[:, h, :], XT[:, c], start=True, stop=True)
                ins.then_inc(wk_done, 1)
                beside.some(2, 1)
                pe.wait_ge(ao_low, t + 2)
                pe.wait_ge(wk_taken, t + 1)
                for h, c in heads():
                    nc.tensor.matmul(B34[:, 1, c], XT[:, c], vb[:, h, :], start=True, stop=False)
                    ins = nc.tensor.matmul(B34[:, 1, c], wkT[:, c], S[:, c], start=False, stop=True)
                ins.then_inc(u_done, 1)
                beside.some(2, 1)
                pe.wait_ge(u_taken, t + 1)
                for h, c in heads():
                    nc.tensor.matmul(B56[:, 0, c], qdT[:, c], S[:, c], start=True, stop=False)
                    nc.tensor.matmul(B56[:, 0, c], ATm[:, c], us[:, c], start=False, stop=True)
                for h, c in heads():
                    ins = nc.tensor.matmul(B56[:, 1, c], kd[:, h, :], us[:, c], start=True, stop=True)
                ins.then_inc(od_done, 1)
                turn_qk(t + 1)
                beside.rest()
                pe.wait_ge(on_ready, t + 1)
                for h, c in heads():
                    ins = nc.tensor.transpose(B7[:, c], of[:, h, :], ident)
                ins.then_inc(on_done, 1)

            pe.wait_ge(of_low, TILES)
            pe.wait_ge(ds_dve, 1)
            nc.tensor.matmul(B34[:, 0, 0:64], dcst[0:SAMPLES, D_ONE:D_ONE + P],
                             sdiag[:].rearrange("s x b h -> s (x b h)"), start=True, stop=True).then_inc(ds_pe, 1)
            pe.wait_ge(ds_act, 2)
            one = dcst[:, D_ONE:D_ONE + 1]
            nc.tensor.matmul(B34[0:64, 1, 0:1], s64[:, 0, :], one, start=True, stop=True).then_inc(ds_pe, 1)
            pe.wait_ge(rs_ready, 2 * TILES + 2)
            nc.tensor.matmul(B34[:, 1, 64:128], s64[0:64, 1, 0:1].to_broadcast([64, P]), ident[0:64, 0:64], start=True,
                             stop=True).then_inc(ds_pe, 1)
            pe.wait_ge(ds_dve, 2)

            def sample_out(n):
                h, b0 = n // 2, n % 2 * 4
                pe.wait_ge(ds_new, n + 1)
                for i in range(4):
                    col = h * SAMPLES + b0 + i
                    ins = nc.tensor.matmul(B7[:, col:col + 1], sS[:, h, b0 + i, :], s64[:, 2, col:col + 1], start=True,
                                           stop=True)
                return ins

            for n in range(8):
                h, b0 = n // 2, n % 2 * 4
                pe.wait_ge(ds_scaled, n + 1)
                bank = B56[:, n % 2, :]
                nc.tensor.matmul(bank, dcst[:, D_ONE:D_ONE + P], sdv[:, n % 2].rearrange("p i k -> p (i k)"),
                                 start=True, stop=False)
                for i in range(4):
                    col = h * SAMPLES + b0 + i
                    ins = nc.tensor.matmul(bank[:, i * P:(i + 1) * P], s64[:, 4, col:col + 1].to_broadcast([P, P]),
                                           sS[:, h, b0 + i, :], start=False, stop=i == 3)
                ins.then_inc(ds_prod, 1)
                if n > 0:
                    sample_out(n - 1)
            sample_out(7).then_inc(ds_o, 1)
            pe.wait_ge(ds_act, 3)
            nc.tensor.matmul(B34[0:32, 1, 0:1], s64[:, 0, 0:32], one, start=True, stop=True).then_inc(ds_pe, 1)
            pe.wait_ge(rs_ready, 2 * TILES + 3)
            nc.tensor.matmul(B34[:, 1, 64:96], s64[0:32, 1, 1:2].to_broadcast([32, P]), ident[0:32, 0:32], start=True,
                             stop=True).then_inc(ds_pe, 1)

            dbank = (B34[:, 0, :], B34[:, 1, :], B56[:, 0, :])
            pe.wait_ge(of_low, TILES + 1)
            pe.wait_ge(taken, 3 * U_BRANCH)

            def branch(f, par, skip_wait):
                u = f + U_BRANCH
                pe.wait_ge(w_lo, u + 1)
                for j in range(THIRDS):
                    if not skip_wait:
                        pe.wait_ge(used, f * 3 + (j - 2))
                    products(U[:, j, 0:TW], par, j, [(k, k) for k in range(2)], (oh, ol))
                    products(dbank[j][:, 0:TW], par, j, [(k, k) for k in range(2, 6)], (oh, ol)).then_inc(slice_done, 1)

            for f in range(2):
                branch(f, f, f == 0)
            for f, par, _ in pairs(pe, 2, KT - 2):
                branch(f, par, False)
            pe.wait_ge(m_low, 3 * KT)

            def from_used(u, par, j, n, parts, ks):
                pe.wait_ge(used, n)
                pe.wait_ge(w_lo, u + 1)
                products(U[:, j, 0:TW], par, j, ks, parts).then_inc(slice_done, 1)

            all_k = [(k, k) for k in range(KT)]
            for f, par, _ in pairs(pe, 0, KT):
                for j in range(THIRDS):
                    from_used(f + U_MIX, par, j, f * 3 + (3 * KT + j - 2), (xh, xl), all_k)

            by_feature = ((U[:, 0, :], U[:, 1, :]), (U[:, 2, :], B7[:, :]))

            def by_token(t, first):
                par, win, m = window(t)
                bank = (B34, B56)[par]
                after(pe, ln_norm, first + t - 1)
                for k in range(KT):
                    ins = nc.tensor.transpose(bank[0:m, k // 4, k % 4 * P:(k % 4 + 1) * P], acc[:, k, win], ident)
                ins.then_inc(ln_in, 1)

            pe.wait_ge(used, 3 * (U_FFN - U_BRANCH))
            by_token(0, 0)
            by_token(1, 0)
            for t in range(WINDOWS):
                par, win, m = window(t)
                pe.wait_ge(ln_norm, t + 1)
                after(pe, ln_front, t - 1)
                after(pe, ln_rear, t - 1)
                for k in range(KT):
                    ins = nc.tensor.transpose(by_feature[par][k // 4][:, k % 4 * P:k % 4 * P + m],
                                              xn[par][0:m, k * P:(k + 1) * P], ident[0:m, 0:m])
                ins.then_inc(ln_back, 1)
                if t + 2 < WINDOWS:
                    by_token(t + 2, 0)
            pe.wait_ge(h_low, WINDOWS)
            for n, f0, u0, before in pieces():
                pe.wait_ge(used, before)
                for p, par, i in pairs(pe, 0, n):
                    for j in range(THIRDS):
                        after(pe, f_prod, (p + f0) * 3)
                        pe.wait_ge(w_lo, p * 2 + (u0 + 1))
                        products(U[:, j, 0:TW], 0, j, all_k, (hh, hl)).then_inc(slice_done, 1)
                    for j in range(THIRDS):
                        pe.wait_ge(a_taken, (p + f0) * 3 + (j + 1))
                        pe.wait_ge(w_lo, p * 2 + (u0 + 2))
                        products(U[:, j, 0:TW], 1, j, all_k, (hh, hl)).then_inc(slice_done, 1)
                pe.wait_ge(f_low, f0 + n)
                if f0 + n == FT:
                    break
                for f, par, i in pairs(pe, 0, KT):
                    for j in range(THIRDS):
                        from_used(f + (u0 + 2 * n), par, j, f * 3 + (before + j - 2), (xh, xl),
                                  [(k, k) for k in range(n)])
            for j, f, s, window_after in last_slices():
                after(pe, used, before + s - 2)
                pe.wait_ge(w_lo, U_LAST + f + 1)
                ks = range(PIECES[-1])
                whf, wlf = (wh[:, 0], wl[:, 0]) if f == 0 else (dwh[:, f - 1], dwl[:, f - 1])
                for k in ks:
                    c = slice(k * P, (k + 1) * P)
                    for m, (a, b) in enumerate(((whf, xh), (wlf, xh), (whf, xl))):
                        ins = nc.tensor.matmul(U[:, s % 3, 0:TW], a[:, c], b[:, k, third(j)], start=k == 0 and m == 0,
                                               stop=k == ks[-1] and m == 2)
                ins.then_inc(slice_done, 1)
                if window_after is not None:
                    pe.wait_ge(used, before + j * KT)
                    by_token(window_after, WINDOWS)
            pe.wait_ge(used, LAST_USED)
            for t in range(BESIDE_LAST, WINDOWS):
                by_token(t, WINDOWS)

        @block.scalar
        def _(act):
            act.dma_start(cst[:], I["cst"]).then_inc(consts_in, 16)
            act.dma_start(wba[:], I["wba"]).then_inc(consts_in, 16)
            act.dma_start(sconv[:], I["sconv"]).then_inc(consts_in, 16)
            act.dma_start(bac[:], I["bac"].to_broadcast([P, 2, DN_H])).then_inc(consts_in, 16)
            act.dma_start(bias[:], I["bias"][0]).then_inc(bias_in, 16)

            def high(u, par):
                act.wait_ge(w_in[par], (u - par) * 8 + 16)
                after(act, slice_done, u * 3 - 3)
                nc.scalar.activation(wh[:, par, :], stage[:, par, :], ACT.Copy).then_inc(w_hi, 1)

            def take(u, j, dst):
                act.wait_ge(slice_done, u * 3 + (j + 1))
                nc.scalar.activation(dst, U[:, j, 0:TW], ACT.Copy).then_inc(taken, 1)

            high(0, 0)
            for k in range(KT):
                act.wait_ge(x_in[k // 2], 16)
                nc.scalar.activation(xh[:, k, :], xraw[:, k, :], ACT.Copy).then_inc(x_hi, 1)
            act.wait_ge(x_lo, KT)
            for u, par, _ in bulk(act):
                high(u + 1, 1 - par)
                for j in range(THIRDS):
                    take(u, j, qkv[:, bass.ds(u, 1), third(j)].squeeze(1))
            act.wait_ge(ba_raw, 1)
            act.wait_ge(ba_dve, 1)
            nc.scalar.activation(babuf[:, 2], babuf[:, 0], ACT.Tanh, scale=0.5).then_inc(ba_act, 1)
            nc.scalar.activation(babuf[:, 4], babuf[:, 3], ACT.Exp, scale=-1.0).then_inc(ba_act, 1)
            nc.scalar.activation(bac[:, 0, :], bac[:, 0, :], ACT.Exp).then_inc(ba_act, 1)
            act.wait_ge(ba_dve, 2)
            nc.scalar.activation(babuf[:, 5], babuf[:, 4], ACT.Ln).then_inc(ba_act, 1)
            act.wait_ge(zeroed, 1)
            for b, par, g, n, prev, kind in blocks_of(act):
                u = b + U_BLK
                parts = 2 if prev else 1
                high(u + 1, 1 - par)

                def take_part(j):
                    if kind == "att":
                        take(u, j, qkv[:, bass.ds(u, 1), third(j)].squeeze(1))
                        return
                    if j == 0:
                        act.wait_ge(conv_out, b - BLOCKS)
                    take(u, j, pre[:, par, 3 + j * TW:3 + (j + 1) * TW])

                take_part(0)
                act.wait_ge(v_done, b + 1)
                after(act, pv_done, b)
                nc.scalar.activation(vtok[:, par, :], B7[:, 0:256], ACT.Copy).then_inc(v_taken, 1)
                act.wait_ge(maxed, b + 1)
                after(act, pt_done, b)
                after(act, o_stored[par], stored_before(b, par, g, n))
                for slot in range(HPG):
                    h = (slot % 2) * 2 + slot // 2
                    ins = nc.scalar.activation(pb[:, slot, 0:parts, :], sb[:, slot, 0:parts, :], ACT.Exp,
                                               bias=nmax[:, slot:slot + 1], accum_out=obuf[:, par, h, 64:65])
                ins.then_inc(exped, 1)
                take_part(1)
                act.wait_ge(pt_done, b + 1)
                after(act, pv_done, b)
                if parts == 2:
                    src, dst = B56[:, :, :], pts[:].rearrange("p (a c) k -> p a (c k)", a=2)
                else:
                    src = B56[:].rearrange("p a (c t k) -> p a c t k", t=2, k=P)[:, :, :, 0, :]
                    dst = pts[:].rearrange("p (a c t) k -> p a c t k", a=2, t=2)[:, :, :, 0, :]
                nc.scalar.activation(dst, src, ACT.Copy).then_inc(pt_taken, 1)
                take_part(2)
                if kind != "att":
                    f = b - BLOCKS
                    after(act, conv_stored, f * 16)
                if kind == "dn":
                    act.wait_ge(conv_step, f * CONV_STEPS + CONV_STEPS)
                    nc.scalar.activation(thb[:], cb[:], ACT.Tanh, scale=0.5).then_inc(conv_tanh, 1)
                elif kind == "z":
                    act.wait_ge(taken, u * 3 + 3)
                    nc.scalar.activation(thb[:], pre[:, par, 3:3 + TOK], ACT.Tanh, scale=0.5).then_inc(conv_tanh, 1)


            def start_unit(u, par):
                high(u + 1, 1 - par)

            def quarter(u, par, j, c):
                if c == 5:
                    act.wait_ge(slice_done, u * 3 + (j + 1))
                    if j == 0:
                        after(act, gate_stored[par], (u - (U_GATE + par)) * 8)
                    nc.scalar.activation(gth[:, par, third(j)], U[:, j, 0:TW], ACT.Tanh, scale=0.5).then_inc(taken, 1)

            beside = Beside(U_GATE, 0, EARLY, quarter, start_unit)
            act.wait_ge(samp_pe, 1)
            act.wait_ge(pv_done, 24)
            for par in (0, 1):
                act.wait_ge(o_stored[par], 16 * (4 + 4 + 8))
            act.wait_ge(kv_stored, 48)
            act.wait_ge(conv_stored, 16 * 16)
            act.wait_ge(tail_stored, 16)
            act.wait_ge(conv_out, 17)
            flat = sq[:].rearrange("b g k e -> b (g k e)")
            nc.scalar.activation(flat[:, 0:1024], B34[0:SAMPLES, :, :], ACT.Copy)
            nc.scalar.activation(flat[:, 1024:2048], B56[0:SAMPLES, :, :], ACT.Copy)
            nc.scalar.activation(flat[:, 2048:2304], B7[0:SAMPLES, 0:256], ACT.Copy).then_inc(samp_act, 1)
            act.wait_ge(samp_act, 1)
            nc.scalar.activation(sq[:, :, 0, :], sq[:, :, 0, :], ACT.Copy, scale=HD ** -0.5).then_inc(samp_act, 1)
            beside.run(8)
            act.wait_ge(samp_pe, 2)
            nc.scalar.activation(qb[:, 0:2, :], B34[:, 0, :], ACT.Copy)
            nc.scalar.activation(qb[:, 2, :], B34[:, 1, 0:256], ACT.Copy).then_inc(samp_act, 1)
            beside.run(30)
            act.wait_ge(samp_pe, 5)
            act.wait_ge(samp_dve, 3)
            act.wait_ge(small_step, SMALL_S)
            nc.scalar.activation(ssc[:], ssc[:], ACT.Exp)
            nc.scalar.activation(self_s[:], self_s[:], ACT.Exp).then_inc(samp_act, 1)
            beside.run(22)
            beside.run(4)
            act.wait_ge(samp_pe, 7)
            osp = B34[:, 1, 0:2 * SAMPLES].rearrange("p (n b) -> p n b", n=2)
            nc.scalar.activation(oh[:, 0:2, SEQ:TOK], osp, ACT.Copy).then_inc(ao_high, 1)

            act.wait_ge(cf_pe, 1)
            act.wait_ge(ao_low, 1)
            nc.scalar.activation(cf[:, 1, 0:32], B7[:, 0:32], ACT.Exp)
            nc.scalar.activation(cf[:, 2, 0:32], B7[:, 32:64], ACT.Exp).then_inc(cf_act, 1)
            act.wait_ge(cf_dve, 1)
            nc.scalar.activation(cf[:, 3, 0:32], cf[:, 3, 0:32], ACT.Exp).then_inc(cf_act, 1)
            nc.scalar.activation(onh[:], cst[:, C_ON:C_ON + 1], ACT.Copy, scale=0.5).then_inc(cf_act, 1)

            def squares(t):
                act.wait_ge(tr1_done, t + 1)
                nc.scalar.activation(sq2[:].rearrange("p (a h) k -> p a (h k)", a=2), B34[:, :, :], ACT.Square,
                                     scale=0.5).then_inc(squared, 1)

            beside.rest()
            squares(0)
            for t, u, par, units in tiles(act):
                beside = Beside(u, par, units, quarter, start_unit)
                beside.some(3, 1)
                act.wait_ge(tr2_done, t + 1)
                nc.scalar.activation(kqT[:], B34[:, :, :], ACT.Copy).then_inc(kqT_taken, 1)
                beside.some(2, 1)
                act.wait_ge(tr3_done, t + 1)
                nc.scalar.activation(kbT[:], B56[:, 0, :], ACT.Copy)
                nc.scalar.activation(qdT[:], B7[:, :], ACT.Copy).then_inc(kbqd_taken, 1)
                act.wait_ge(decay_sum, t + 1)
                nc.scalar.activation(ET[:], ET[:], ACT.Exp).then_inc(decay_exp, 1)
                beside.some(3, 1)
                beside.some(4, 2)
                act.wait_ge(x_done, t + 1)
                nc.scalar.activation(X[:], B56[:, 0, :], ACT.Copy).then_inc(x_taken, 1)
                beside.some(2, 1)
                for lv in range(LEVELS):
                    act.wait_ge(y_done, t * LEVELS + (lv + 1))
                    nc.scalar.activation(Y, B56[:, 1, :], ACT.Copy).then_inc(y_taken, 1)
                    beside.some(2, 1)
                    if lv == 0:
                        act.wait_ge(ae_ready, t + 1)
                        nc.scalar.activation(amx[:, 1:4, :], amx[:, 1:4, :], ACT.Exp).then_inc(ae_exp, 1)
                    if lv == 3:
                        act.wait_ge(ao_done, t + 1)
                        nc.scalar.activation(oh[:, 0:2, bass.ds(t * P, P)], B34[:, 1, 0:256].rearrange(
                            "p (n k) -> p n k", n=2), ACT.Copy).then_inc(ao_high, 1)
                act.wait_ge(wk_done, t + 1)
                nc.scalar.activation(wkT, B34[:, 0, :], ACT.Copy, scale=-1.0).then_inc(wk_taken, 1)
                beside.some(2, 1)
                act.wait_ge(u_done, t + 1)
                nc.scalar.activation(us, B34[:, 1, :], ACT.Copy).then_inc(u_taken, 1)
                beside.some(2, 1)
                act.wait_ge(od_done, t + 1)
                nc.scalar.activation(X[:], B56[:, 0, :], ACT.Square).then_inc(o_squared, 1)
                squares(t + 1)
                beside.rest()
                act.wait_ge(of_ready, t + 1)
                nc.scalar.activation(oh[:, 2:6, bass.ds(t * P, P)], of[:], ACT.Copy).then_inc(of_high, 1)

            nc.scalar.activation(babuf[0:SAMPLES, 6, TILES, :], babuf[0:SAMPLES, 1, TILES, :], ACT.Exp).then_inc(
                ds_act, 1)
            act.wait_ge(ds_in, 16)
            nc.scalar.activation(s64[:, 0, :], sin[:, 0:8, :].rearrange("p h b -> p (h b)"), ACT.Square,
                                 scale=0.5).then_inc(ds_act, 1)
            act.wait_ge(ds_o, 1)
            nc.scalar.activation(s64[:, 0, 0:32], B7[:, 0:32], ACT.Square).then_inc(ds_act, 1)
            act.wait_ge(of_ready, TILES + 1)
            nc.scalar.activation(oh[:, 2:6, SEQ:TOK], sof[:], ACT.Copy).then_inc(of_high, 1)

            def merge_high(f):
                for j in range(THIRDS):
                    act.wait_ge(merged, f * 3 + (j + 1))
                    nc.scalar.activation(xh[:, bass.ds(f, 1), third(j)].squeeze(1), cc[:, third(j)], ACT.Copy,
                                         scale=0.5).then_inc(m_high, 1)

            for f, par, _ in pairs(act, 0, KT):
                high(f + (U_BRANCH + 1), 1 - par)
                merge_high(f)
            for f, par, _ in pairs(act, 0, KT):
                high(f + (U_MIX + 1), 1 - par)

            def normed(t, first):
                par, win, m = window(t)
                act.wait_ge(ln_shift, first + t + 1)
                nc.scalar.activation(xn[par][0:m].rearrange("p (a n) -> p a n", a=2), (B34, B56)[par][0:m],
                                     ACT.Identity, bias=mv[0:m, par, 3:4], scale=mv[0:m, par, 2:3]).then_inc(ln_norm, 1)

            for t in range(WINDOWS + 2):
                if t >= 2:
                    par, win, m = window(t - 2)
                    act.wait_ge(ln_back, t - 1)
                    for k in range(4, KT):
                        ins = nc.scalar.activation(acc[:, k, win], (U[:, 1, :], B7[:, :])[par][
                            :, k % 4 * P:k % 4 * P + m], ACT.Identity, bias=cst[:, C_B1 + k:C_B1 + k + 1],
                            scale=cst[:, C_G1 + k:C_G1 + k + 1])
                    ins.then_inc(ln_rear, 1)
                    act.wait_ge(ln_rear, t - 1)
                    act.wait_ge(ln_front, t - 1)
                    nc.scalar.activation(hh[:, :, win], acc[:, :, win], ACT.Copy).then_inc(h_high, 1)
                if t < WINDOWS:
                    normed(t, 0)
            for n, f0, u0, before in pieces():
                for p, par, i in pairs(act, 0, n):
                    u, F = p * 2 + u0, p + f0
                    high(u + 1, 1)
                    after(act, f_step, F * FFN_STEPS)
                    for j in range(THIRDS):
                        act.wait_ge(slice_done, u * 3 + (j + 1))
                        nc.scalar.activation(ab[:, 2 + j * TW:2 + (j + 1) * TW], U[:, j, 0:TW], ACT.Copy).then_inc(
                            a_taken, 1)
                    high(u + 2, 0)
                    act.wait_ge(f_step, F * FFN_STEPS + FFN_STEPS)
                    after(act, f_prod, F * 3)
                    nc.scalar.activation(gl[:], cc[:], ACT.Gelu_apprx_tanh,
                                         bias=cst[:, bass.ds(F + C_FFB, 1)]).then_inc(f_gelu, 1)
                    for j in range(THIRDS):
                        act.wait_ge(f_prod, F * 3 + (j + 1))
                        nc.scalar.activation(xh[:, bass.ds(p, 1), third(j)].squeeze(1), cc[:, third(j)],
                                             ACT.Copy).then_inc(f_high, 1)
                if f0 + n == FT:
                    break
                for f, par, i in pairs(act, 0, KT):
                    high(f + (u0 + 2 * n + 1), 1 - par)
            act.wait_ge(slice_done, 3 * U_LAST)
            for u in range(U_LAST + 1, UNITS):
                act.wait_ge(w_in[u % 2], (u - u % 2) * 8 + 16)
                nc.scalar.activation(dwh[:, u - U_LAST - 1, :], stage[:, u % 2, 0:PIECES[-1] * P], ACT.Copy).then_inc(
                    w_hi, 1)
            act.wait_ge(f_low, FT)
            for t in range(WINDOWS):
                after(act, ln_mul, WINDOWS + t - 1)
                normed(t, WINDOWS)

        @block.vector
        def _(dve):
            nc.vector.memset(pre[:, 0, 0:3], 0.0).then_inc(zeroed, 1)
            nc.vector.memset(pre[:, 1, 0:3], 0.0).then_inc(conv_out, 1)
            nc.vector.memset(babuf[:], 0.0).then_inc(zeroed, 1)
            for k in range(KT):
                dve.wait_ge(x_hi, k + 1)
                nc.vector.tensor_tensor(xl[:, k, :], xraw[:, k, :], xh[:, k, :].bitcast(F32),
                                        ALU.subtract).then_inc(x_lo, 1)
            dve.wait_ge(ba_rows, 1)
            for j in range(THIRDS):
                src = (B34[0:8, 0, 0:TW], B34[0:8, 1, 0:TW], B56[0:8, 0, 0:TW])[j]
                ins = nc.vector.tensor_copy(cb[0:8, third(j)], src)
            ins.then_inc(ba_staged, 1)
            dve.wait_ge(ba_done, 1)
            dve.wait_ge(zeroed, 2)
            ba = B7[:, 0:72].rearrange("p (t c) -> p t c", c=8)
            nc.vector.tensor_copy(babuf[:, 0, 0:TILES, :], ba[:, 0:TILES, 0:4])
            nc.vector.tensor_copy(babuf[0:SAMPLES, 0, TILES, :], ba[0:SAMPLES, TILES, 0:4])
            nc.vector.tensor_copy(babuf[:, 1, 0:TILES, :], ba[:, 0:TILES, 4:8])
            nc.vector.tensor_copy(babuf[0:SAMPLES, 1, TILES, :], ba[0:SAMPLES, TILES, 4:8]).then_inc(ba_raw, 1)
            st = Steps(dve, small_step)
            dve.wait_ge(ba_raw, 1)
            dve.wait_ge(consts_in, 16 * N_CONSTS)
            st.link(nc.vector.tensor_tensor(babuf[:, 1], babuf[:, 1], bac[:, 1, :].unsqueeze(1).to_broadcast(
                [P, 9, DN_H]), ALU.add))
            nc.vector.scalar_tensor_tensor(babuf[:, 3], babuf[:, 1], -1.0, babuf[:, 1], ALU.mult, ALU.max).then_inc(
                ba_dve, 1)
            dve.wait_ge(ba_act, 3)
            nc.vector.tensor_scalar(babuf[:, 4], babuf[:, 4], 1.0, None, ALU.add).then_inc(ba_dve, 1)
            st.link(nc.vector.tensor_scalar(babuf[:, 0], babuf[:, 2], 0.5, 0.5, ALU.mult, ALU.add))
            dve.wait_ge(ba_dve, 1)
            st.link(nc.vector.tensor_scalar(babuf[:, 1], babuf[:, 1], 0.0, None, ALU.max))
            dve.wait_ge(ba_act, 4)
            st.link(nc.vector.tensor_tensor(babuf[:, 1], babuf[:, 1], babuf[:, 5], ALU.add))
            st.link(nc.vector.scalar_tensor_tensor(babuf[:, 1], babuf[:, 1], -1.0, bac[:, 0, :].unsqueeze(1)
                                                   .to_broadcast([P, 9, DN_H]), ALU.mult, ALU.mult))
            cv = Steps(dve, conv_step)

            def silu(b, par, kind):
                dve.wait_ge(conv_tanh, b - (BLOCKS - 1))
                src = cb[:] if kind == "dn" else pre[:, par, 3:3 + TOK]
                nc.vector.scalar_tensor_tensor(thb[:], thb[:], 1.0, src, ALU.add, ALU.mult).then_inc(conv_out, 1)

            for b, par, g, n, prev, kind in blocks_of(dve):
                parts = 2 if prev else 1
                u = b + U_BLK
                dve.wait_ge(taken, 3 * 6 if g == 0 else ALL_QKV)
                after(dve, s_done, b)
                t = GT[g]
                for dst, tile, scale in ((q_st[:], 0, HD ** -0.5), (k_st[:, par], 2, 1.0)):
                    ins = nc.vector.tensor_scalar(packed(dst, g), cols(qkv[:, t + tile:t + tile + 2, 0:SEQ], g, n),
                                                  scale, None, ALU.mult)
                ins.then_inc(qk_staged, 1)
                after(dve, v_done, b)
                nc.vector.tensor_scalar(packed(v_st[:], g), cols(qkv[:, t + 4:t + 6, 0:SEQ], g, n),
                                        1.0, None, ALU.mult).then_inc(v_staged, 1)
                dve.wait_ge(s_done, b + 1)
                after(dve, exped, b)
                dve.wait_ge(bias_in, 16 * (g + 1))
                s_all = B34[:].rearrange("p a (j t k) -> p (a j) t k", j=2, t=2)
                nc.vector.tensor_tensor(sb[:, :, 0:parts, :], s_all[:, :, 0:parts, :], bias[:, :, 0:parts, :],
                                        ALU.add).then_inc(biased, 1)
                dve.wait_ge(biased, b + 1)
                after(dve, o_taken, b)
                nc.vector.tensor_reduce(nmax[:], sb[:, :, 0:parts, :], AX.XY, ALU.max, negate=True).then_inc(maxed, 1)
                if kind != "att" and not (isinstance(b, int) and b == BLOCKS):
                    first_z = isinstance(b, int) and b == 2 * BLOCKS + 4
                    silu(b - 1, 1 - par, "dn" if kind == "dn" or first_z else "z")
                if kind == "dn":
                    f = b - BLOCKS
                    cv.item(f, CONV_STEPS)
                    dnw = [cst[:, bass.ds(f * 4 + (C_DNW + i), 1)] for i in range(4)]
                    dve.wait_ge(conv_out, f + 1)
                    for j in range(THIRDS):
                        dve.wait_ge(taken, u * 3 + (j + 1))
                        a, w = j * TW, (TW if j < 2 else SEQ - 2 * TW)
                        cv.link(nc.vector.tensor_scalar(cb[:, a:a + w], pre[:, par, a + 3:a + 3 + w], dnw[3], None,
                                                        ALU.mult))
                        for i in (2, 1, 0):
                            cv.link(nc.vector.scalar_tensor_tensor(cb[:, a:a + w], pre[:, par, a + i:a + i + w],
                                                                   dnw[i], cb[:, a:a + w], ALU.mult, ALU.add))
                    cv.link(nc.vector.tensor_scalar(cb[:, SEQ:TOK], pre[:, par, SEQ + 3:TOK + 3], dnw[3], None,
                                                    ALU.mult))
                    for i in (2, 1, 0):
                        cv.link(nc.vector.scalar_tensor_tensor(
                            cb[:, SEQ:TOK], sconv[:, bass.ds(f, 1), :, i].squeeze(1), dnw[i], cb[:, SEQ:TOK],
                            ALU.mult, ALU.add))
                    nc.vector.tensor_scalar(tails[:, bass.ds(f, 1), :].squeeze(1), pre[:, par, SEQ:SEQ + 11], 1.0, None,
                                            ALU.mult)
                dve.wait_ge(pv_done, b + 1)
                dve.wait_ge(maxed, b + 1)
                after(dve, o_stored[par], stored_before(b, par, g, n))
                nc.vector.tensor_scalar(obuf[:, par, :, 65].rearrange("p (j a) -> p a j", a=2),
                                        nmax[:].rearrange("p (a j) -> p a j", a=2), -1.0, None, ALU.mult)
                nc.vector.tensor_scalar(obuf[:, par, :, 0:64], B7[:, 256:512].rearrange("p (h e) -> p h e", e=64),
                                        1.0, None, ALU.mult).then_inc(o_taken, 1)
            silu(2 * BLOCKS + 7, 1, "z")

            def mark(ins):
                ins.then_inc(samp_dve, 1)

            def wide(ap, n):
                return ap.unsqueeze(3).to_broadcast([*ap.shape, n])

            st.n = SMALL_0
            dve.wait_ge(samp_act, 3)
            st.link(nc.vector.tensor_tensor(self_p[:], sq[:, :, 0, :], sq[:, :, 1, :], ALU.mult))
            st.link(nc.vector.tensor_reduce(self_s[:], self_p[:].rearrange("b g (h e) -> b g h e", e=HD), AX.X, ALU.add))
            dve.wait_ge(samp_in, 16 * 5)
            k0 = 0
            for n, g in enumerate((0, 2, 1)):
                m = SKEYS[g]
                keys = kvc[:, k0:k0 + m, 0, :]
                if n < 2:
                    st.link(nc.vector.tensor_tensor(keys, keys, qb[:, n, :].unsqueeze(1).to_broadcast([P, m, 256]),
                                                    ALU.mult))
                else:
                    dve.wait_ge(samp_pool, 1)
                st.link(nc.vector.tensor_reduce(ssc[:, k0:k0 + m, :], keys.rearrange("p j (h e) -> p j h e", e=HD),
                                                AX.X, ALU.add))
                k0 += m
            st.link(nc.vector.tensor_tensor(ssc[:], ssc[:], sbias[:], ALU.add))
            nc.vector.tensor_reduce(sm[0:SAMPLES, 1, :], self_s[:].rearrange("b g h -> b h g"), AX.X, ALU.max)
            mark(nc.vector.tensor_reduce(sm[:, 0, :], ssc[:].rearrange("p k h -> p h k"), AX.X, ALU.max))
            dve.wait_ge(samp_pe, 3)
            m48 = sm[0:4, 2:4, :].rearrange("p a c -> p (a c)")
            n48 = sm[0:4, 4:6, :].rearrange("p a c -> p (a c)")
            st.link(nc.vector.tensor_reduce(m48, B7[0:4, 0:P].rearrange("p (b c) -> p b c", c=16), AX.X, ALU.max))
            mark(nc.vector.tensor_tensor(n48, B7[0:4, P:P + SAMPLES], m48, ALU.max))
            dve.wait_ge(samp_pe, 4)
            mark(nc.vector.tensor_copy(sm[0:SAMPLES, 6, :], B34[0:SAMPLES, 0, 0:4]))
            dve.wait_ge(samp_pe, 5)
            dve.wait_ge(samp_dve, 3)
            st.link(nc.vector.tensor_copy(sm[:, 8, :], B56[:, 0, 0:4]))
            st.link(nc.vector.tensor_tensor(ssc[:], ssc[:], sm[:, 8, :].unsqueeze(1).to_broadcast([P, SK, 4]),
                                            ALU.subtract))
            st.link(nc.vector.tensor_tensor(self_s[:], self_s[:], sm[0:SAMPLES, 6, :].unsqueeze(1).to_broadcast(
                [SAMPLES, 3, 4]), ALU.subtract))
            assert st.n == SMALL_S
            dve.wait_ge(samp_act, 4)
            dve.wait_ge(values_in, 16 * 3)
            st.link(nc.vector.tensor_reduce(sm[:, 7, :], ssc[:].rearrange("p k h -> p h k"), AX.X, ALU.add))
            k0 = 0
            for n, g in enumerate((0, 2, 1)):
                m = SKEYS[g]
                vals = kvc[:, k0:k0 + m, 1, :].rearrange("p j (h e) -> p j h e", e=HD)
                if n < 2:
                    st.link(nc.vector.tensor_tensor(vals, vals, wide(ssc[:, k0:k0 + m, :], HD), ALU.mult))
                else:
                    dve.wait_ge(samp_pool, 2)
                st.link(nc.vector.tensor_reduce(og[:, n, :], vals.rearrange("p j h e -> p (h e) j"), AX.X, ALU.add))
                k0 += m
            mark(nc.vector.tensor_tensor(self_p[:].rearrange("b g (h e) -> b g h e", e=HD),
                                         sq[:, :, 2, :].rearrange("b g (h e) -> b g h e", e=HD),
                                         wide(self_s[:], HD), ALU.mult))
            dve.wait_ge(samp_pe, 6)
            st.link(nc.vector.reciprocal(sm[0:SAMPLES, 9, :], B7[0:SAMPLES, 256:260]))
            mark(nc.vector.tensor_tensor(o8.rearrange("b (h e) -> b h e", e=HD),
                                         B7[0:SAMPLES, 0:256].rearrange("b (h e) -> b h e", e=HD),
                                         sm[0:SAMPLES, 9, :].unsqueeze(2).to_broadcast([SAMPLES, 4, HD]), ALU.mult))
            dve.wait_ge(ao_high, 1)
            nc.vector.tensor_tensor(ol[:, 0:2, SEQ:TOK], B34[:, 1, 0:2 * SAMPLES].rearrange("p (n b) -> p n b", n=2),
                                    oh[:, 0:2, SEQ:TOK].bitcast(F32), ALU.subtract).then_inc(ao_low, 1)

            dve.wait_ge(ao_low, 1)
            dve.wait_ge(cf_act, 1)
            st.link(nc.vector.tensor_copy(cf[:, 0, 0:32], B7[:, 0:32]))
            nc.vector.tensor_tensor(cf[:, 3, 0:32], B7[:, 32:64], cf[:, 0, 0:32], ALU.subtract).then_inc(cf_dve, 1)
            nc.vector.memset(cf[:, 1, 32:36], 0.0)
            nc.vector.memset(S[:], 0.0).then_inc(s_ready, 1)
            dve.wait_ge(cf_act, 3)
            dve.wait_ge(dcst_in, 16)
            dn = Steps(dve, dn_step)
            heads4 = lambda ap: ap.rearrange("p (h k) -> p h k", h=DN_H)
            per_head = lambda ap: ap.unsqueeze(2).to_broadcast([P, DN_H, P])
            same = lambda ap: ap.unsqueeze(1).to_broadcast([P, DN_H, P])
            q4, k4, v4, G4 = (heads4(x) for x in (B34[:, 0, :], B34[:, 1, :], B56[:, 0, :], B56[:, 1, :]))

            def stage_g(t):
                nc.vector.tensor_scalar(gB, per_head(babuf[:, 1, bass.ds(t, 1), :].squeeze(1)), 1.0, None,
                                        ALU.mult).then_inc(g_staged, 1)

            def norm_sums(t, steps):
                dve.wait_ge(squared, t + 1)
                steps.link(nc.vector.tensor_reduce(rn[:, 0, :], sq2[:], AX.X, ALU.add))
                nc.vector.tensor_scalar(rn[:, 1, :], rn[:, 0, :], RMS_EPS, None, ALU.add).then_inc(ss_ready, 1)

            def normed(t, steps):
                dve.wait_ge(rs_ready, t * 2 + 1)
                nc.vector.tensor_scalar(rn[:, 2, 0:4], rn[:, 1, 0:4], 0.5 * DN_D ** -0.5, None, ALU.mult)
                steps.link(nc.vector.tensor_scalar(rn[:, 2, 4:8], rn[:, 1, 4:8], 0.5, None, ALU.mult))
                nc.vector.tensor_tensor(qn[:], q4, per_head(rn[:, 2, 0:4]), ALU.mult)
                nc.vector.tensor_tensor(kn[:], k4, per_head(rn[:, 2, 4:8]), ALU.mult).then_inc(qkn_ready, 1)

            def beta_of(t):
                return babuf[:, 0, bass.ds(t, 1), :].squeeze(1)

            def weighted(t):
                dve.wait_ge(qkn_ready, t + 1)
                nc.vector.tensor_tensor(kb[:], kn[:], per_head(beta_of(t)), ALU.mult)
                nc.vector.tensor_tensor(qd[:], qn[:], per_head(cf[:, 1, bass.ds(t * DN_H, DN_H)]), ALU.mult).then_inc(
                    kbqd_ready, 1)

            stage_g(0)
            norm_sums(0, st)
            normed(0, st)
            weighted(0)
            for t, _, _, _ in tiles(dve):
                dn.item(t, DN_STEPS)
                th = bass.ds(t * DN_H, DN_H)
                gc, eg, egt, ekd = (cf[:, n, th] for n in range(4))
                beta = beta_of(t)
                dve.wait_ge(tv_done, t + 1)
                nc.vector.scalar_tensor_tensor(vb[:], v4, 0.5, per_head(beta), ALU.mult, ALU.mult).then_inc(v_ready, 1)
                dve.wait_ge(g_done, t + 1)
                nc.vector.tensor_tensor(ET[:], G4, same(dcst[:, D_NEG:D_NEG + P]), ALU.add).then_inc(g_read, 1)
                dve.wait_ge(g_read, t + 1)
                nc.vector.tensor_tensor(ET[:], ET[:], per_head(gc), ALU.subtract).then_inc(decay_sum, 1)
                dve.wait_ge(kbqd_ready, t + 1)
                nc.vector.tensor_tensor(kbe[:], kb[:], per_head(eg), ALU.mult)
                dve.wait_ge(decay_exp, t + 1)
                dn.link(nc.vector.tensor_tensor(ETs[:], ET[:], same(dcst[:, D_STR:D_STR + P]), ALU.mult))
                dve.wait_ge(la_done, t + 1)
                lev = lambda n: same(dcst[:, D_LEV + n * P:D_LEV + (n + 1) * P])
                dn.link(nc.vector.tensor_tensor(heads4(LTm[:]), q4, ETs[:], ALU.mult))
                dn.link(nc.vector.tensor_tensor(heads4(XT[:]), heads4(LTm[:]), lev(0), ALU.mult))
                nc.vector.tensor_tensor(heads4(XT[:]), heads4(XT[:]), same(ident), ALU.add).then_inc(xt_ready, 1)
                nc.vector.tensor_tensor(heads4(Lb[:, 1]), heads4(LTm[:]), lev(1), ALU.mult).then_inc(lb_ready, 1)
                dn.link(nc.vector.tensor_tensor(heads4(ATm[:]), k4, ET[:], ALU.mult))
                nc.vector.tensor_tensor(kd[:], kn[:], per_head(ekd), ALU.mult)
                for lv in range(LEVELS):
                    if lv + 2 < LEVELS + 1:
                        after(dve, y_done, t * LEVELS + lv)
                        dn.link(nc.vector.tensor_tensor(heads4(Lb[:, lv % 2]), heads4(LTm[:]), lev(lv + 2), ALU.mult))
                    if lv == 0:
                        dve.wait_ge(att_in, t * 16 + 16)
                        dve.wait_ge(ao_low, t + 1)
                        dn.link(nc.vector.tensor_tensor(amx[:, 0, :], abuf[:, 0, :, 65], abuf[:, 1, :, 65], ALU.max))
                        dn.link(nc.vector.tensor_tensor(amx[:, 0, :], amx[:, 0, :], abuf[:, 2, :, 65], ALU.max))
                        nc.vector.tensor_tensor(amx[:, 1:4, :], abuf[:, :, :, 65], amx[:, 0, :].unsqueeze(1)
                                                .to_broadcast([P, 3, 4]), ALU.subtract).then_inc(ae_ready, 1)
                    if lv < LEVELS - 1:
                        dve.wait_ge(z_done, t * (LEVELS - 1) + (lv + 1))
                        nc.vector.tensor_tensor(X[:], X[:], B56[:, 0, :], ALU.add).then_inc(x_added, 1)
                    dve.wait_ge(zt_done, t * LEVELS + (lv + 1))
                    nc.vector.tensor_tensor(XT[:], XT[:], B7[:, :], ALU.add).then_inc(xt_ready, 1)
                    if lv == 1:
                        dve.wait_ge(ae_exp, t + 1)
                        w3 = amx[:, 1:4, :].unsqueeze(3).to_broadcast([P, 3, 4, 65])
                        dn.link(nc.vector.tensor_tensor(abuf[:, :, :, 0:65], abuf[:, :, :, 0:65], w3, ALU.mult))
                        dn.link(nc.vector.tensor_tensor(abuf[:, 0, :, 0:65], abuf[:, 0, :, 0:65], abuf[:, 1, :, 0:65],
                                                        ALU.add))
                    if lv == 2:
                        dn.link(nc.vector.tensor_tensor(abuf[:, 0, :, 0:65], abuf[:, 0, :, 0:65], abuf[:, 2, :, 0:65],
                                                        ALU.add))
                        dn.link(nc.vector.reciprocal(amx[:, 4, :], abuf[:, 0, :, 64]))
                        nc.vector.tensor_tensor(ao[:], abuf[:, 0, :, 0:64], amx[:, 4, :].unsqueeze(2).to_broadcast(
                            [P, 4, 64]), ALU.mult).then_inc(ao_ready, 1)
                    if lv == 4:
                        dve.wait_ge(ao_high, t + 2)
                        nc.vector.tensor_tensor(ol[:, 0:2, bass.ds(t * P, P)], B34[:, 1, 0:256].rearrange(
                            "p (n k) -> p n k", n=2), oh[:, 0:2, bass.ds(t * P, P)].bitcast(F32),
                            ALU.subtract).then_inc(ao_low, 1)
                dve.wait_ge(od_done, t + 1)
                dve.wait_ge(s_ready, t + 1)
                dn.link(nc.vector.tensor_tensor(heads4(S[:]), heads4(S[:]), per_head(egt), ALU.mult))
                nc.vector.tensor_tensor(S[:], S[:], B56[:, 1, :], ALU.add).then_inc(s_ready, 1)
                dve.wait_ge(o_squared, t + 1)
                dn.link(nc.vector.tensor_reduce(rn[:, 3, 0:4], heads4(X[:]), AX.X, ALU.add))
                nc.vector.tensor_scalar(rn[:, 3, 4:8], rn[:, 3, 0:4], 1.0 / DN_D, RMS_EPS, ALU.mult, ALU.add).then_inc(
                    ss_ready, 1)
                norm_sums(t + 1, dn)
                stage_g(t + 1)
                dve.wait_ge(rs_ready, t * 2 + 2)
                nc.vector.tensor_tensor(of[:], v4, per_head(rn[:, 3, 4:8]), ALU.mult).then_inc(on_ready, 1)
                normed(t + 1, dn)
                dve.wait_ge(on_done, t + 1)
                dve.wait_ge(z_in, t * 16 + 16)
                nc.vector.scalar_tensor_tensor(of[:], heads4(B7[:, :]), onh[:], zin[:], ALU.mult, ALU.mult).then_inc(
                    of_ready, 1)
                weighted(t + 1)
                dve.wait_ge(of_high, t + 1)
                nc.vector.tensor_tensor(ol[:, 2:6, bass.ds(t * P, P)], of[:], oh[:, 2:6, bass.ds(t * P, P)].bitcast(F32),
                                        ALU.subtract).then_inc(of_low, 1)
                assert dn.n == DN_STEPS, dn.n

            dve.wait_ge(of_low, TILES)
            dve.wait_ge(ds_in, 16)
            dve.wait_ge(ds_act, 2)
            by_b = lambda ap: ap.unsqueeze(1).to_broadcast([SAMPLES, SAMPLES, DN_H])
            eye8 = ident[0:SAMPLES, 0:SAMPLES].unsqueeze(2).to_broadcast([SAMPLES, SAMPLES, DN_H])
            nc.vector.tensor_tensor(sdiag[:, 0], eye8, by_b(babuf[0:SAMPLES, 0, TILES, :]), ALU.mult)
            nc.vector.tensor_tensor(sdiag[:, 1], eye8, by_b(babuf[0:SAMPLES, 6, TILES, :]), ALU.mult).then_inc(ds_dve, 1)
            dve.wait_ge(ds_pe, 2)
            nc.vector.tensor_scalar(s64[0:64, 1, 0:1], B34[0:64, 1, 0:1], RMS_EPS, None, ALU.add).then_inc(ss_ready, 1)
            st.link(nc.vector.tensor_scalar(s64[:, 3, :].rearrange("p (x h b) -> p x b h", x=2, h=DN_H),
                                            B34[:, 0, 0:64].rearrange("p (x b h) -> p x b h", x=2, h=DN_H), 1.0, None,
                                            ALU.mult))
            dve.wait_ge(ds_pe, 3)
            qk = sin[:, 0:8, :].rearrange("p h b -> p (h b)")
            st.link(nc.vector.scalar_tensor_tensor(s64[:, 2, :], qk, 0.5, B34[:, 1, 64:128], ALU.mult, ALU.mult))
            nc.vector.tensor_scalar(s64[:, 4, 0:32], s64[:, 2, 32:64], -1.0, None, ALU.mult)
            nc.vector.tensor_tensor(s64[:, 4, 32:64], s64[:, 2, 32:64], s64[:, 3, 0:32], ALU.mult)
            nc.vector.tensor_scalar(s64[:, 5, 0:32], sin[:, 8:12, :].rearrange("p h b -> p (h b)"), 0.5, None, ALU.mult)
            nc.vector.tensor_scalar(s64[:, 2, 0:32], s64[:, 2, 0:32], DN_D ** -0.5, None, ALU.mult).then_inc(ds_dve, 1)
            dve.wait_ge(ds_dve, 2)
            across = lambda ap: ap.unsqueeze(2).to_broadcast([P, 4, P])

            def group_of(n):
                h, b0 = n // 2, n % 2 * 4
                col = h * SAMPLES + b0
                return sS[:, h, b0:b0 + 4, :], lambda part, base: across(s64[:, part, base + col:base + col + 4])

            def decayed(n):
                state, by = group_of(n)
                dve.wait_ge(state_in[n // 2], 16)
                st.link(nc.vector.tensor_tensor(state, state, by(3, 32), ALU.mult))
                nc.vector.tensor_tensor(sdv[:, n % 2], same(ident), by(5, 0), ALU.mult).then_inc(ds_scaled, 1)

            decayed(0)
            for n in range(8):
                if n < 7:
                    decayed(n + 1)
                state, by = group_of(n)
                dve.wait_ge(ds_prod, n + 1)
                st.link(nc.vector.tensor_tensor(sdv[:, n % 2], heads4(B56[:, n % 2, :]), by(4, 32), ALU.mult))
                nc.vector.tensor_tensor(state, state, sdv[:, n % 2], ALU.add).then_inc(ds_new, 1)
                dve.wait_ge(ds_new, n + 1)
            dve.wait_ge(ds_pe, 4)
            nc.vector.tensor_scalar(s64[0:32, 1, 1:2], B34[0:32, 1, 0:1], 1.0 / DN_D, RMS_EPS, ALU.mult, ALU.add).then_inc(
                ss_ready, 1)
            dve.wait_ge(ds_pe, 5)
            st.link(nc.vector.tensor_copy(s64[:, 5, 32:64], B34[:, 1, 64:96]))
            hb = lambda ap: ap.rearrange("p (h b) -> p h b", h=DN_H)
            st.link(nc.vector.tensor_tensor(sof[:], hb(B7[:, 0:32]), hb(s64[:, 5, 32:64]), ALU.mult))
            nc.vector.scalar_tensor_tensor(sof[:], sof[:], onh[:], sin[:, 12:16, :], ALU.mult, ALU.mult).then_inc(
                of_ready, 1)
            dve.wait_ge(of_high, TILES + 1)
            nc.vector.tensor_tensor(ol[:, 2:6, SEQ:TOK], sof[:], oh[:, 2:6, SEQ:TOK].bitcast(F32),
                                    ALU.subtract).then_inc(of_low, 1)

            dbank = (B34[:, 0, :], B34[:, 1, :], B56[:, 0, :])
            dve.wait_ge(fstate_in, 16)
            dve.wait_ge(of_low, TILES + 1)
            for f, par, i in pairs(dve, 0, KT):
                dve.wait_ge(gates_in[par], (f - par) * 8 + 16)
                after(dve, m_low, f * 3)
                for j in range(THIRDS):
                    dve.wait_ge(slice_done, (f + U_BRANCH) * 3 + (j + 1))
                    nc.vector.scalar_tensor_tensor(cc[:, third(j)], gates[:, par, 0, third(j)], 1.0,
                                                   U[:, j, 0:TW], ALU.add, ALU.mult)
                    dve.wait_ge(merged, f * 3 + j)
                    nc.vector.scalar_tensor_tensor(mt, gates[:, par, 1, third(j)], 1.0,
                                                   dbank[j][:, 0:TW], ALU.add, ALU.mult).then_inc(used, 1)
                    dve.wait_ge(used, f * 3 + (j + 1))
                    nc.vector.tensor_tensor(cc[:, third(j)], cc[:, third(j)], mt, ALU.add).then_inc(merged, 1)
                for j in range(THIRDS):
                    dve.wait_ge(m_high, f * 3 + (j + 1))
                    x = (slice(None), bass.ds(f, 1), third(j))
                    nc.vector.scalar_tensor_tensor(xl[x].squeeze(1), cc[:, third(j)], 0.5, xh[x].squeeze(1).bitcast(F32),
                                                   ALU.mult, ALU.subtract).then_inc(m_low, 1)
            dve.wait_ge(acc_in, 16 * (KT - 1))
            for f, par, i in pairs(dve, 0, KT):
                for j in range(THIRDS):
                    dve.wait_ge(slice_done, (f + U_MIX) * 3 + (j + 1))
                    a = acc[:, bass.ds(f, 1), third(j)].squeeze(1)
                    nc.vector.scalar_tensor_tensor(a, a, ALPHA, U[:, j, 0:TW], ALU.mult, ALU.add).then_inc(used, 1)
            nc.vector.memset(ab[:, 0:2], 0.0).then_inc(f_zero, 1)

            def moments(t, first):
                par, win, m = window(t)
                n = first + t
                dve.wait_ge(ln_in, n + 1)
                after(dve, ln_norm, n - 1)
                for a in range(2):
                    ins = nc.vector.bn_stats(stats[0:m, par, a, :], (B34, B56)[par][0:m, a, :])
                ins.then_inc(ln_step, 1)
                dve.wait_ge(ln_step, 2 * n + 1)
                nc.vector.bn_aggr(mv[0:m, par, 0:2], stats[0:m, par].rearrange("p a s -> p (a s)")).then_inc(ln_step, 1)
                dve.wait_ge(ln_step, 2 * n + 2)
                nc.vector.tensor_scalar(mv[0:m, par, 1:2], mv[0:m, par, 1:2], LN_EPS, None, ALU.add).then_inc(ln_var, 1)

            def shift(t, first):
                par, win, m = window(t)
                dve.wait_ge(ln_root, first + t + 1)
                nc.vector.scalar_tensor_tensor(mv[0:m, par, 3:4], mv[0:m, par, 0:1], -1.0, mv[0:m, par, 2:3], ALU.mult,
                                               ALU.mult).then_inc(ln_shift, 1)

            for t in range(WINDOWS + 2):
                if t < WINDOWS:
                    moments(t, 0)
                if t >= 2:
                    par, win, m = window(t - 2)
                    row = lambda c: cst[:, c:c + 4].unsqueeze(2).to_broadcast([P, 4, m])
                    src = U[:, 2 * par, :].rearrange("p (k t) -> p k t", k=4)[:, :, 0:m]
                    dve.wait_ge(ln_back, t - 1)
                    nc.vector.tensor_tensor(acc[:, 0:4, win], src, row(C_G1), ALU.mult).then_inc(ln_mul, 1)
                    dve.wait_ge(ln_mul, t - 1)
                    nc.vector.tensor_tensor(acc[:, 0:4, win], acc[:, 0:4, win], row(C_B1), ALU.add).then_inc(
                        ln_front, 1)
                if t < WINDOWS:
                    shift(t, 0)
            fs = Steps(dve, f_step)
            dve.wait_ge(f_zero, 1)
            for n, f0, u0, before in pieces():
                for p, par, i in pairs(dve, 0, n):
                    u, F = p * 2 + u0, p + f0
                    fs.item(F, FFN_STEPS)
                    w3 = [cst[:, bass.ds(F * 3 + (C_FFW + k), 1)] for k in range(3)]
                    after(dve, f_low, F)
                    for j in range(THIRDS):
                        dve.wait_ge(a_taken, F * 3 + (j + 1))
                        a, w = j * TW, (TW if j < 2 else SEQ - 2 * TW)
                        fs.link(nc.vector.tensor_scalar(cc[:, a:a + w], ab[:, a + 2:a + 2 + w], w3[2], None, ALU.mult))
                        for k in (1, 0):
                            fs.link(nc.vector.scalar_tensor_tensor(cc[:, a:a + w], ab[:, a + k:a + k + w], w3[k],
                                                                   cc[:, a:a + w], ALU.mult, ALU.add))
                    fs.link(nc.vector.tensor_scalar(cc[:, SEQ:TOK], ab[:, SEQ + 2:TOK + 2], w3[2], None, ALU.mult))
                    fs.link(nc.vector.scalar_tensor_tensor(cc[:, SEQ:TOK], fstate[:, bass.ds(F, 1), :, 1].squeeze(1),
                                                           w3[1], cc[:, SEQ:TOK], ALU.mult, ALU.add))
                    nc.vector.tensor_scalar(ftails[:, bass.ds(F, 1), :].squeeze(1), ab[:, SEQ:SEQ + 10], 1.0, None,
                                            ALU.mult)
                    fs.link(nc.vector.scalar_tensor_tensor(cc[:, SEQ:TOK], fstate[:, bass.ds(F, 1), :, 0].squeeze(1),
                                                           w3[0], cc[:, SEQ:TOK], ALU.mult, ALU.add))
                    dve.wait_ge(f_gelu, F + 1)
                    for j in range(THIRDS):
                        dve.wait_ge(slice_done, u * 3 + (3 + j + 1))
                        nc.vector.tensor_tensor(cc[:, third(j)], gl[:, third(j)], U[:, j, 0:TW],
                                                ALU.mult).then_inc(f_prod, 1)
                    dve.wait_ge(f_high, F * 3 + 3)
                    x = (slice(None), bass.ds(p, 1), slice(None))
                    nc.vector.tensor_tensor(xl[x].squeeze(1), cc[:], xh[x].squeeze(1).bitcast(F32),
                                            ALU.subtract).then_inc(f_low, 1)
                if f0 + n == FT:
                    break
                for f, par, i in pairs(dve, 0, KT):
                    for j in range(THIRDS):
                        dve.wait_ge(slice_done, (f + (u0 + 2 * n)) * 3 + (j + 1))
                        a = acc[:, bass.ds(f, 1), third(j)].squeeze(1)
                        nc.vector.scalar_tensor_tensor(a, a, ALPHA if f0 == 0 else 1.0, U[:, j, 0:TW], ALU.mult,
                                                       ALU.add).then_inc(used, 1)
                dve.wait_ge(used, before + 3 * KT)
            def window_step(t):
                if t < WINDOWS:
                    moments(t, WINDOWS)
                if t >= 1:
                    par, win, m = window(t - 1)
                    dve.wait_ge(ln_norm, WINDOWS + t)
                    after(dve, y_stored[par], (t - 1) // 2 * 16)
                    nc.vector.tensor_tensor(yt[0:m, par, :], xn[par][0:m], g2r[0:m], ALU.mult).then_inc(ln_mul, 1)
                    dve.wait_ge(ln_mul, WINDOWS + t)
                    nc.vector.tensor_tensor(yt[0:m, par, 0:512], yt[0:m, par, 0:512], b2r[0:m, 0:512], ALU.add).then_inc(
                        y_ready, 1)
                if t < WINDOWS:
                    shift(t, WINDOWS)

            pending = None
            for j, f, s, window_after in last_slices():
                dve.wait_ge(slice_done, 3 * U_LAST + s + 1)
                nc.vector.tensor_tensor(acc[:, f, third(j)], acc[:, f, third(j)], U[:, s % 3, 0:TW], ALU.add).then_inc(
                    used, 1)
                if pending is not None:
                    if pending == 0:
                        dve.wait_ge(rows2_in, 32)
                    window_step(pending)
                pending = window_after
            for t in range(BESIDE_LAST, WINDOWS + 1):
                window_step(t)


def layout(x):
    f = np.float32
    g = lambda n: np.asarray(x[n])
    out = {}
    xs = np.concatenate([g("x_prompt")[0], g("x_sample")[:, 0]], 0)
    out["xT"] = np.ascontiguousarray(xs.T.reshape(KT, P, TOK).transpose(1, 0, 2))
    win, wup, wo, wdn = g("w_in")[0], g("w_up")[0], g("w_o")[0], g("w_down")[0]
    wad = np.concatenate([g("w_att_out")[0], g("w_dn_out")[0]], 0)
    wu = np.zeros((UNITS, P, KT, P), f)
    n = 0

    def put(w, k0, ks, c0):
        nonlocal n
        wu[n, :, 0:ks] = w[k0 * P:(k0 + ks) * P, c0:c0 + P].reshape(ks, P, P).transpose(1, 0, 2)
        n += 1

    for grp, kinds in ((0, (0, 1, 2)), (2, (0, 1, 2)), (1, (0, 1, 2))):
        for kind in kinds:
            for j in range(2):
                put(win, 0, KT, kind * ATT_W + grp * 256 + j * P)
    for i in range(12):
        put(win, 0, KT, OFF_DN + i * P)
    for i in range(DN_H):
        put(win, 0, KT, OFF_Z + i * P)
    for i in range(KT):
        put(win, 0, KT, OFF_GATE + i * P)
        put(win, 0, KT, OFF_GATE + D_MODEL + i * P)
    for i in range(KT):
        put(wad, 0, 6, i * P)
    for i in range(KT):
        put(wo, 0, KT, i * P)
    f0 = 0
    for m in PIECES:
        for i in range(m):
            put(wup, 0, KT, (f0 + i) * P)
            put(wup, 0, KT, D_FF + (f0 + i) * P)
        for i in range(KT):
            put(wdn, f0, m, i * P)
        f0 += m
    assert n == UNITS and f0 == FT
    out["wu"] = wu.reshape(UNITS, P, KT * P)
    out["wba"] = np.ascontiguousarray(win[:, OFF_BA:OFF_GATE].reshape(KT, P, 8).transpose(1, 0, 2))
    out["bac"] = np.stack([g("dn_a_log")[0], g("dn_dt_bias")[0]])[None]
    cst = np.zeros((P, C_END), f)
    cst[:, C_ID:C_DNW] = np.eye(P, dtype=f)
    cst[:, C_DNW:C_FFW] = g("w_dn_conv")[0].reshape(4, 12, P).transpose(2, 1, 0).reshape(P, 48)
    cst[:, C_FFW:C_FFB] = g("w_ffn_conv")[0].reshape(3, FT, P).transpose(2, 1, 0).reshape(P, 3 * FT)
    cst[:, C_FFB:C_G1] = g("b_ffn_conv")[0].reshape(FT, P).T
    cst[:, C_G1:C_B1] = g("ln1_g")[0].reshape(KT, P).T
    cst[:, C_B1:C_ON] = g("ln1_b")[0].reshape(KT, P).T
    cst[:, C_ON:C_R] = g("dn_onorm_w")[0][:, None]
    cst[0:SAMPLES, C_R:C_END] = (np.arange(P)[None] // 16 == np.arange(SAMPLES)[:, None]).astype(f)
    out["cst"] = cst
    out["sconv"] = np.ascontiguousarray(g("state_dn_conv")[0].reshape(SAMPLES, 3, 12, P).transpose(3, 2, 0, 1))
    slopes = np.exp2(np.float32(-8.0) * np.arange(1, 13, dtype=f) / np.float32(12)).astype(f).reshape(3, 4)
    q, k = np.arange(P)[:, None], np.arange(P)[None]
    bias = np.full((3, P, 4, 2, P), NEG, f)
    for grp, (win_, d) in enumerate(DIL):
        for slot in range(4):
            h = (slot % 2) * 2 + slot // 2
            if grp < 2:
                own, ok = q - k, q >= k
                pv, okp = P + q - k, k >= q
                bias[grp, :, slot, 1] = np.where(okp, -slopes[grp, h] * (d * pv).astype(f), f(NEG))
            else:
                own, ok = q - k, (q >= k) & (q // 64 == k // 64)
            bias[grp, :, slot, 0] = np.where(ok, -slopes[grp, h] * (d * own).astype(f), f(NEG))
    out["bias"] = bias
    for grp, name in enumerate(("cache_kv_w128", "cache_kv_w512", "cache_kv_w2048")):
        out[f"cache{grp}"] = g(name)[0].reshape(SAMPLES, PAST[grp], 2 * HPG * HD)
    sbias, k0 = np.zeros((P, SK, 4), f), 0
    for grp in (0, 2, 1):
        m, d = SKEYS[grp], DIL[grp][1]
        back = 16 * m - (np.arange(P)[:, None] % 16 * m + np.arange(m)[None])
        sbias[:, k0:k0 + m] = -slopes[grp][None, None] * (d * back).astype(f)[:, :, None]
        k0 += m
    out["sbias"] = sbias
    out["rt"] = np.ascontiguousarray(cst[0:SAMPLES, C_R:C_END].T)
    dc = np.zeros((P, D_END), f)
    dc[:, D_TRI:D_NEG] = q <= k
    dc[:, D_NEG:D_STR] = np.where(q <= k, f(0), f(NEG))
    dc[:, D_STR:D_ONE] = np.where(q < k, f(-1), f(0))
    dc[:, D_ONE:D_LEV] = 1
    for i in range(7):
        n = 1 << i
        dc[:, D_LEV + i * P:D_LEV + (i + 1) * P] = (q // (2 * n) == k // (2 * n)) & (k // n % 2 == 1) & (q // n % 2 == 0)
    out["dcst"] = dc
    out["dnrows"], out["ffnrows"] = g("state_dn_conv")[0], g("state_ffn_conv")[0]
    out["fstate"] = np.ascontiguousarray(g("state_ffn_conv")[0].reshape(SAMPLES, 2, FT, P).transpose(3, 2, 0, 1))
    out["g2"], out["b2"] = g("ln2_g"), g("ln2_b")
    out["sS"] = np.ascontiguousarray(g("state_dn_S")[0].transpose(2, 1, 0, 3))
    return out


OUTS = {"kv0": (P, 4, 136), "kv1": (P, 4, 520), "kv2": (P, 4, TOK), "dnconv": (P, 12, 11), "shift0": (SAMPLES, 127, 512),
        "shift1": (SAMPLES, 511, 512), "shift2": (SAMPLES, 1023, 512), "pS": (P, DN_H * P), "sS": (P, DN_H, SAMPLES, P),
        "dnrows": (SAMPLES, 2, 12 * P), "ffnrows": (SAMPLES, 1, D_FF), "ffnconv": (P, FT, 10), "y": (TOK, D_MODEL)}


def gather(r):
    y = r["y"]
    heads = (2, HPG, HD)
    kv_p, kv_s = [], []
    for grp in range(GROUPS):
        rows = r[f"kv{grp}"].transpose(2, 1, 0).reshape(-1, *heads)
        kv_p.append(rows[None, None, :-SAMPLES])
        old = r[f"shift{grp}"].reshape(SAMPLES, -1, *heads)
        kv_s.append(np.concatenate([old, rows[-SAMPLES:, None]], 1)[None])
    dn = r["dnconv"].transpose(2, 1, 0).reshape(3 + SAMPLES, 12 * P)
    ffn = r["ffnconv"].transpose(2, 1, 0).reshape(2 + SAMPLES, D_FF)
    return (y[None, :SEQ], y[SEQ:, None], *kv_p,
            dn[None, None, :3], r["pS"].reshape(P, DN_H, P).transpose(1, 0, 2)[None, None], ffn[None, None, :2],
            *kv_s,
            np.concatenate([r["dnrows"], dn[3:, None]], 1)[None], r["sS"].transpose(2, 1, 0, 3)[None],
            np.concatenate([r["ffnrows"], ffn[2:, None]], 1)[None])


def kernel(**inputs):
    import concourse.bacc as bacc
    from concourse.bass_utils import run_bass_kernel_spmd

    nc = bacc.Bacc("TRN2", target_bir_lowering=False, num_devices=1)
    arrays = {"in_" + name: np.ascontiguousarray(a) for name, a in layout(inputs).items()}
    ins = {name[3:]: nc.dram_tensor(name, a.shape, mybir.dt.from_np(a.dtype), kind="ExternalInput").ap()
           for name, a in arrays.items()}
    outs = {name: nc.dram_tensor("out_" + name, shape, F32, kind="ExternalOutput").ap() for name, shape in OUTS.items()}
    build(nc, ins, outs)
    r = run_bass_kernel_spmd(nc, [arrays], core_ids=[0])
    r = {name: r.results[0]["out_" + name] for name in OUTS}
    return tuple(np.ascontiguousarray(a) for a in gather(r))
```
